# Optimizing a Trainium2 kernel written in Bass

```python
import math
import jax, jax.numpy as jnp
from jax import lax
import numpy as np

D_MODEL = 1024
BATCH = 1
SEQ = 256
DEPTH = 1

CHUNK = 64
N_MEM = 256
EPS = 1e-6
NEG_INF = -1e30
N_NORMS = 6

BRANCH_DIM = D_MODEL // 2
N_BRANCH = 3

HEAD_DIM = 64
A_Q_HEADS = BRANCH_DIM // HEAD_DIM
A_KV_HEADS = 2
A_GROUP = A_Q_HEADS // A_KV_HEADS
A_Q_DIM = A_Q_HEADS * HEAD_DIM
A_KV_DIM = A_KV_HEADS * HEAD_DIM
WINDOW = 128
WINDOW_CHUNKS = WINDOW // CHUNK
ATT_BLOCK = 128

SGU_CHUNK = 128
SGU_GROUPS = 4
SGU_DIM = BRANCH_DIM
SGU_GROUP_DIM = SGU_DIM // SGU_GROUPS

POOL_WINDOWS = (2, 4, 8, 16)
POOL_GROUPS = 4
POOL_DIM = BRANCH_DIM
POOL_GROUP_DIM = POOL_DIM // POOL_GROUPS

IN_SIZES = (A_Q_DIM, A_KV_DIM, A_KV_DIM, SGU_DIM, SGU_DIM, POOL_DIM, N_BRANCH * D_MODEL)
IN_DIM = A_Q_DIM + 2 * A_KV_DIM + 2 * SGU_DIM + POOL_DIM + N_BRANCH * D_MODEL

MEM_HEADS = 4
MEM_HEAD_DIM = 128
MEM_DIM = MEM_HEADS * MEM_HEAD_DIM

D_FF = 4 * D_MODEL


def rmsnorm(x, g):
    xf = x.astype(jnp.float32)
    y = xf * lax.rsqrt(jnp.mean(xf * xf, axis=-1, keepdims=True) + EPS)
    return (y * g.astype(jnp.float32)).astype(x.dtype)

def split_columns(proj):
    parts, start = [], 0
    for size in IN_SIZES:
        parts.append(proj[..., start:start + size])
        start += size
    return parts

def window_sink_attention(q, k, v, sinks):
    B, S, _ = q.shape
    nb = S // ATT_BLOCK
    qb = q.reshape(B, nb, ATT_BLOCK, A_KV_HEADS, A_GROUP, HEAD_DIM)

    def band(t):
        t = t.reshape(B, S, A_KV_HEADS, HEAD_DIM)
        t = jnp.pad(t, ((0, 0), (ATT_BLOCK, 0), (0, 0), (0, 0)))
        t = t.reshape(B, nb + 1, ATT_BLOCK, A_KV_HEADS, HEAD_DIM)
        return jnp.concatenate([t[:, :-1], t[:, 1:]], axis=2)

    kb, vb = band(k), band(v)
    s = jnp.einsum('bnqhgd,bnkhd->bnhgqk', qb, kb).astype(jnp.float32) * (1.0 / math.sqrt(HEAD_DIM))

    blk = jnp.arange(nb)[:, None, None]
    qpos = blk * ATT_BLOCK + jnp.arange(ATT_BLOCK)[None, :, None]
    kpos = (blk - 1) * ATT_BLOCK + jnp.arange(2 * ATT_BLOCK)[None, None, :]
    qc, kc = qpos // CHUNK, kpos // CHUNK
    valid = (kpos >= 0) & (kc <= qc) & (kc >= qc - WINDOW_CHUNKS)
    s = jnp.where(valid[None, :, None, None], s, NEG_INF)

    sink = sinks.astype(jnp.float32).reshape(A_KV_HEADS, A_GROUP)[None, None, :, :, None, None]
    m = jnp.maximum(jnp.max(s, axis=-1, keepdims=True), sink)
    p = jnp.exp(s - m)
    p = p / (jnp.sum(p, axis=-1, keepdims=True) + jnp.exp(sink - m))
    o = jnp.einsum('bnhgqk,bnkhd->bnqhgd', p.astype(v.dtype), vb)
    return o.reshape(B, S, A_Q_DIM)

def spatial_gating(u, v, g_sgu, w_s, b_s):
    B, S, _ = u.shape
    nc = S // SGU_CHUNK
    u = jax.nn.gelu(u)
    v = rmsnorm(jax.nn.gelu(v), g_sgu)
    vb = v.reshape(B, nc, SGU_CHUNK, SGU_GROUPS, SGU_GROUP_DIM)
    pc = jnp.arange(SGU_CHUNK) // CHUNK
    mask = pc[None, :] <= pc[:, None]
    w = jnp.where(mask[None], w_s, 0.0).astype(v.dtype)
    sp = jnp.einsum('gij,bnjgc->bnigc', w, vb) + b_s.T[:, :, None].astype(v.dtype)
    return u * sp.reshape(B, S, SGU_DIM)

def multiscale_pool(c, w_pool, pool_scale):
    B, S, _ = c.shape
    cs = jnp.cumsum(c.astype(jnp.float32), axis=1)
    t = jnp.arange(S)
    outs = []
    for gi, w in enumerate(POOL_WINDOWS):
        cg = cs[..., gi * POOL_GROUP_DIM:(gi + 1) * POOL_GROUP_DIM]
        lag = jnp.pad(cg, ((0, 0), (w, 0), (0, 0)))[:, :S]
        cnt = jnp.minimum(t + 1, w).astype(jnp.float32)[None, :, None]
        outs.append((cg - lag) / cnt)
    pooled = jnp.concatenate(outs, axis=-1).astype(c.dtype) - c
    pooled = pooled.reshape(B, S, POOL_GROUPS, POOL_GROUP_DIM)
    mixed = jnp.einsum('bsgc,gcd->bsgd', pooled, w_pool).reshape(B, S, POOL_DIM)
    return mixed * pool_scale

def memory_attention(h, mem_n, w_q, w_kv, w_o):
    B, S, _ = h.shape
    q = (h @ w_q).reshape(B, S, MEM_HEADS, MEM_HEAD_DIM)
    kv = mem_n @ w_kv
    k = kv[..., :MEM_DIM].reshape(B, N_MEM, MEM_HEADS, MEM_HEAD_DIM)
    v = kv[..., MEM_DIM:].reshape(B, N_MEM, MEM_HEADS, MEM_HEAD_DIM)
    s = jnp.einsum('bshd,bmhd->bhsm', q, k).astype(jnp.float32) * (1.0 / math.sqrt(MEM_HEAD_DIM))
    p = jax.nn.softmax(s, axis=-1).astype(h.dtype)
    o = jnp.einsum('bhsm,bmhd->bshd', p, v).reshape(B, S, MEM_DIM)
    return o @ w_o

def first_inputs(seed: int = 0) -> dict:
    key = jax.random.key(seed)
    ks = jax.random.split(key, 20)
    f32 = jnp.float32

    def dense(k, shape, fan_in):
        return jax.random.normal(k, shape, f32) * (fan_in ** -0.5)

    return {
        "x": jax.random.normal(ks[0], (BATCH, SEQ, D_MODEL), f32),
        "mem": jax.random.normal(ks[1], (BATCH, N_MEM, D_MODEL), f32),
        "g_norm": 1.0 + 0.1 * jax.random.normal(ks[2], (DEPTH, N_NORMS, D_MODEL), f32),
        "g_mem": 1.0 + 0.1 * jax.random.normal(ks[3], (DEPTH, D_MODEL), f32),
        "w_in": dense(ks[4], (DEPTH, D_MODEL, IN_DIM), D_MODEL),
        "attn_sinks": 0.5 * jax.random.normal(ks[5], (DEPTH, A_Q_HEADS), f32),
        "w_spatial": dense(ks[6], (DEPTH, SGU_GROUPS, SGU_CHUNK, SGU_CHUNK), SGU_CHUNK),
        "b_spatial": 1.0 + 0.1 * jax.random.normal(ks[7], (DEPTH, SGU_GROUPS, SGU_CHUNK), f32),
        "g_sgu": 1.0 + 0.1 * jax.random.normal(ks[8], (DEPTH, SGU_DIM), f32),
        "w_pool": dense(ks[9], (DEPTH, POOL_GROUPS, POOL_GROUP_DIM, POOL_GROUP_DIM), POOL_GROUP_DIM),
        "pool_scale": 1.0 + 0.1 * jax.random.normal(ks[10], (DEPTH, POOL_DIM), f32),
        "w_branch": dense(ks[11], (DEPTH, N_BRANCH, BRANCH_DIM, D_MODEL), BRANCH_DIM),
        "w_out": dense(ks[12], (DEPTH, D_MODEL, D_MODEL), D_MODEL),
        "w_q_mem": dense(ks[13], (DEPTH, D_MODEL, MEM_DIM), D_MODEL),
        "w_kv_mem": dense(ks[14], (DEPTH, D_MODEL, 2 * MEM_DIM), D_MODEL),
        "w_o_mem": dense(ks[15], (DEPTH, MEM_DIM, D_MODEL), MEM_DIM),
        "w_up": dense(ks[16], (DEPTH, D_MODEL, D_FF), D_MODEL),
        "w_down": dense(ks[17], (DEPTH, D_FF, D_MODEL), D_FF),
    }

def first_block(x, mem, g_norm, g_mem, w_in, attn_sinks, w_spatial, b_spatial, g_sgu,
              w_pool, pool_scale, w_branch, w_out, w_q_mem, w_kv_mem, w_o_mem, w_up, w_down):
    B, S, _ = x.shape
    for l in range(DEPTH):
        h = rmsnorm(x, g_norm[l, 0])
        q, k, v, su, sv, pc, gate = split_columns(h @ w_in[l])
        ya = window_sink_attention(q, k, v, attn_sinks[l])
        yb = spatial_gating(su, sv, g_sgu[l], w_spatial[l], b_spatial[l])
        yc = multiscale_pool(pc, w_pool[l], pool_scale[l])
        branches = jnp.stack([ya, yb, yc], axis=2)
        proj = jnp.einsum('bsnc,ncd->bsnd', branches, w_branch[l])
        gates = jax.nn.sigmoid(gate.reshape(B, S, N_BRANCH, D_MODEL))
        merged = jnp.sum(gates * proj, axis=2)
        x = x + rmsnorm(merged @ w_out[l], g_norm[l, 1])
        hm = rmsnorm(x, g_norm[l, 2])
        mem_n = rmsnorm(mem, g_mem[l])
        ym = memory_attention(hm, mem_n, w_q_mem[l], w_kv_mem[l], w_o_mem[l])
        x = x + rmsnorm(ym, g_norm[l, 3])
        hf = rmsnorm(x, g_norm[l, 4])
        yf = jnp.square(jax.nn.relu(hf @ w_up[l])) @ w_down[l]
        x = x + rmsnorm(yf, g_norm[l, 5])
    return x


DEPTH_2 = 2

N_A = DEPTH_2 // 2
N_B = DEPTH_2 - N_A
N_HEADS = D_MODEL // HEAD_DIM
N_META = 16
BLOCK = 128
PAD = BLOCK - N_META
D_DECAY_LORA = max(32, int(round(1.8 * D_MODEL ** 0.5 / 32)) * 32)
D_AAA_LORA = max(32, int(round(1.8 * D_MODEL ** 0.5 / 32)) * 32)
D_MV_LORA = max(32, int(round(1.3 * D_MODEL ** 0.5 / 32)) * 32)
D_GATE_LORA = max(32, int(round(0.6 * D_MODEL ** 0.8 / 32)) * 32)
D_FF_2 = int(math.ceil(8 * D_MODEL / 3 / 256)) * 256
CONV_WIDTH = 3
GN_EPS = 64e-5
RMS_EPS = 1e-6


def rms_norm(x, g):
    xf = x.astype(jnp.float32)
    y = xf * lax.rsqrt(jnp.mean(xf * xf, axis=-1, keepdims=True) + RMS_EPS) * g.astype(jnp.float32)
    return y.astype(x.dtype)

def token_shift(x):
    return jnp.pad(x, ((0, 0), (1, 0), (0, 0)))[:, :-1]

def conv_glu_ffn(x, w_up, conv_w, conv_b, w_down):
    u = x @ w_up
    c = u.shape[-1]
    u = lax.conv_general_dilated(
        u, conv_w.reshape(CONV_WIDTH, 1, c).astype(u.dtype),
        window_strides=(1,), padding=[(CONV_WIDTH - 1, 0)],
        dimension_numbers=('NWC', 'WIO', 'NWC'), feature_group_count=c) + conv_b
    gate, val = jnp.split(u, 2, axis=-1)
    return (jax.nn.silu(gate) * val) @ w_down

def rwkv7_time_mix(x, v_first, v_res, mix, w_r, w_k, w_v, w_o, w0, w1, w2,
                   a0, a1, a2, g1, g2, k_k, k_a, r_k, lnx_g, lnx_b):
    bsz, L, C = x.shape
    f32 = jnp.float32
    xx = token_shift(x) - x
    xr, xw, xk, xv, xa, xg = [x + xx * mix[i] for i in range(6)]
    r = xr @ w_r
    k = xk @ w_k
    v = xv @ w_v
    w_log = -jax.nn.softplus(-(w0 + jnp.tanh(xw @ w1) @ w2)) - 0.5
    a = jax.nn.sigmoid(a0 + (xa @ a1) @ a2)
    g = jax.nn.sigmoid(xg @ g1) @ g2

    def heads(t):
        return t.astype(f32).reshape(bsz, L, N_HEADS, HEAD_DIM)

    kk = heads(k * k_k)
    kk = kk / jnp.maximum(jnp.linalg.norm(kk, axis=-1, keepdims=True), 1e-12)
    k = k * (1 + (a - 1) * k_a)
    if v_res is None:
        v_first = v
    else:
        v0, v1, v2 = v_res
        v = v + (v_first - v) * jax.nn.sigmoid(v0 + (xv @ v1) @ v2)
    rh, kh, vh, ah = heads(r), heads(k), heads(v), heads(a)
    decay = jnp.exp(-jnp.exp(heads(w_log)))
    seq = tuple(jnp.moveaxis(t, 1, 0) for t in (rh, decay, kh, vh, -kk, kk * ah))

    def step(S, inp):
        r_t, w_t, k_t, v_t, a_t, b_t = inp
        sa = jnp.einsum('bhij,bhj->bhi', S, a_t)
        S = (S * w_t[:, :, None, :] + sa[..., None] * b_t[:, :, None, :]
             + v_t[..., None] * k_t[:, :, None, :])
        return S, jnp.einsum('bhij,bhj->bhi', S, r_t)

    S0 = jnp.zeros((bsz, N_HEADS, HEAD_DIM, HEAD_DIM), f32)
    _, y = lax.scan(step, S0, seq)
    y = jnp.moveaxis(y, 0, 1)
    mu = jnp.mean(y, axis=-1, keepdims=True)
    var = jnp.mean(jnp.square(y - mu), axis=-1, keepdims=True)
    y = ((y - mu) * lax.rsqrt(var + GN_EPS)).reshape(bsz, L, C) * lnx_g.astype(f32) + lnx_b.astype(f32)
    bonus = jnp.sum(rh * kh * r_k.astype(f32), axis=-1, keepdims=True) * vh
    y = (y + bonus.reshape(bsz, L, C)).astype(x.dtype)
    return (y * g) @ w_o, v_first

def to_padded_heads(t):
    bsz, L, _ = t.shape
    t = t.reshape(bsz, L, N_HEADS, HEAD_DIM)
    t = jnp.pad(t, ((0, 0), (PAD, 0), (0, 0), (0, 0)))
    return jnp.transpose(t, (0, 2, 1, 3))

def stick_breaking_attention(q, k, v):
    bsz, nh, lp, dh = q.shape
    nb = lp // BLOCK
    scale = dh ** -0.5
    key_pos = jnp.arange(lp)
    qb = jnp.moveaxis(q.reshape(bsz, nh, nb, BLOCK, dh), 2, 0)

    def one_block(args):
        q_blk, blk = args
        z = jnp.einsum('bhqd,bhkd->bhqk', q_blk, k).astype(jnp.float32) * scale
        q_pos = blk * BLOCK + jnp.arange(BLOCK)
        valid = (key_pos[None, :] < q_pos[:, None]) & (key_pos[None, :] >= PAD)
        log_1m = jnp.where(valid, jax.nn.log_sigmoid(-z), 0.0)
        log_after = lax.cumsum(log_1m, axis=3, reverse=True) - log_1m
        w = jnp.where(valid, jnp.exp(jax.nn.log_sigmoid(z) + log_after), 0.0)
        return jnp.einsum('bhqk,bhkd->bhqd', w.astype(v.dtype), v)

    out = lax.map(one_block, (qb, jnp.arange(nb)))
    out = jnp.moveaxis(out, 0, 2).reshape(bsz, nh, lp, dh)
    return jnp.transpose(out, (0, 2, 1, 3))[:, PAD:].reshape(bsz, lp - PAD, nh * dh)

def second_inputs(seed: int = 0) -> dict:
    key = jax.random.key(seed)
    ks = jax.random.split(key, 40)
    counter = iter(range(40))

    def nk():
        return ks[next(counter)]

    def nrm(shape, s):
        return jax.random.normal(nk(), shape, jnp.float32) * s

    def uni(shape, lo, hi):
        return jax.random.uniform(nk(), shape, jnp.float32, lo, hi)

    D, F2 = D_MODEL, 2 * D_FF_2
    nv = max(N_A - 1, 0)
    return {
        "x": nrm((BATCH, SEQ, D), 1.0),
        "meta_tokens": nrm((N_META, D), 1.0),
        "norm_mix_g": 1.0 + nrm((DEPTH_2, D), 0.02),
        "norm_ffn_g": 1.0 + nrm((DEPTH_2, D), 0.02),
        "ffn_up": nrm((DEPTH_2, D, F2), D ** -0.5),
        "ffn_conv_w": nrm((DEPTH_2, CONV_WIDTH, F2), CONV_WIDTH ** -0.5),
        "ffn_conv_b": nrm((DEPTH_2, F2), 0.01),
        "ffn_down": nrm((DEPTH_2, D_FF_2, D), D_FF_2 ** -0.5),
        "rw_mix": uni((N_A, 6, D), 0.0, 1.0),
        "rw_wr": nrm((N_A, D, D), D ** -0.5),
        "rw_wk": nrm((N_A, D, D), D ** -0.5),
        "rw_wv": nrm((N_A, D, D), D ** -0.5),
        "rw_wo": nrm((N_A, D, D), D ** -0.5),
        "rw_w0": uni((N_A, D), -6.5, -1.0),
        "rw_w1": nrm((N_A, D, D_DECAY_LORA), D ** -0.5),
        "rw_w2": nrm((N_A, D_DECAY_LORA, D), 0.1 * D_DECAY_LORA ** -0.5),
        "rw_a0": nrm((N_A, D), 0.1),
        "rw_a1": nrm((N_A, D, D_AAA_LORA), D ** -0.5),
        "rw_a2": nrm((N_A, D_AAA_LORA, D), 0.1 * D_AAA_LORA ** -0.5),
        "rw_g1": nrm((N_A, D, D_GATE_LORA), D ** -0.5),
        "rw_g2": nrm((N_A, D_GATE_LORA, D), D_GATE_LORA ** -0.5),
        "rw_kk": 0.85 + nrm((N_A, D), 0.05),
        "rw_ka": 1.0 + nrm((N_A, D), 0.05),
        "rw_rk": nrm((N_A, N_HEADS, HEAD_DIM), 0.1),
        "rw_lnx_g": 1.0 + nrm((N_A, D), 0.02),
        "rw_lnx_b": nrm((N_A, D), 0.01),
        "rw_v0": 1.0 + nrm((nv, D), 0.1),
        "rw_v1": nrm((nv, D, D_MV_LORA), D ** -0.5),
        "rw_v2": nrm((nv, D_MV_LORA, D), 0.1 * D_MV_LORA ** -0.5),
        "kv_norm_g": 1.0 + nrm((D,), 0.02),
        "sb_wk": nrm((D, D), D ** -0.5),
        "sb_wv": nrm((D, D), D ** -0.5),
        "sb_wq": nrm((N_B, D, D), D ** -0.5),
        "sb_wo": nrm((N_B, D, D), D ** -0.5),
        "final_norm_g": 1.0 + nrm((D,), 0.02),
    }

def second_block(x, meta_tokens, norm_mix_g, norm_ffn_g, ffn_up, ffn_conv_w, ffn_conv_b, ffn_down,
              rw_mix, rw_wr, rw_wk, rw_wv, rw_wo, rw_w0, rw_w1, rw_w2, rw_a0, rw_a1, rw_a2,
              rw_g1, rw_g2, rw_kk, rw_ka, rw_rk, rw_lnx_g, rw_lnx_b, rw_v0, rw_v1, rw_v2,
              kv_norm_g, sb_wk, sb_wv, sb_wq, sb_wo, final_norm_g):
    bsz = x.shape[0]
    meta = jnp.broadcast_to(meta_tokens.astype(x.dtype)[None], (bsz, N_META, D_MODEL))
    h = jnp.concatenate([meta, x], axis=1)
    v_first = None
    k_sh = v_sh = None
    for layer in range(DEPTH_2):
        hn = rms_norm(h, norm_mix_g[layer])
        if layer < N_A:
            i = layer
            v_res = None if i == 0 else (rw_v0[i - 1], rw_v1[i - 1], rw_v2[i - 1])
            mix_out, v_first = rwkv7_time_mix(
                hn, v_first, v_res, rw_mix[i], rw_wr[i], rw_wk[i], rw_wv[i], rw_wo[i],
                rw_w0[i], rw_w1[i], rw_w2[i], rw_a0[i], rw_a1[i], rw_a2[i], rw_g1[i], rw_g2[i],
                rw_kk[i], rw_ka[i], rw_rk[i], rw_lnx_g[i], rw_lnx_b[i])
        else:
            j = layer - N_A
            if layer == N_A:
                kvn = rms_norm(h, kv_norm_g)
                k_sh = to_padded_heads(kvn @ sb_wk)
                v_sh = to_padded_heads(kvn @ sb_wv)
            q = to_padded_heads(hn @ sb_wq[j])
            mix_out = stick_breaking_attention(q, k_sh, v_sh) @ sb_wo[j]
        h = h + mix_out
        h = h + conv_glu_ffn(rms_norm(h, norm_ffn_g[layer]), ffn_up[layer], ffn_conv_w[layer],
                             ffn_conv_b[layer], ffn_down[layer])
    return rms_norm(h, final_norm_g)[:, N_META:, :]


def setup_inputs(seed=0):
    out = dict(first_inputs(seed))
    for name, value in second_inputs(seed + 1).items():
        if name != "x":
            out[name + "_2"] = value
    return out


def reference(
    x, mem, g_norm, g_mem, w_in, attn_sinks, w_spatial, b_spatial, g_sgu, w_pool, pool_scale,
    w_branch, w_out, w_q_mem, w_kv_mem, w_o_mem, w_up, w_down, meta_tokens_2, norm_mix_g_2,
    norm_ffn_g_2, ffn_up_2, ffn_conv_w_2, ffn_conv_b_2, ffn_down_2, rw_mix_2, rw_wr_2, rw_wk_2,
    rw_wv_2, rw_wo_2, rw_w0_2, rw_w1_2, rw_w2_2, rw_a0_2, rw_a1_2, rw_a2_2, rw_g1_2, rw_g2_2,
    rw_kk_2, rw_ka_2, rw_rk_2, rw_lnx_g_2, rw_lnx_b_2, rw_v0_2, rw_v1_2, rw_v2_2, kv_norm_g_2,
    sb_wk_2, sb_wv_2, sb_wq_2, sb_wo_2, final_norm_g_2,
):
    x = first_block(
        x, mem, g_norm, g_mem, w_in, attn_sinks, w_spatial, b_spatial, g_sgu, w_pool,
        pool_scale, w_branch, w_out, w_q_mem, w_kv_mem, w_o_mem, w_up, w_down,
    )
    return second_block(
        x, meta_tokens_2, norm_mix_g_2, norm_ffn_g_2, ffn_up_2, ffn_conv_w_2, ffn_conv_b_2,
        ffn_down_2, rw_mix_2, rw_wr_2, rw_wk_2, rw_wv_2, rw_wo_2, rw_w0_2, rw_w1_2, rw_w2_2,
        rw_a0_2, rw_a1_2, rw_a2_2, rw_g1_2, rw_g2_2, rw_kk_2, rw_ka_2, rw_rk_2, rw_lnx_g_2,
        rw_lnx_b_2, rw_v0_2, rw_v1_2, rw_v2_2, kv_norm_g_2, sb_wk_2, sb_wv_2, sb_wq_2, sb_wo_2,
        final_norm_g_2,
    )


_drawn_inputs = setup_inputs


def setup_inputs(seed=0):
    import zlib

    import numpy as np

    out = dict(_drawn_inputs(seed))
    spreads = {}
    factors = {'attn_sinks': 8.0,
     'norm_mix_g_2': 5.196,
     'norm_ffn_g_2': 4.959,
     'ffn_conv_b_2': 8.0,
     'rw_w1_2': 8.0,
     'rw_w2_2': 8.0,
     'rw_a0_2': 4.356,
     'rw_a1_2': 4.645,
     'rw_a2_2': 4.725,
     'rw_lnx_g_2': 64.0,
     'rw_lnx_b_2': 64.0,
     'kv_norm_g_2': 26.658,
     'final_norm_g_2': 8.082}
    for name, (base, spread) in spreads.items():
        noise = np.random.default_rng([zlib.crc32(name.encode()), seed]).standard_normal(out[name].shape)
        drawn = base * np.exp(spread * noise) if base else spread * noise
        out[name] = __import__('jax').numpy.asarray(drawn.astype(out[name].dtype))
    for name, factor in factors.items():
        out[name] = (out[name] * factor).astype(out[name].dtype)
    return out
```

```python
from contextlib import ExitStack

import numpy as np

import concourse.bass as bass
from concourse import mybir

ALU = mybir.AluOpType
ACT = mybir.ActivationFunctionType
F32 = mybir.dt.float32
AX_X = mybir.AxisListType.X

P = 128
D = 1024
KT = D // P
S = 256
META = 16
L = S + META
RING = 8
BLK = 8 * P
EPS = 1e-6
GN_EPS = 64e-5
NEG = -1e30
GB = 4

N_QKV, N_SU, N_SV, N_PC, N_GATE = 6, 4, 4, 4, 24
N_IN = N_QKV + N_SU + N_SV + N_PC + N_GATE
FF = 4096 // P
F2 = 2816 // P
F2B = 3
STREAM = [("in", N_IN), ("branch", 12), ("out", 8), ("mem_kv", 8), ("mem_q", 4), ("mem_o", 4),
          ("up", FF), ("down", 4 * KT),
          ("rw_r", 8), ("rw_k", 8), ("rw_v", 8), ("rw_o", 8),
          ("ffa_up", 2 * F2), ("ffa_down", F2B * KT),
          ("sb_k", 8), ("sb_v", 8), ("sb_q", 8), ("sb_o", 8),
          ("ffb_up", 2 * F2), ("ffb_down", F2B * KT)]
FIRST = {}
_n = 0
for _name, _count in STREAM:
    FIRST[_name] = _n
    _n += _count
N_BLOCKS = _n

COLS = {}
_n = 0
for _name, _count in [("g_norm", 48), ("g_mem", 8), ("g_sgu", 4), ("pool_scale", 4), ("mix_g", 16),
                      ("ffn_g", 16), ("rw_mix", 48), ("w0", 8), ("a0", 8), ("k_k", 8), ("k_a", 8),
                      ("r_k", 8), ("lnx_g", 8), ("lnx_b", 8), ("kv_g", 8), ("fin_g", 8),
                      ("conv_w", 2 * 3 * 2 * F2), ("conv_b", 2 * 2 * F2)]:
    COLS[_name] = _n
    _n += _count
N_COLS = _n

CH = 32
LEVELS = (1, 2, 4, 8, 16)


def shape_constants():
    i = np.arange(P)
    r, c = i[:, None], i[None, :]
    same = r // CH == c // CH
    parts = {
        "ident": r == c,
        "mean": np.full((P, P), 1.0 / D),
        "ones": np.ones((P, P)),
        "after": r >= c,
        "strict": r < c,
        "att0": np.where((r < 64) & (c >= 64), NEG, 0.0),
        "chunk_strict": same & (r < c),
        "chunk_incl": same & (r <= c),
        "level1t": (r // 2 == c // 2) & (r > c),
        "scan": np.tile((np.arange(L) % CH != 0).astype(np.float32), (P, 1)),
    }
    c2 = np.arange(2 * P)[None, :]
    parts["att1"] = np.where(((r < 64) & (c2 >= 192)) | ((r >= 64) & (c2 < 64)), NEG, 0.0)
    for m in LEVELS:
        parts[f"level{m}"] = (r // (2 * m) == c // (2 * m)) & (r % (2 * m) < m) & (c % (2 * m) >= m)
    heads = (2 * np.arange(KT)[None, :, None] + r[:, :, None] // 64) == np.arange(16)[None, None, :]
    parts["to_head"] = heads.reshape(P, KT * 16)
    back = np.zeros((P, KT, P))
    back[:16] = heads.transpose(2, 1, 0)
    parts["from_head"] = back.reshape(P, KT * P)
    parts["strict_neg"] = np.where(r < c, 0.0, NEG)
    t = np.arange(16) + 1
    parts["inv_cnt"] = np.tile(np.concatenate([1.0 / np.minimum(t, w) for w in (2, 4, 8, 16)]), (P, 1))
    at, n = {}, 0
    for k, v in parts.items():
        at[k] = (n, n + v.shape[1])
        n += v.shape[1]
    return np.concatenate([np.asarray(v, np.float32) for v in parts.values()], axis=1), at


CONSTS, CONST_AT = shape_constants()


class Chain:

    def __init__(self, eng, sem):
        self.eng, self.sem, self.n, self.loop = eng, sem, 0, None

    def __call__(self, ins):
        ins.then_inc(self.sem, 1)
        self.n += 1
        self.eng.wait_ge(self.sem, self.n if self.loop is None else self.loop * self.per + self.n)

    def enter(self, index, per):
        self.loop, self.per, self.base = index, per, self.n

    def leave(self, times):
        assert self.n - self.base == self.per, (self.n - self.base, self.per)
        self.loop, self.n = None, self.base + self.per * times


class Marks:

    def __init__(self, sem, names):
        self.sem, self.names, self.next = sem, names.split(), 0

    def reach(self, ins, name):
        assert self.names[self.next % len(self.names)] == name, (self.names[self.next], name)
        self.next += 1
        ins.then_inc(self.sem, 1)

    def wait(self, eng, name, it=None):
        n = self.names.index(name) + 1
        eng.wait_ge(self.sem, n if it is None else it * len(self.names) + n)


class Space:

    def __init__(self, tensor, width):
        self.t, self.width, self.at = tensor, width, 0

    def take(self, *dims):
        n = int(np.prod(dims))
        a = self.t[:, self.at:self.at + n]
        self.at += n
        assert self.at <= self.width, (self.at, self.width)
        if len(dims) == 2:
            return a.rearrange("p (a b) -> p a b", a=dims[0])
        if len(dims) == 4:
            return a.rearrange("p (a b c d) -> p a b c d", a=dims[0], b=dims[1], c=dims[2])
        if len(dims) == 3:
            return a.rearrange("p (a b c) -> p a b c", a=dims[0], b=dims[1])
        return a


def program(nc, stream, x_t, mem_t, meta_t, cols_d, consts_d, sinks_d, ws_t, b_sp, w_pool,
            w1_d, a1_d, g1_d, w2_d, a2_d, g2_d, out_t):
    with ExitStack() as ctx:
        def sem(name):
            return ctx.enter_context(nc.semaphore(name))

        ring = ctx.enter_context(nc.sbuf_tensor("ring", [P, RING, BLK], F32))
        consts = ctx.enter_context(nc.sbuf_tensor("consts", [P, CONSTS.shape[1]], F32))
        cols = ctx.enter_context(nc.sbuf_tensor("cols", [P, N_COLS], F32))
        res = ctx.enter_context(nc.sbuf_tensor("res", [P, KT, L], F32))
        small = ctx.enter_context(nc.sbuf_tensor("small", [P, 64], F32))
        rs = ctx.enter_context(nc.sbuf_tensor("rs", [P, L], F32))
        width = (212863 // 4) - (RING * BLK + CONSTS.shape[1] + N_COLS + KT * L + 64 + L) - 16
        width -= width % 8
        arena = ctx.enter_context(nc.sbuf_tensor("arena", [P, width], F32))
        ps = ctx.enter_context(nc.psum_tensor("ps", [P, 8, 512], F32))

        def const(name, rows=P):
            a, b = CONST_AT[name]
            return consts[0:rows, a:b]

        def col(name, k, rows=P):
            return cols[0:rows, COLS[name] + k:COLS[name] + k + 1]

        def col_wide(name, k, n, t):
            a = COLS[name] + k
            return cols[:, a:a + n].unsqueeze(2).to_broadcast([P, n, t])

        def over(a, n):
            return a.unsqueeze(1).to_broadcast([P, n, a.shape[1]])

        ident = const("ident")
        xr = res[:, :, META:L]

        one = Space(arena, width)
        eps_c = small[:, 0:1]
        gn_eps_c = small[:, 1:2]
        one_c = small[:, 2:3]
        sink_sb = small[:, 8:16]
        h = one.take(KT, S)
        qkv = one.take(N_QKV, S)
        su, sv = one.take(4, S), one.take(4, S)
        pcp = one.take(4, L)
        gates = one.take(24, S)
        sc1, sc0 = one.take(8, 2 * P), one.take(8, P)
        pt1, pt0 = one.take(2, 8, P), one.take(8, P)
        act_up = arena[:, one.at - 24 * S - 16 * P - 8 * P - 16 * P - 8 * P:one.at][:, 0:FF * S].rearrange(
            "p (a b) -> p a b", a=FF)
        vtok = one.take(2, P)
        svt = one.take(2, 512)
        ya, yb, yc = one.take(4, S), one.take(4, S), one.take(4, S)
        merged = one.take(KT, S)
        memn = one.take(KT, S)
        sq = one.take(KT, S)
        y1 = arena[:, one.at:one.at + KT * S].rearrange("p (a b) -> p a b", a=KT)
        win_a, win_b = one.take(4, L), one.take(4, L)
        memk, memv = one.take(4, S), one.take(2, 512)
        qm = one.take(4, S)
        om = su
        wst, wpl = one.take(4, P), one.take(4, P)
        bsp = one.take(512)
        tmp = one.take(4, S)
        msc = sc1
        mpt = pt1

        ld_c, ld_x, ld_m, ld_s = sem("ld_consts"), sem("ld_x"), sem("ld_mem"), sem("ld_small")
        landed = [sem(f"landed{i}") for i in range(RING)]
        used = sem("blocks_used")
        act_chain, dve_chain, pool_chain = sem("act_chain"), sem("dve_chain"), sem("pool_chain")
        init_done = sem("init_done")
        ev = {}
        for name in ("qkvs", "gate", "branch", "out", "mem_k", "mem_v", "mem_q", "mem_o", "up", "down"):
            ev[name] = sem("ev_" + name)
        sqd, summed, rooted, normed = sem("squared"), sem("summed"), sem("rooted"), sem("normed")
        at_s, at_m, at_p, at_n = sem("at_scores"), sem("at_max"), sem("at_exp"), sem("at_norm")
        at_t, at_tc, at_o, at_y = sem("at_turned"), sem("at_turned_copied"), sem("at_out"), sem("ya_done")
        sg_n, sg_t, sg_tc, sg_o, sg_y = (sem("sgu_normed"), sem("sgu_turned"), sem("sgu_turned_copied"),
                                         sem("sgu_out"), sem("yb_done"))
        pl_w, pl_o, pl_y = sem("pooled"), sem("pool_out"), sem("yc_done")
        mm_s, mm_m, mm_p, mm_n, mm_t, mm_tc, mm_o, mm_y = [sem("mem_" + s) for s in (
            "scores", "max", "exp", "norm", "turned", "turned_copied", "out", "done")]
        yg_done, res_up = sem("y_scaled"), sem("res_updated")
        halves, normed0, up_sq = sem("half_blocks_used"), sem("mem_normed"), sem("up_squared")
        merged_done = sem("merged_done")
        stored, passed = sem("stored"), sem("passed")

        NORM = {n: i + 1 for i, n in enumerate(
            ["mem", "in", "sgu", "out", "hm", "ym", "hf", "yf",
             "r1", "f1", "kv", "f2", "fin"])}

        def arrived(eng, b, it=None):
            v = 16 * (b // RING + 1)
            eng.wait_ge(landed[b % RING], v if it is None else it * 16 + v)

        two = Space(arena, width)
        r_y, k2, vv, lw, bb, gg, kkn = [two.take(KT, L) for _ in range(7)]
        s16a, s16b = two.take(L), two.take(L)
        loop_at = two.at
        hnp = two.take(KT, L + 1)
        xx = two.take(KT, L)
        xm = [two.take(KT, L) for _ in range(3)]
        w1s, a1s, g1s = two.take(KT, 64), two.take(KT, 64), two.take(KT, 160)
        w2s, a2s = two.take(D), two.take(D)
        g2s, g2t = two.take(D), two.take(D)
        tw, ta, tg0, tg1 = two.take(L), two.take(L), two.take(L), two.take(L)
        two.at = loop_at
        TW = [P, P, META]
        AW = 4 * L

        def sq_blocks(buf, n):
            w = TW[n]
            return buf[0:w, 512 * n:512 * n + 4 * w].rearrange("p (a b) -> p a b", a=4)

        ar = two.take(2, 2, L)
        yy_at = two.at
        bt, kt_ = two.take(2, L), two.take(2, L)
        yy = arena[:, yy_at:yy_at + AW]
        exps = two.at
        cum, ep, en, epre = two.take(2, L), two.take(2, L), two.take(2, L), two.take(2, L)
        dg = arena[:, exps:exps + 2048].rearrange("p (c e j) -> p c e j", c=8, e=4)
        eh = two.take(2, S)
        wu_at = two.at
        bh, kh, vst = two.take(2, S), two.take(2, S), two.take(2, L)
        wu = arena[:, wu_at:wu_at + 12 * P].rearrange("p (n e j) -> p n e j", n=3, e=4)
        lev_at = two.at
        levs = [two.take(AW) for _ in LEVELS[1:]]
        pbuf = arena[:, lev_at:lev_at + 2048].rearrange("p (c e j) -> p c e j", c=8, e=4)
        gbuf = arena[:, lev_at + 2048:lev_at + 4096].rearrange("p (c e j) -> p c e j", c=8, e=4)
        s_at = two.at
        ab, tm, _ = two.take(AW), two.take(AW), two.take(9 * 256 - 2 * AW)
        states = arena[:, s_at:s_at + 9 * 256].rearrange("p (c e j) -> p c e j", c=9, e=4)
        tmt, rb, ak, rk = two.take(AW), two.take(AW), two.take(AW), two.take(AW)
        qq = ak
        vtk, bhk, khk = two.take(3, 2, P), two.take(2, 2, P), two.take(2, 2, P)
        rhs_ = two.take(3, 4, P)
        ecs = two.take(4, 8)

        three = Space(arena, width)
        hf = three.take(KT, L)
        sqb = three.take(KT, L)
        cu = three.take(4, L)
        act2 = three.take(F2, L)
        hq = three.take(KT, L)
        kT, vT, qT, oT = [three.take(KT, L) for _ in range(4)]
        four = Space(arena, width)
        kst, vs2, qst = four.take(2, 384), four.take(2, 384), four.take(2, L)
        ZW = L + (L - P) + META
        zs, ll, ee = four.take(4, ZW), four.take(4, ZW), four.take(4, ZW)
        vk2 = four.take(3, 2, P)
        assert four.at <= KT * L * 2 + 4 * L + F2 * L
        ZC = [0, L, L + L - P]

        for name in ("rw_r", "rw_k", "rw_v", "lora", "exp_kk", "exp_rk", "rw_o", "ffa_up", "ffa_down",
                     "sb_k", "sb_v", "sb_q", "sb_o", "ffb_up", "ffb_down"):
            ev[name] = sem("ev_" + name)
        ld_l = sem("ld_lora")
        mixed = sem("mixed")
        lora_mm, head_mm, lnx, y_root = sem("lora_mm"), sem("head_mm"), sem("lnx"), sem("y_root")
        pe2 = Marks(sem("time_mix_pe"), "w1 a1 g1 kk_sum rk_sum y_sum yv_sum")
        act2m = Marks(sem("time_mix_act"), "tw ta tg tg1 kk_root")
        dve2 = Marks(sem("time_mix_dve"), "kk_sq rk kk_floor kk_inv kkn mu yc_sq var y_inv")

        def tiles_of(m):
            return range(3) if 2 * m <= META else range(2)

        def top(n):
            return LEVELS[-1] if n < 2 else META // 2

        def per_level(*kinds):
            return " " + " ".join(f"{k}{m}_{n}" for m in LEVELS[1:] for k in kinds for n in tiles_of(m)) + " "
        rp = Marks(sem("chunk_pe"), "turned ends a0 a1 a2" + per_level("y", "u") +
                   "akv_0 akv_1 akv_2 wu_0 wu_1 wu_2 pg_0 pg_1 "
                   "s2 q_0 s3 q_1 s4 q_2 s5 s6 s7 s8 yo_0 yo_1 yo_2")
        ra = Marks(sem("chunk_act"), "exps vturned turned ab0 ab1 ab2" + per_level("y") +
                   "wu_0 wu_1 wu_2 g_0 g_1 q_0 q_1 q_2")
        rd = Marks(sem("chunk_dve"), "cum ar bk hats turned ends a0 t0_0 a1 t0_1 a2 t0_2" + per_level("t") +
                   "akv_0 akv_1 akv_2 p_0 p_1 s1 s2 s3 s4 s5 s6 s7 s8 yo_0 yo_1 yo_2")
        rl = Marks(sem("chunk_pool"), "v" + per_level("x"))
        ffc, ffs, ffm = sem("conv_tap"), sem("conv_silu"), sem("conv_product")
        sp_ = Marks(sem("stick_pe"), "v z sfx o")
        sa = Marks(sem("stick_act"), "k abs exp ln w")
        sd = Marks(sem("stick_dve"), "v q vk l arg o")
        zeroed = sem("pads_zeroed")
        CHUNK_LINKS, STICK_LINKS = 8, 2

        def take_wait(eng):
            eng.sem_inc(passed, 1)

        def gps(n, w=L):
            return ps[:, n, 0:w]

        def second_sync(sp):
            sp.wait_ge(normed, 9)
            sp.dma_start(out_t, hf[:, :, META:L]).then_inc(stored, 16)
            sp.wait_ge(stored, 16)

        def second_tensor(pe, mm, tiles, total):
            pe.wait_ge(sqd, 9)
            total(6, xm[0], KT, L, "r1")
            pe.wait_ge(ld_l, 16 * 7)

            def lora_in(buf, w, m0, m1, bank, mark, k_mix):
                pe.wait_ge(mixed, k_mix)
                for k in range(KT):
                    last = mm(ps[0:m1 - m0, bank, 0:L], w[:, k, m0:m1], buf[:, k, :], k == 0, k == KT - 1)
                if mark:
                    pe2.reach(last, mark)
            lora_in(xm[0], w1s, 0, 64, 4, "w1", 1)
            lora_in(xm[1], a1s, 0, 64, 5, "a1", 2)
            pe.wait_ge(rooted, 9)
            lora_in(xm[2], g1s, 0, P, 6, None, 3)
            lora_in(xm[2], g1s, P, 160, 7, "g1", 3)
            pe.sem_inc(ev["rw_r"], GB)
            pe.sem_inc(ev["rw_k"], GB)
            pe.sem_inc(ev["rw_v"], GB)
            pe.sem_inc(ev["lora"], GB)
            pe.wait_ge(mixed, 4)
            tiles("rw_r", FIRST["rw_r"], 8, xm[0], L)

            def lora_out(w, src, j0, w_b=None, src_b=None):
                for n in range(KT):
                    j = j0 + n
                    pe.wait_ge(ev["lora"], j + 1)
                    o = gps(4 + j % GB)
                    last = mm(o, w[0:src.shape[0], n * P:(n + 1) * P], src, True, w_b is None)
                    if w_b is not None:
                        last = mm(o, w_b[0:32, n * P:(n + 1) * P], src_b, False, True)
                    last.then_inc(lora_mm, 1)
            act2m.wait(pe, "tg1")
            lora_out(w2s, tw[0:64, :], 0)
            pe.wait_ge(ev["rw_r"], GB + 8)
            pe.wait_ge(mixed, 5)
            tiles("rw_k", FIRST["rw_k"], 8, xm[1], L)
            lora_out(a2s, ta[0:64, :], 8)
            lora_out(g2s, tg0[:, :], 16, g2t, tg1[0:32, :])
            pe.wait_ge(ev["rw_k"], GB + 8)
            pe.wait_ge(mixed, 6)
            tiles("rw_v", FIRST["rw_v"], 8, xm[2], L)

            def to_heads(src, bank, mark):
                for n in range(KT):
                    last = mm(ps[0:16, bank, 0:L], const("to_head")[:, n * 16:(n + 1) * 16], src[:, n, :],
                              n == 0, n == KT - 1)
                pe2.reach(last, mark)

            def from_heads(src, name, j0=0):
                for n in range(KT):
                    pe.wait_ge(ev[name], j0 + n + 1)
                    mm(gps(4 + n % GB), const("from_head")[0:16, n * P:(n + 1) * P], src[0:16, :]
                       ).then_inc(head_mm, 1)
            dve2.wait(pe, "kk_sq")
            pe.wait_ge(ev["lora"], GB + 24)
            to_heads(xx, 4, "kk_sum")
            dve2.wait(pe, "rk")
            to_heads(hnp[:, :, 0:L], 5, "rk_sum")
            dve2.wait(pe, "kk_inv")
            pe.sem_inc(ev["exp_kk"], GB)
            from_heads(s16a, "exp_kk")
            dve2.wait(pe, "kkn")

            with pe.Fori(0, 4) as it:
                chunk_tensor(pe, mm, it)

            rd.wait(pe, "yo_2", 3)
            to_heads(r_y, 4, "y_sum")
            dve2.wait(pe, "mu")
            from_heads(s16a, "exp_kk", 8)
            dve2.wait(pe, "yc_sq")
            pe.wait_ge(ev["exp_kk"], GB + 16)
            to_heads(lw, 4, "yv_sum")
            dve2.wait(pe, "y_inv")
            from_heads(s16a, "exp_kk", 16)
            pe.wait_ge(ev["exp_kk"], GB + 24)
            pe.sem_inc(ev["exp_rk"], GB)
            from_heads(s16b, "exp_rk")
            pe.wait_ge(mixed, 7)
            pe.sem_inc(ev["rw_o"], GB)
            tiles("rw_o", FIRST["rw_o"], 8, bb, L)
            ffn_tensor(pe, mm, tiles, total, "ffa", 10, 5)
            pe.wait_ge(sqd, 11)
            total(6, sqb, KT, L, "kv")
            pe.wait_ge(normed, 6)
            pe.sem_inc(ev["sb_k"], GB)
            tiles("sb_k", FIRST["sb_k"], 8, hf, L)
            pe.wait_ge(ev["sb_k"], GB + 8)
            pe.sem_inc(ev["sb_v"], GB)
            tiles("sb_v", FIRST["sb_v"], 8, hf, L)
            pe.wait_ge(ev["sb_v"], GB + 8)
            pe.wait_ge(normed, 7)
            pe.sem_inc(ev["sb_q"], GB)
            tiles("sb_q", FIRST["sb_q"], 8, hq, L)
            pe.wait_ge(ev["sb_q"], GB + 8)
            with pe.Fori(0, 4) as it:
                stick_tensor(pe, mm, it)
            sd.wait(pe, "o", 3)
            pe.sem_inc(ev["sb_o"], GB)
            tiles("sb_o", FIRST["sb_o"], 8, oT, L)
            ffn_tensor(pe, mm, tiles, total, "ffb", 12, 8)
            pe.wait_ge(sqd, 13)
            total(6, sqb, KT, L, "fin")

        def ffn_tensor(pe, mm, tiles, total, name, n_sq, n_normed):
            pe.wait_ge(sqd, n_sq)
            total(6, sqb, KT, L, name)
            pe.wait_ge(normed, n_normed)
            up, down = name + "_up", name + "_down"
            pe.sem_inc(ev[up], GB)
            tiles(up, FIRST[up], 2 * F2, hf, L)
            pe.wait_ge(ev[up], GB + 2 * F2)
            pe.wait_ge(ffm, 2 + F2 if name == "ffa" else 4 + 2 * F2)
            pe.sem_inc(ev[down], GB)
            for n in range(KT):
                pe.wait_ge(ev[down], n + 1)
                for q in range(F2B):
                    b = FIRST[down] + n * F2B + q
                    arrived(pe, b)
                    for k in range(8 * q, min(F2, 8 * q + 8)):
                        last = mm(gps(n % GB), ring[:, b % RING, (k - 8 * q) * P:(k - 8 * q + 1) * P],
                                  act2[:, k, :], k == 0, k == F2 - 1)
                    last.then_inc(used, 1)

        def chunk_tensor(pe, mm, it):
            tr = nc.tensor.transpose

            def head(e):
                p, q = e // 2, e % 2
                return p, q, slice(64 * p, 64 * p + 64)
            rd.wait(pe, "ar", it)
            for n in range(2):
                for q in range(2):
                    tr(ps[:, 0, (2 * n + q) * P:(2 * n + q + 1) * P], ar[:, 0, q, n * P:(n + 1) * P], ident)
            rl.wait(pe, "v", it)
            for n in range(2):
                for q in range(2):
                    tr(ps[:, 1, (2 * n + q) * P:(2 * n + q + 1) * P], vst[:, q, n * P:(n + 1) * P], ident)
            for q in range(2):
                tr(ps[0:META, 5, q * P:(q + 1) * P], ar[:, 0, q, S:L], ident)
                tr(ps[0:META, 5, (2 + q) * P:(3 + q) * P], vst[:, q, S:L], ident)
            rd.wait(pe, "hats", it)
            for n in range(2):
                for q in range(2):
                    tr(ps[:, 2, (2 * n + q) * P:(2 * n + q + 1) * P], bh[:, q, n * P:(n + 1) * P], ident)
                    last = tr(ps[:, 3, (2 * n + q) * P:(2 * n + q + 1) * P], kh[:, q, n * P:(n + 1) * P], ident)
            rp.reach(last, "turned")
            for e in range(4):
                p, q, r = head(e)
                last = mm(ps[0:64, 4, 8 * e:8 * e + 8], const("ident")[:, r], ep[:, q, CH - 1:S:CH])
            rp.reach(last, "ends")
            for n in range(3):
                t0, w = n * P, TW[n]
                if n == 0:
                    ra.wait(pe, "turned", it)
                    rd.wait(pe, "ends", it)
                else:
                    rd.wait(pe, f"a{n - 1}", it)
                    ra.wait(pe, f"ab{n - 1}", it)
                if n == 2:
                    take_wait(pe)
                for p in range(2):
                    r = slice(64 * p, 64 * p + 64)
                    for q in range(2):
                        both = ar[r, :, q, t0:t0 + w]
                        mm(ps[0:w, p, q * 2 * w:(q + 1) * 2 * w], bt[r, q, t0:t0 + w], both)
                        mm(ps[0:w, 2 + p, q * 2 * w:(q + 1) * 2 * w], kt_[r, q, t0:t0 + w], both)
                        last = mm(ps[0:w, 4 + p, q * w:(q + 1) * w], ar[r, 0, q, t0:t0 + w],
                                  bt[r, q, t0:t0 + w])
                rp.reach(last, f"a{n}")
            ybank, uabank, ubbank = [0, 1, 6], [2, 4, 7], [3, 5, 7]
            prev = "t0"
            for li, m in enumerate(LEVELS[1:]):
                for n in tiles_of(m):
                    w = TW[n]
                    rd.wait(pe, "t0_2" if li == 0 and n == 0 else f"{prev}_{n}", it)
                    rl.wait(pe, f"x{m}_{n}", it)
                    if n == 2:
                        take_wait(pe)
                    for e in range(4):
                        last = mm(ps[0:w, ybank[n], e * w:(e + 1) * w], sq_blocks(levs[li], n)[:, e, :],
                                  sq_blocks(tm, n)[:, e, :])
                    rp.reach(last, f"y{m}_{n}")
                for n in tiles_of(m):
                    w = TW[n]
                    ra.wait(pe, f"y{m}_{n}", it)
                    o2 = 64 if n == 2 else 0
                    if n == 2:
                        take_wait(pe)
                    for e in range(4):
                        y_e, tt_e = sq_blocks(yy, n)[:, e, :], sq_blocks(tmt, n)[:, e, :]
                        if m != top(n):
                            mm(ps[0:w, uabank[n], e * w:(e + 1) * w], tt_e, y_e)
                        last = mm(ps[0:w, ubbank[n], o2 + e * w:o2 + (e + 1) * w], y_e, tt_e)
                    rp.reach(last, f"u{m}_{n}")
                prev = f"t{m}"
            for n in range(3):
                w = TW[n]
                rd.wait(pe, f"t{top(n)}_{n}", it)
                if n == 2:
                    take_wait(pe)
                for e in range(4):
                    p, q, r = head(e)
                    last = mm(ps[0:w, n, e * 64:(e + 1) * 64], sq_blocks(ak, n)[:, e, :], vtk[0:w, n, q, r])
                rp.reach(last, f"akv_{n}")
            for n in range(3):
                w = TW[n]
                rd.wait(pe, f"akv_{n}", it)
                if n == 2:
                    take_wait(pe)
                for e in range(4):
                    last = mm(ps[0:w, 3 + n, e * P:(e + 1) * P], sq_blocks(tmt, n)[:, e, :], rhs_[0:w, n, e, :])
                rp.reach(last, f"wu_{n}")
            ra.wait(pe, "wu_2", it)
            for n in range(2):
                for c in range(4):
                    rows = slice(CH * c, CH * c + CH)
                    for e in range(4):
                        p, q, r = head(e)
                        o = ps[0:64, 4 * n + c, 64 * e:64 * e + 64]
                        mm(o, wu[rows, n, e, 0:64], bhk[rows, n, q, r])
                    for e in range(4):
                        p, q, r = head(e)
                        o = ps[0:64, 4 * n + c, 256 + 64 * e:256 + 64 * e + 64]
                        mm(o, bhk[rows, n, q, r], wu[rows, n, e, 64:P], True, False)
                        last = mm(o, khk[rows, n, q, r], vtk[rows, n, q, r], False, True)
                rp.reach(last, f"pg_{n}")

            def state(c):
                rd.wait(pe, f"s{c - 1}", it)
                take_wait(pe)
                for e in range(4):
                    last = mm(ps[0:64, 0, 64 * e:64 * e + 64], pbuf[0:64, c - 1, e, :], states[0:64, c - 1, e, :])
                rp.reach(last, f"s{c}")

            def queries(n):
                w = TW[n]
                if n == 0:
                    ra.wait(pe, "g_0", it)
                for e in range(4):
                    p, q, r = head(e)
                    o = ps[0:64, 1 + n, e * w:(e + 1) * w]
                    mm(o, wu[0:w, n, e, 0:64], sq_blocks(rb, n)[:, e, :], True, False)
                    last = mm(o, const("ident")[:, r], ar[:, 1, q, n * P:n * P + w], False, True)
                rp.reach(last, f"q_{n}")
            for c in range(2, 9):
                state(c)
                if c < 5:
                    queries(c - 2)
            rd.wait(pe, "s8", it)
            for n in range(3):
                w = TW[n]
                ra.wait(pe, f"q_{n}", it)
                for e in range(4):
                    p, q, r = head(e)
                    o = ps[r, 5 + n, q * w:(q + 1) * w]
                    mm(o, wu[0:w, n, e, 64:P], sq_blocks(rb, n)[:, e, :], True, False)
                    chunks = [c for c in range(4 * n, min(4 * n + 4, 9)) if c]
                    last = mm(o, vtk[0:w, n, q, r], sq_blocks(rk, n)[:, e, :], False, False)
                    for c in chunks:
                        a0 = (c - 4 * n) * CH
                        a1 = min(a0 + CH, w)
                        last = mm(ps[r, 5 + n, q * w + a0:q * w + a1], states[0:64, c, e, :],
                                  qb(n)[0:64, e, a0:a1], False, c == chunks[-1])
                rp.reach(last, f"yo_{n}")

        def qb(n):
            w = TW[n]
            return qq[:, 512 * n:512 * n + 4 * w].rearrange("p (a b) -> p a b", a=4)

        def stick_tensor(pe, mm, it):
            sd.wait(pe, "v", it)
            for n in range(3):
                for q in range(2):
                    last = nc.tensor.transpose(ps[:, 4 + n, q * P:(q + 1) * P], vs2[:, q, n * P:(n + 1) * P],
                                               ident)
            sp_.reach(last, "v")
            sa.wait(pe, "k", it)
            sd.wait(pe, "q", it)
            for q in range(2):
                for p in range(2):
                    r = slice(64 * p, 64 * p + 64)
                    for i in range(3):
                        last = mm(ps[:, 2 * q + p, ZC[i]:ZC[i] + L - i * P], kst[r, q, i * P:(i + 1) * P],
                                  qst[r, q, i * P:L])
            sp_.reach(last, "z")
            sd.wait(pe, "l", it)
            for e in range(4):
                for i in range(3):
                    last = mm(ps[:, 4 + e, ZC[i]:ZC[i] + L - i * P], const("after"), ll[:, e, ZC[i]:ZC[i] + L - i * P],
                              True, i == 2)
                    for j in range(i + 1, 3):
                        w = L - j * P
                        last = mm(ps[:, 4 + e, ZC[i] + (j - i) * P:ZC[i] + (j - i) * P + w], const("ones"),
                                  ll[:, e, ZC[j]:ZC[j] + w], False, j == 2)
            sp_.reach(last, "sfx")
            sa.wait(pe, "w", it)
            for q in range(2):
                for p in range(2):
                    r = slice(64 * p, 64 * p + 64)
                    for i in range(3):
                        last = mm(ps[r, q, i * P:L], vk2[:, i, q, r], ee[:, 2 * q + p, ZC[i]:ZC[i] + L - i * P],
                                  i == 0, i == 2)
            sp_.reach(last, "o")

        def second_scalar(act, link, f, root, squares_of_y):
            cp = nc.scalar.copy
            for dst, src in ((w1s, w1_d), (a1s, a1_d), (g1s, g1_d), (w2s[0:64, :], w2_d), (a2s[0:64, :], a2_d),
                             (g2s, g2_d[0:P, :]), (g2t[0:32, :], g2_d[P:160, :])):
                if dst is w1s:
                    act.wait_ge(res_up, 3)
                act.dma_start(dst, src).then_inc(ld_l, 16)
            f(xm[0], res[:], ACT.Square).then_inc(sqd, 1)
            root(6, L, which=9)
            pe2.wait(act, "w1")
            act2m.reach(f(tw[0:64, :], ps[0:64, 4, 0:L], ACT.Tanh), "tw")
            pe2.wait(act, "a1")
            act2m.reach(cp(ta[0:64, :], ps[0:64, 5, 0:L]), "ta")
            pe2.wait(act, "g1")
            act2m.reach(f(tg0, ps[:, 6, 0:L], ACT.Sigmoid), "tg")
            act2m.reach(f(tg1[0:32, :], ps[0:32, 7, 0:L], ACT.Sigmoid), "tg1")
            for j in range(24):
                act.wait_ge(lora_mm, j + 1)
                n, src = j % 8, gps(4 + j % GB)
                if j < 8:
                    ins = f(lw[:, n, :], src, ACT.Sigmoid, bias=col("w0", n))
                elif j < 16:
                    ins = f(bb[:, n, :], src, ACT.Sigmoid, bias=col("a0", n))
                else:
                    ins = cp(gg[:, n, :], src)
                ins.then_inc(ev["lora"], 1)
            dve2.wait(act, "kk_floor")
            act2m.reach(f(s16a[0:16, :], s16a[0:16, :], ACT.Sqrt), "kk_root")
            with act.Fori(0, 4) as it:
                chunk_scalar(act, it)
            dve2.wait(act, "var")
            f(s16a[0:16, :], s16a[0:16, :], ACT.Sqrt).then_inc(y_root, 1)
            for n in range(KT):
                act.wait_ge(ev["exp_kk"], GB + 16 + n + 1)
                ins = f(kkn[:, n, :], kkn[:, n, :], ACT.Identity, scale=col("lnx_g", n), bias=col("lnx_b", n))
                ins.then_inc(lnx, 1)
            act.wait_ge(ev["rw_o"], GB + 8)
            f(sqb, res[:], ACT.Square).then_inc(sqd, 1)
            ffn_scalar(act, f, root, "ffa", 0, 10)
            act.wait_ge(ev["ffa_down"], GB + 8)
            f(sqb, res[:], ACT.Square).then_inc(sqd, 1)
            root(6, L, which=11)
            act.wait_ge(zeroed, 1)
            with act.Fori(0, 4) as it:
                stick_scalar(act, f, it)
            act.wait_ge(ev["sb_o"], GB + 8)
            f(sqb, res[:], ACT.Square).then_inc(sqd, 1)
            ffn_scalar(act, f, root, "ffb", 1, 12)
            act.wait_ge(ev["ffb_down"], GB + 8)
            f(sqb, res[:], ACT.Square).then_inc(sqd, 1)
            root(6, L, which=13)

        def ffn_scalar(act, f, root, name, layer, which):
            root(6, L, which=which)
            b = FIRST[name + "_up"]
            wc = COLS["conv_w"] + layer * 3 * 2 * F2 + 2 * 2 * F2
            bc = COLS["conv_b"] + layer * 2 * F2
            m0 = layer * (2 + F2)

            def pair(m, it=None):
                for s in (2 * m, 2 * m + 1):
                    add = (lambda v: v) if it is None else (lambda v: it * 8 + v)
                    addp = (lambda v: v) if it is None else (lambda v: it * 4 + v)
                    act.wait_ge(used, add(b + s + 1))
                    act.wait_ge(ffm, addp(m0 + m + 1))
                    if it is None:
                        sc, bi = cols[:, wc + s:wc + s + 1], cols[:, bc + s:bc + s + 1]
                    else:
                        sc, bi = cols[:, bass.ds(it * 8 + (wc + s), 1)], cols[:, bass.ds(it * 8 + (bc + s), 1)]
                    f(cu[:, s % 4, :], gps(s % GB), ACT.Identity, scale=sc, bias=bi).then_inc(ffc, 1)
                act.wait_ge(ev[name + "_up"], add(GB + 2 * m + 1))
                f(cu[:, (2 * m) % 4, :], cu[:, (2 * m) % 4, :], ACT.Silu).then_inc(ffs, 1)
            with act.Fori(0, 5) as it:
                for m in range(4):
                    pair(m, it)
            for m in (20, 21):
                pair(m)

        def chunk_scalar(act, it):
            f, cp = nc.scalar.activation, nc.scalar.copy
            rd.wait(act, "cum", it)
            f(ep, cum, ACT.Exp)
            f(en, cum, ACT.Exp, scale=-1.0)
            f(epre, epre, ACT.Exp)
            ra.reach(f(eh, eh, ACT.Exp), "exps")
            rp.wait(act, "turned", it)
            src = ps[:, 0, :].rearrange("p (n q r j) -> p n q r j", n=2, q=2, r=2)
            for n in range(2):
                for r in range(2):
                    cp(rhs_[:, n, 2 * r:2 * r + 2, 0:64], src[:, n, :, r, :])
            ra.reach(cp(vtk[:, 0:2], ps[:, 1, :].rearrange("p (n q j) -> p n q j", n=2, q=2)), "vturned")
            ra.reach(cp(bhk, ps[:, 2, :].rearrange("p (n q j) -> p n q j", n=2, q=2)), "turned")
            for n in range(3):
                w = TW[n]
                rp.wait(act, f"a{n}", it)
                ab4 = sq_blocks(ab, n)
                for p in range(2):
                    last = cp(ab4[:, 2 * p:2 * p + 2, :],
                              ps[0:w, p, 0:4 * w].rearrange("p (q k t) -> p q k t", q=2, k=2)[:, :, 0, :])
                ra.reach(last, f"ab{n}")
            ybank = [0, 1, 6]
            for m in LEVELS[1:]:
                for n in tiles_of(m):
                    w = TW[n]
                    rp.wait(act, f"y{m}_{n}", it)
                    ra.reach(cp(sq_blocks(yy, n), ps[0:w, ybank[n], 0:4 * w].rearrange(
                        "p (a b) -> p a b", a=4)), f"y{m}_{n}")
            for n in range(3):
                w = TW[n]
                rp.wait(act, f"wu_{n}", it)
                ra.reach(cp(wu[0:w, n], ps[0:w, 3 + n, :].rearrange("p (a b) -> p a b", a=4)), f"wu_{n}")
            for n in range(2):
                rp.wait(act, f"pg_{n}", it)
                rd.wait(act, f"p_{n}", it)
                ra.reach(cp(gbuf[0:64, 4 * n:4 * n + 4], ps[0:64, 4 * n:4 * n + 4, 256:512].rearrange(
                    "p c (e j) -> p c e j", e=4)), f"g_{n}")
            for n in range(3):
                w = TW[n]
                rp.wait(act, f"q_{n}", it)
                ra.reach(cp(qb(n)[0:64], ps[0:64, 1 + n, 0:4 * w].rearrange("p (a b) -> p a b", a=4)), f"q_{n}")

        def stick_scalar(act, f, it):
            with_k = nc.scalar.copy(kst[:, :, 0:L], kT[:, bass.ds(it * 2, 2), :])
            sa.reach(with_k, "k")
            sp_.wait(act, "z", it)
            z = ps[:, 0:4, 0:ZW]
            sa.reach(f(ee, z, ACT.Abs, scale=0.125), "abs")
            sa.wait(act, "abs", it)
            sa.reach(f(ee, ee, ACT.Exp, scale=-1.0), "exp")
            sa.wait(act, "exp", it)
            sa.reach(f(ee, ee, ACT.Ln, bias=one_c), "ln")
            sd.wait(act, "arg", it)
            sa.reach(f(ee, zs, ACT.Exp), "w")

        def second_vector(dve, link, v, tt, stt, ts, inverse_root, residual, normed_to, take):
            cpv = v.tensor_copy
            dve.wait_ge(sqd, 9)
            link(v.memset(hnp[:, :, 0:1], 0.0))
            hn = hnp[:, :, 1:L + 1]
            link(tt(hn, res[:], col_wide("mix_g", 0, KT, L), ALU.mult))
            normed_to(hn, 9, L, 4)
            dve.wait_ge(normed, 4)
            link(tt(xx, hnp[:, :, 0:L], hn, ALU.subtract))
            for j, (which, buf) in enumerate(((1, 0), (4, 1), (5, 2), (0, 0), (2, 1), (3, 2))):
                if j >= 3:
                    pe2.wait(dve, ("w1", "a1", "g1")[j - 3])
                for k in range(KT):
                    last = stt(out=xm[buf][:, k, :], in0=xx[:, k, :], scalar=col("rw_mix", 8 * which + k),
                               in1=hn[:, k, :], op0=ALU.mult, op1=ALU.add)
                last.then_inc(mixed, 1)
            dve.wait_ge(mixed, 6)
            take("rw_r", FIRST["rw_r"], 8, r_y, L)
            take("rw_k", FIRST["rw_k"], 8, k2, L)
            dve.wait_ge(ev["rw_k"], GB + 8)
            link(tt(kkn, k2, col_wide("k_k", 0, KT, L), ALU.mult))
            dve2.reach(tt(xx, kkn, kkn, ALU.mult), "kk_sq")
            dve.wait_ge(ev["lora"], GB + 16)
            link(stt(out=hnp[:, :, 0:L], in0=bb, scalar=-1.0, in1=col_wide("k_a", 0, KT, L), op0=ALU.add,
                     op1=ALU.mult))
            link(stt(out=k2, in0=hnp[:, :, 0:L], scalar=1.0, in1=k2, op0=ALU.add, op1=ALU.mult))
            link(tt(hnp[:, :, 0:L], r_y, k2, ALU.mult))
            dve2.reach(tt(hnp[:, :, 0:L], hnp[:, :, 0:L], col_wide("r_k", 0, KT, L), ALU.mult), "rk")
            link(ts(lw, lw, -float(np.exp(-0.5)), None, ALU.mult))
            take("rw_v", FIRST["rw_v"], 8, vv, L)
            pe2.wait(dve, "kk_sum")
            dve2.reach(ts(s16a[0:16, :], ps[0:16, 4, 0:L], 1e-24, None, ALU.max), "kk_floor")
            pe2.wait(dve, "rk_sum")
            link(cpv(s16b[0:16, :], ps[0:16, 5, 0:L]))
            act2m.wait(dve, "kk_root")
            dve2.reach(v.reciprocal(s16a[0:16, :], s16a[0:16, :]), "kk_inv")

            def heads_times(dst, src, name, mm0, op=ALU.mult, ext=None):
                for n in range(KT):
                    dve.wait_ge(head_mm, mm0 + n + 1)
                    if ext is not None:
                        ext(n)
                    tt(dst[:, n, :], src[:, n, :], gps(4 + n % GB), op).then_inc(ev[name], 1)
            heads_times(kkn, kkn, "exp_kk", 0)
            dve.wait_ge(ev["exp_kk"], GB + 8)
            dve2.reach(tt(bb, kkn, bb, ALU.mult), "kkn")
            dve2.wait(dve, "kkn")
            with dve.Fori(0, 4) as it:
                link.enter(it, CHUNK_LINKS)
                chunk_vector(dve, link, it, v, tt, stt, cpv)
                link.leave(4)
            rd.wait(dve, "yo_2", 3)
            pe2.wait(dve, "y_sum")
            dve2.reach(ts(s16a[0:16, :], ps[0:16, 4, 0:L], 1.0 / 64, None, ALU.mult), "mu")
            heads_times(kkn, r_y, "exp_kk", 8, ALU.subtract)
            dve.wait_ge(ev["exp_kk"], GB + 16)
            dve2.reach(tt(lw, kkn, kkn, ALU.mult), "yc_sq")
            pe2.wait(dve, "yv_sum")
            dve2.reach(ts(s16a[0:16, :], ps[0:16, 4, 0:L], 1.0 / 64, GN_EPS, ALU.mult, ALU.add), "var")
            dve.wait_ge(y_root, 1)
            dve2.reach(v.reciprocal(s16a[0:16, :], s16a[0:16, :]), "y_inv")
            heads_times(kkn, kkn, "exp_kk", 16)
            heads_times(r_y, vv, "exp_rk", 24)
            dve.wait_ge(lnx, 8)
            dve.wait_ge(ev["exp_rk"], GB + 8)
            link(tt(kkn, kkn, r_y, ALU.add))
            tt(bb, kkn, gg, ALU.mult).then_inc(mixed, 1)

            def add_to_res(name, per):
                for j in range(KT):
                    dve.wait_ge(used, FIRST[name] + per * (j + 1))
                    tt(res[:, j, :], res[:, j, :], gps(j % GB), ALU.add).then_inc(ev[name], 1)
            add_to_res("rw_o", 1)
            ffn_vector(dve, link, tt, stt, normed_to, add_to_res, "ffa", 0, 10)
            dve.wait_ge(ev["ffa_down"], GB + 8)
            link(tt(hf, res[:], col_wide("kv_g", 0, KT, L), ALU.mult))
            link(tt(hq, res[:], col_wide("mix_g", 8, KT, L), ALU.mult))
            normed_to(hf, 11, L, 6)
            tt(hq, hq, over(rs[:, 0:L], KT), ALU.mult).then_inc(normed, 1)
            take("sb_k", FIRST["sb_k"], 8, kT, L)
            take("sb_v", FIRST["sb_v"], 8, vT, L)
            take("sb_q", FIRST["sb_q"], 8, qT, L)
            v.memset(kst[:, :, L:384], 0.0)
            v.memset(vs2[:, :, L:384], 0.0).then_inc(zeroed, 1)
            with dve.Fori(0, 4) as it:
                link.enter(it, STICK_LINKS)
                stick_vector(dve, link, it, v, tt, stt, ts, cpv)
                link.leave(4)
            sd.wait(dve, "o", 3)
            add_to_res("sb_o", 1)
            ffn_vector(dve, link, tt, stt, normed_to, add_to_res, "ffb", 1, 12)
            dve.wait_ge(ev["ffb_down"], GB + 8)
            link(tt(hf, res[:], col_wide("fin_g", 0, KT, L), ALU.mult))
            normed_to(hf, 13, L, 9)

        def ffn_vector(dve, link, tt, stt, normed_to, add_to_res, name, layer, which):
            dve.wait_ge(ev["rw_o" if layer == 0 else "sb_o"], GB + 8)
            link(tt(hf, res[:], col_wide("ffn_g", 8 * layer, KT, L), ALU.mult))
            normed_to(hf, which, L, 0)
            wc = COLS["conv_w"] + layer * 3 * 2 * F2
            dve.sem_inc(ffm, 2)

            def pair(m, it=None):
                add = (lambda x: x) if it is None else (lambda x: it * 8 + x)
                addp = (lambda x: x) if it is None else (lambda x: it * 4 + x)
                for s in (2 * m, 2 * m + 1):
                    dve.wait_ge(ffc, add(layer * 2 * F2 + s + 1))
                    for back, tap in ((1, 1), (2, 0)):
                        at = wc + tap * 2 * F2 + s
                        w = cols[:, at:at + 1] if it is None else cols[:, bass.ds(it * 8 + at, 1)]
                        c = cu[:, s % 4, back:L]
                        ins = stt(out=c, in0=ps[:, s % GB, 0:L - back], scalar=w, in1=c, op0=ALU.mult,
                                  op1=ALU.add)
                        if back == 1:
                            link(ins)
                        else:
                            ins.then_inc(ev[name + "_up"], 1)
                dve.wait_ge(ev[name + "_up"], add(GB + 2 * m + 2))
                dve.wait_ge(ffs, addp(layer * F2 + m + 1))
                dst = act2[:, m, :] if it is None else act2[:, bass.ds(it * 4 + m, 1), :]
                tt(dst, cu[:, (2 * m) % 4, :], cu[:, (2 * m + 1) % 4, :], ALU.mult).then_inc(ffm, 1)
            with dve.Fori(0, 5) as it:
                link.enter(it, 8)
                for m in range(4):
                    pair(m, it)
                link.leave(5)
            for m in (20, 21):
                pair(m)
            add_to_res(name + "_down", F2B)

        def masks(name, w):
            return const(name, w)[:, 0:w].unsqueeze(1).unsqueeze(1).to_broadcast([w, 2, 2, w])

        def chunk_vector(dve, link, it, v, tt, stt, cpv):
            two_ = bass.ds(it * 2, 2)
            for q in range(2):
                link(v.tensor_tensor_scan(cum[:, q, :], const("scan"),
                                          lw[:, bass.ds(it * 2 + q, 1), :].rearrange("p a b -> p (a b)"),
                                          0.0, ALU.mult, ALU.add))
            tt(epre, cum, lw[:, two_, :], ALU.subtract)
            c4 = cum[:, :, 0:S].rearrange("p q (c t) -> p q c t", c=8)
            rd.reach(tt(eh.rearrange("p q (c t) -> p q c t", c=8),
                        c4[:, :, :, CH - 1:CH].to_broadcast([P, 2, 8, CH]), c4, ALU.subtract), "cum")
            ra.wait(dve, "exps", it)
            stt(out=ar[:, 0], in0=kkn[:, two_, :], scalar=-1.0, in1=epre, op0=ALU.mult, op1=ALU.mult)
            rd.reach(tt(ar[:, 1], r_y[:, two_, :], ep, ALU.mult), "ar")
            tt(bt, bb[:, two_, :], en, ALU.mult)
            rd.reach(tt(kt_, k2[:, two_, :], en, ALU.mult), "bk")
            tt(bh, bb[:, two_, 0:S], eh, ALU.mult)
            rd.reach(tt(kh, k2[:, two_, 0:S], eh, ALU.mult), "hats")
            rp.wait(dve, "turned", it)
            cpv(khk, ps[:, 3, :].rearrange("p (n q j) -> p n q j", n=2, q=2))
            last = ps[0:META, 5, :].rearrange("p (k q r j) -> p k q r j", k=2, q=2, r=2)
            for r in range(2):
                cpv(rhs_[0:META, 2, 2 * r:2 * r + 2, 0:64], last[:, 0, :, r, :])
            rd.reach(cpv(vtk[0:META, 2], ps[0:META, 5, 256:512].rearrange("p (q j) -> p q j", q=2)), "turned")
            rp.wait(dve, "ends", it)
            rd.reach(cpv(ecs[0:64], ps[0:64, 4, 0:32].rearrange("p (e c) -> p e c", e=4)), "ends")
            for n in range(3):
                w = TW[n]
                rp.wait(dve, f"a{n}", it)
                if n == 1:
                    rd.wait(dve, "ends", it)
                    tt(dg[0:64], const("ident", 64)[:, 0:64].unsqueeze(1).unsqueeze(1).to_broadcast(
                        [64, 8, 4, 64]), ecs_wide(), ALU.mult)
                ab_rb = ps[0:w, 0:2, 0:4 * w].rearrange("p b (q k t) -> p b q k t", q=2, k=2)
                ak_rk = ps[0:w, 2:4, 0:4 * w].rearrange("p b (q k t) -> p b q k t", q=2, k=2)

                def out4(buf):
                    return sq_blocks(buf, n).rearrange("p (b q) t -> p b q t", b=2)
                tt(out4(ak), ak_rk[:, :, :, 0, :], masks("chunk_strict", w), ALU.mult)
                tt(out4(rk), ak_rk[:, :, :, 1, :], masks("chunk_incl", w), ALU.mult)
                link(tt(out4(tm), ps[0:w, 4:6, 0:2 * w].rearrange("p b (q t) -> p b q t", q=2),
                        masks("level1t", w), ALU.mult))
                ra.wait(dve, f"ab{n}", it)
                rd.reach(tt(out4(rb), ab_rb[:, :, :, 1, :], masks("chunk_incl", w), ALU.mult), f"a{n}")
                tt(out4(tm), out4(tm), masks("ident", w), ALU.add)
                link(tt(out4(tmt), out4(ab), masks("level1", w), ALU.mult))
                rd.reach(tt(out4(tmt), out4(tmt), masks("ident", w), ALU.add), f"t0_{n}")
            uabank, ubbank = [2, 4, 7], [3, 5, 7]
            for m in LEVELS[1:]:
                for n in tiles_of(m):
                    w = TW[n]
                    o2 = 64 if n == 2 else 0
                    rp.wait(dve, f"u{m}_{n}", it)
                    if m != top(n):
                        tt(sq_blocks(tm, n), sq_blocks(tm, n),
                           ps[0:w, uabank[n], 0:4 * w].rearrange("p (a b) -> p a b", a=4), ALU.add)
                    rd.reach(tt(sq_blocks(tmt, n), sq_blocks(tmt, n),
                                ps[0:w, ubbank[n], o2:o2 + 4 * w].rearrange("p (a b) -> p a b", a=4),
                                ALU.add), f"t{m}_{n}")
            for n in range(3):
                w = TW[n]
                rp.wait(dve, f"akv_{n}", it)
                rd.reach(cpv(rhs_[0:w, n, :, 64:P], ps[0:w, n, 0:256].rearrange("p (a b) -> p a b", a=4)),
                         f"akv_{n}")
            for n in range(2):
                rp.wait(dve, f"pg_{n}", it)
                rd.reach(tt(pbuf[0:64, 4 * n:4 * n + 4], dg[0:64, 4 * n:4 * n + 4],
                            ps[0:64, 4 * n:4 * n + 4, 0:256].rearrange("p c (e j) -> p c e j", e=4), ALU.add),
                         f"p_{n}")
            ra.wait(dve, "g_0", it)
            rd.reach(cpv(states[0:64, 1], gbuf[0:64, 0]), "s1")
            for c in range(2, 9):
                rp.wait(dve, f"s{c}", it)
                if c == 5:
                    ra.wait(dve, "g_1", it)
                rd.reach(tt(states[0:64, c], gbuf[0:64, c - 1],
                            ps[0:64, 0, 0:256].rearrange("p (e j) -> p e j", e=4), ALU.add), f"s{c}")
            for n in range(3):
                w = TW[n]
                rp.wait(dve, f"yo_{n}", it)
                take_wait(dve)
                rd.reach(cpv(r_y[:, two_, n * P:n * P + w],
                             ps[:, 5 + n, 0:2 * w].rearrange("p (q t) -> p q t", q=2)), f"yo_{n}")

        def ecs_wide():
            return ecs[0:64].rearrange("p e c -> p c e").unsqueeze(3).to_broadcast([64, 8, 4, 64])

        def stick_vector(dve, link, it, v, tt, stt, ts, cpv):
            two_ = bass.ds(it * 2, 2)
            take_wait(dve)
            sd.reach(cpv(vs2[:, :, 0:L], vT[:, two_, :]), "v")
            sd.reach(cpv(qst, qT[:, two_, :]), "q")
            sp_.wait(dve, "v", it)
            sd.reach(cpv(vk2.rearrange("p n q j -> p n (q j)"), ps[:, 4:7, 0:256]), "vk")
            sa.wait(dve, "abs", it)
            z = ps[:, 0:4, 0:ZW]
            diag = [(ZC[i], min(P, L - i * P)) for i in range(3)]
            rest = [(P, L), (L + P, L + P + META)]
            for a, w in diag:
                stt(out=zs[:, :, a:a + w], in0=z[:, :, a:a + w], scalar=0.125,
                    in1=over(const("strict_neg")[:, 0:w], 4), op0=ALU.mult, op1=ALU.add)
            for a, b in rest:
                ts(zs[:, :, a:b], z[:, :, a:b], 0.125, None, ALU.mult)
            link(ts(ll, z, 0.125, 0.0, ALU.mult, ALU.max))
            sa.wait(dve, "ln", it)
            link(stt(out=ll, in0=ll, scalar=-1.0, in1=ee, op0=ALU.mult, op1=ALU.subtract))
            for a, w in diag:
                last = tt(ll[:, :, a:a + w], ll[:, :, a:a + w], over(const("strict")[:, 0:w], 4), ALU.mult)
            sd.reach(last, "l")
            sp_.wait(dve, "sfx", it)
            sd.reach(tt(zs, zs, ps[:, 4:8, 0:ZW], ALU.add), "arg")
            sp_.wait(dve, "o", it)
            take_wait(dve)
            sd.reach(cpv(oT[:, two_, :], ps[:, 0:2, 0:L]), "o")

        def second_gpsimd(pool, link, g):
            with pool.Fori(0, 4) as it:
                rd.wait(pool, "cum", it)
                rl.reach(g.tensor_copy(vst, vv[:, bass.ds(it * 2, 2), :]), "v")
                for li, m in enumerate(LEVELS[1:]):
                    for n in tiles_of(m):
                        w = TW[n]
                        if li == 0:
                            ra.wait(pool, f"ab{n}", it)
                        rl.reach(g.tensor_tensor(sq_blocks(levs[li], n), sq_blocks(ab, n),
                                                 const(f"level{m}", w)[:, 0:w].unsqueeze(1).to_broadcast(
                                                     [w, 4, w]), ALU.mult), f"x{m}_{n}")
        block = ctx.enter_context(nc.Block())

        @block.sync
        def _(sp):
            sp.dma_start(consts[:], consts_d).then_inc(ld_c, 16)
            sp.dma_start(cols[:], cols_d).then_inc(ld_c, 16)
            sp.dma_start(xr, x_t).then_inc(ld_x, 16)
            for b in range(RING):
                sp.dma_start(ring[:, b, :], stream[b]).then_inc(landed[b], 16)
            turns = (N_BLOCKS - RING) // RING
            with sp.Fori(0, turns) as i:
                for s in range(RING):
                    sp.wait_ge(used, i * RING + (s + 1))
                    sp.dma_start(ring[:, s, :], stream[bass.ds(i * RING + (RING + s), 1)].rearrange(
                        "o p c -> p (o c)")).then_inc(landed[s], 16)
            for b in range(RING + turns * RING, N_BLOCKS):
                sp.wait_ge(used, b - RING + 1)
                sp.dma_start(ring[:, b % RING, :], stream[b]).then_inc(landed[b % RING], 16)
            second_sync(sp)

        @block.tensor
        def _(pe):
            def mm(out, lhs, rhs, start=True, stop=True):
                return nc.tensor.matmul(out, lhs, rhs, start=start, stop=stop)

            def tiles(name, b0, n, rhs, t, j0=0, ev_sem=None):
                e = ev_sem or ev[name]

                def body(s, it=None):
                    b, j = b0 + s, j0 + s
                    arrived(pe, b, it)
                    pe.wait_ge(e, j + 1 if it is None else it * RING + (j + 1))
                    for k in range(KT):
                        last = mm(ps[:, j % GB, 0:t], ring[:, b % RING, k * P:(k + 1) * P], rhs[:, k, :],
                                  k == 0, k == KT - 1)
                    last.then_inc(used, 1)
                turns = n // RING if n >= 2 * RING else 0
                if turns:
                    with pe.Fori(0, turns) as it:
                        for s in range(RING):
                            body(s, it)
                for s in range(turns * RING, n):
                    body(s)

            def total(bank, src, n, t, which, matrix="mean"):
                for k in range(n):
                    last = mm(ps[:, bank, 0:t], const(matrix), src[:, k, :], k == 0, k == n - 1)
                last.then_inc(summed, 1)

            pe.wait_ge(ld_c, 32)
            pe.wait_ge(sqd, 1)
            total(4, sq, KT, S, "mem")
            pe.wait_ge(sqd, 2)
            total(5, merged, KT, S, "in")
            pe.wait_ge(normed, 1)
            pe.sem_inc(ev["qkvs"], GB)
            tiles("qkvs", FIRST["in"], 18, h, S)
            pe.wait_ge(ev["qkvs"], GB + N_QKV)
            pe.wait_ge(summed, 2)
            pe.wait_ge(rooted, 2)
            for kv in range(2):
                r = slice(64 * kv, 64 * kv + 64)
                for t in range(4):
                    last = mm(ps[:, 4 + 2 * kv + t // 2, (t % 2) * 256:(t % 2) * 256 + 256],
                              qkv[r, t, P:S], qkv[r, 4, :])
            last.then_inc(at_s, 1)
            pe.wait_ge(ev["qkvs"], GB + 18)
            pe.sem_inc(ev["gate"], GB)
            tiles("gate", FIRST["in"] + 18, 8, h, S)
            pe.wait_ge(at_m, 1)
            for kv in range(2):
                r = slice(64 * kv, 64 * kv + 64)
                for t in range(4):
                    last = mm(ps[:, 4 + kv, t * P:(t + 1) * P], qkv[r, t, 0:P], qkv[r, 4, 0:P])
            last.then_inc(at_s, 1)
            pe.wait_ge(sqd, 3)
            total(6, tmp, 4, S, "sgu")
            for c in range(2):
                last = nc.tensor.transpose(ps[:, 7, c * P:(c + 1) * P], qkv[:, 5, c * P:(c + 1) * P], ident)
            last.then_inc(at_t, 1)
            tiles("gate", FIRST["in"] + 26, 16, h, S, j0=8)
            pe.wait_ge(at_n, 1)
            pe.wait_ge(at_m, 2)
            pe.wait_ge(rooted, 3)
            pe.wait_ge(at_tc, 1)
            for c in range(2):
                for e in range(8):
                    last = nc.tensor.transpose(ps[:, 4 + 2 * c + e // 4, (e % 4) * P:(e % 4 + 1) * P],
                                               sc1[:, e, c * P:(c + 1) * P], ident)
            last.then_inc(at_t, 1)
            pe.wait_ge(ev["gate"], GB + 24)
            pe.wait_ge(sg_n, 1)
            for c in range(2):
                for g in range(4):
                    last = nc.tensor.transpose(ps[:, c, g * P:(g + 1) * P], sv[:, g, c * P:(c + 1) * P], ident)
            last.then_inc(sg_t, 1)
            pe.wait_ge(pl_w, 1)
            pe.wait_ge(ld_s, 16 * 5)
            for g in range(4):
                last = mm(ps[:, 2 + g // 2, (g % 2) * S:(g % 2 + 1) * S], wpl[:, g, :], pcp[:, g, META:L])
            last.then_inc(pl_o, 1)
            pe.wait_ge(at_tc, 2)
            pe.wait_ge(at_n, 2)
            for e in range(8):
                last = nc.tensor.transpose(ps[:, 4 + e // 4, (e % 4) * P:(e % 4 + 1) * P], sc0[:, e, :], ident)
            last.then_inc(at_t, 1)
            pe.wait_ge(sg_tc, 1)
            pe.wait_ge(init_done, 1)
            for c in range(2):
                for g in range(4):
                    o = ps[:, 6 + c, g * P:(g + 1) * P]
                    mm(o, svt[:, c, g * P:(g + 1) * P], wst[:, g, :], True, False)
                    last = mm(o, const("ones", 1), bsp[0:1, g * P:(g + 1) * P], False, True)
            last.then_inc(sg_o, 1)
            pe.wait_ge(at_tc, 3)
            for kv in range(2):
                o = ps[64 * kv:64 * kv + 64, 0, :]
                vs = slice(64 * kv, 64 * kv + 64)
                mm(o, vtok[:, 0, vs], pt0[:, 4 * kv:4 * kv + 4, :])
                o = ps[64 * kv:64 * kv + 64, 1, :]
                mm(o, vtok[:, 0, vs], pt1[:, 0, 4 * kv:4 * kv + 4, :], True, False)
                last = mm(o, vtok[:, 1, vs], pt1[:, 1, 4 * kv:4 * kv + 4, :], False, True)
            last.then_inc(at_o, 1)
            pe.wait_ge(at_y, 1)
            pe.wait_ge(sg_y, 1)
            pe.wait_ge(pl_y, 1)
            pe.sem_inc(ev["branch"], GB)
            for u in range(24):
                b = FIRST["branch"] + u // 2
                if u % 2 == 0:
                    arrived(pe, b)
                pe.wait_ge(ev["branch"], u + 1)
                src = (ya, yb, yc)[u % 3]
                for k in range(4):
                    kk = (u % 2) * 4 + k
                    last = mm(ps[:, u % GB, 0:S], ring[:, b % RING, kk * P:(kk + 1) * P], src[:, k, :],
                              k == 0, k == 3)
                last.then_inc(used if u % 2 else halves, 1)
            pe.wait_ge(ev["branch"], GB + 24)
            pe.wait_ge(merged_done, 1)
            pe.sem_inc(ev["out"], GB)
            tiles("out", FIRST["out"], 8, merged, S)
            pe.wait_ge(sqd, 4)
            pe.wait_ge(sg_y, 1)
            total(6, sq, KT, S, "out")
            pe.wait_ge(ev["out"], GB + 8)
            pe.sem_inc(ev["mem_k"], GB)
            tiles("mem_k", FIRST["mem_kv"], 4, memn, S)
            pe.wait_ge(sqd, 5)
            total(7, sq, KT, S, "hm")
            pe.wait_ge(ev["mem_k"], GB + 4)
            for j in range(4):
                b = FIRST["mem_kv"] + 4 + j
                arrived(pe, b)
                for c in range(2):
                    for k in range(KT):
                        last = mm(ps[:, c, j * P:(j + 1) * P], memn[:, k, c * P:(c + 1) * P],
                                  ring[:, b % RING, k * P:(k + 1) * P], k == 0, k == KT - 1)
                last.then_inc(used, 1)
            pe.wait_ge(ev["mem_v"], 1)
            pe.wait_ge(normed, 2)
            pe.sem_inc(ev["mem_q"], GB)
            tiles("mem_q", FIRST["mem_q"], 4, h, S)
            pe.wait_ge(ev["mem_q"], GB + 4)
            for c in range(2):
                for e in range(4):
                    last = mm(ps[:, 4 + 2 * c + e // 2, (e % 2) * 256:(e % 2) * 256 + 256],
                              qm[:, e, c * P:(c + 1) * P], memk[:, e, :])
            last.then_inc(mm_s, 1)
            pe.wait_ge(mm_n, 1)
            for c in range(2):
                for m in range(2):
                    for e in range(4):
                        last = nc.tensor.transpose(ps[:, 2 * m + c, e * P:(e + 1) * P],
                                                   msc[:, 4 * c + e, m * P:(m + 1) * P], ident)
            last.then_inc(mm_t, 1)
            pe.wait_ge(mm_tc, 4)
            for c in range(2):
                for e in range(4):
                    o = ps[:, 4 + c, e * P:(e + 1) * P]
                    for m in range(2):
                        last = mm(o, memv[:, m, e * P:(e + 1) * P], mpt[:, m, 4 * c + e, :], m == 0, m == 1)
            last.then_inc(mm_o, 1)
            pe.wait_ge(mm_y, 2)
            pe.sem_inc(ev["mem_o"], GB)
            for j in range(8):
                b = FIRST["mem_o"] + j // 2
                if j % 2 == 0:
                    arrived(pe, b)
                pe.wait_ge(ev["mem_o"], j + 1)
                for k in range(4):
                    kk = (j % 2) * 4 + k
                    last = mm(ps[:, j % GB, 0:S], ring[:, b % RING, kk * P:(kk + 1) * P], om[:, k, :],
                              k == 0, k == 3)
                last.then_inc(used if j % 2 else halves, 1)
            pe.wait_ge(sqd, 6)
            total(6, sq, KT, S, "ym")
            pe.wait_ge(sqd, 7)
            total(7, sq, KT, S, "hf")
            pe.wait_ge(ev["mem_o"], GB + 8)
            pe.wait_ge(normed, 3)
            pe.sem_inc(ev["up"], GB)
            tiles("up", FIRST["up"], FF, h, S)
            pe.wait_ge(ev["up"], GB + FF)
            pe.wait_ge(up_sq, GB + FF)
            pe.sem_inc(ev["down"], GB)
            with pe.Fori(0, KT // 2) as it:
                for j in range(2):
                    pe.wait_ge(ev["down"], it * 2 + (j + 1 + GB - 2))
                    for q in range(4):
                        b = FIRST["down"] + 4 * j + q
                        arrived(pe, b, it)
                        for k in range(8):
                            last = mm(ps[:, j, 0:S], ring[:, b % RING, k * P:(k + 1) * P],
                                      act_up[:, 8 * q + k, :], q == 0 and k == 0, q == 3 and k == 7)
                        last.then_inc(used, 1)
            pe.wait_ge(sqd, 8)
            total(6, sq, KT, S, "yf")
            second_tensor(pe, mm, tiles, total)

        @block.scalar
        def _(act):
            link = Chain(act, act_chain)
            f = nc.scalar.activation

            def root(bank, t, scale=1.0, which=0):
                act.wait_ge(summed, which)
                f(rs[:, 0:t], ps[:, bank, 0:t], ACT.Sqrt, bias=eps_c, scale=scale).then_inc(rooted, 1)

            for dst, src in ((sink_sb, sinks_d), (wst, ws_t), (wpl, w_pool), (bsp[0:1, :], b_sp),
                             (res[:, :, 0:META], meta_t)):
                act.dma_start(dst, src).then_inc(ld_s, 16)
            act.dma_start(h, mem_t).then_inc(ld_m, 16)
            act.wait_ge(ld_m, 16)
            f(sq, h, ACT.Square).then_inc(sqd, 1)
            act.wait_ge(ld_x, 16)
            f(merged, xr, ACT.Square).then_inc(sqd, 1)
            act.wait_ge(init_done, 1)
            root(4, S, which=1)
            act.wait_ge(normed0, 1)
            root(5, S, which=2)
            b = FIRST["in"]
            for j in range(18):
                act.wait_ge(used, b + j + 1)
                src = ps[:, j % GB, 0:S]
                if j < 6:
                    f(qkv[:, j, :], src, ACT.Copy).then_inc(ev["qkvs"], 1)
                elif j < 14:
                    f((su if j < 10 else sv)[:, (j - 6) % 4, :], src, ACT.Gelu_apprx_tanh).then_inc(ev["qkvs"], 1)
                else:
                    f(pcp[:, j - 14, META:L], src, ACT.Copy).then_inc(ev["qkvs"], 1)
            for j in range(8):
                act.wait_ge(used, b + 18 + j + 1)
                f(gates[:, j, :], ps[:, j % GB, 0:S], ACT.Sigmoid).then_inc(ev["gate"], 1)
            act.wait_ge(at_m, 1)
            for e in range(8):
                link(f(sc1[:, e, :], sc1[:, e, :], ACT.Exp, bias=small[:, 16 + e:17 + e],
                       accum_out=small[:, 24 + e:25 + e]))
            f(small[:, 32:40], small[:, 32:40], ACT.Exp).then_inc(at_p, 1)
            act.wait_ge(at_m, 2)
            for e in range(8):
                link(f(sc0[:, e, :], sc0[:, e, :], ACT.Exp, bias=small[:, 40 + e:41 + e],
                       accum_out=small[:, 48 + e:49 + e]))
            f(small[:, 56:64], small[:, 56:64], ACT.Exp).then_inc(at_p, 1)
            root(6, S, scale=2.0, which=3)
            with act.Fori(0, 2) as it:
                for s in range(8):
                    act.wait_ge(used, it * 8 + (b + 26 + s + 1))
                    f(gates[:, bass.ds(it * 8 + (8 + s), 1), :], ps[:, s % GB, 0:S],
                      ACT.Sigmoid).then_inc(ev["gate"], 1)
            act.wait_ge(at_t, 2)
            for c in range(2):
                for q in range(2):
                    last = nc.scalar.copy(pt1[:, c, 4 * q:4 * q + 4, :], ps[:, 4 + 2 * c + q, :])
            last.then_inc(at_tc, 1)
            act.wait_ge(pl_o, 1)
            for g in range(4):
                last = f(yc[:, g, :], ps[:, 2 + g // 2, (g % 2) * S:(g % 2 + 1) * S], ACT.Copy,
                         scale=col("pool_scale", g))
            last.then_inc(pl_y, 1)
            act.wait_ge(at_t, 3)
            for q in range(2):
                last = nc.scalar.copy(pt0[:, 4 * q:4 * q + 4, :], ps[:, 4 + q, :])
            last.then_inc(at_tc, 1)

            def squares_of_y(name, n, t, g, sc, sqv=None, ybuf=None, n0=0):
                for j in range(n):
                    act.wait_ge(ev[name], GB + j + 1)
                    ins = f(sq2(sqv)[:, j, :], sq2(ybuf, 1)[:, j, :], ACT.Square)
                    if j < n - 1:
                        link(ins)
                    else:
                        ins.then_inc(sqd, 1)
                        act.wait_ge(sqd, sc)
                for j in range(n):
                    last = f(sq2(ybuf, 1)[:, j, :], sq2(ybuf, 1)[:, j, :], ACT.Copy, scale=col(g[0], g[1] + j))
                last.then_inc(yg_done, 1)

            def sq2(x, d=0):
                return x if x is not None else (y1 if d else sq)

            squares_of_y("out", 8, S, ("g_norm", 8), 4)
            root(6, S, which=4)
            act.wait_ge(res_up, 1)
            f(sq, xr, ACT.Square).then_inc(sqd, 1)
            b = FIRST["mem_kv"]
            for j in range(4):
                act.wait_ge(used, b + j + 1)
                f(memk[:, j, :], ps[:, j % GB, 0:S], ACT.Copy).then_inc(ev["mem_k"], 1)
            root(7, S, which=5)
            act.wait_ge(mm_m, 1)
            for e in range(8):
                ins = f(msc[:, e, :], ps[:, 4 + e // 2, (e % 2) * 256:(e % 2) * 256 + 256], ACT.Exp,
                        bias=small[:, 16 + e:17 + e], scale=128 ** -0.5, accum_out=small[:, 24 + e:25 + e])
                ins.then_inc(mm_p, 1)
            act.wait_ge(mm_t, 1)
            for c in range(2):
                nc.scalar.copy(mpt[:, c, 0:4, :], ps[:, 2 * c, :]).then_inc(mm_tc, 1)
            act.wait_ge(mm_o, 1)
            nc.scalar.copy(om[:, :, 0:P], ps[:, 4, :].rearrange("p (a b) -> p a b", a=4)).then_inc(mm_y, 1)
            squares_of_y("mem_o", 8, S, ("g_norm", 24), 6)
            root(6, S, which=6)
            act.wait_ge(res_up, 2)
            f(sq, xr, ACT.Square).then_inc(sqd, 1)
            root(7, S, which=7)
            b = FIRST["up"]
            with act.Fori(0, FF // 8) as it:
                for s in range(8):
                    act.wait_ge(used, it * 8 + (b + s + 1))
                    act.wait_ge(up_sq, it * 8 + (s + 1))
                    f(tmp[:, s % 4, :], ps[:, s % GB, 0:S], ACT.Relu).then_inc(ev["up"], 1)
            squares_of_y("down", 8, S, ("g_norm", 40), 8)
            root(6, S, which=8)
            second_scalar(act, link, f, root, squares_of_y)

        @block.vector
        def _(dve):
            link = Chain(dve, dve_chain)
            v = nc.vector
            tt, stt, ts = v.tensor_tensor, v.scalar_tensor_tensor, v.tensor_scalar

            def inverse_root(which, t):
                dve.wait_ge(rooted, which)
                link(v.reciprocal(rs[:, 0:t], rs[:, 0:t]))

            def residual(which, t, x, yv, up=None):
                dve.wait_ge(yg_done, up)
                inverse_root(which, t)
                link(tt(yv, yv, over(rs[:, 0:t], KT), ALU.mult))
                tt(x, x, yv, ALU.add).then_inc(res_up, 1)
                dve.wait_ge(res_up, up)

            def normed_to(dst, which, t, n):
                inverse_root(which, t)
                tt(dst, dst, over(rs[:, 0:t], dst.shape[1]), ALU.mult).then_inc(normed, 1)

            v.memset(small[:, 0:1], EPS)
            v.memset(small[:, 1:2], GN_EPS)
            v.memset(small[:, 2:3], 1.0)
            dve.wait_ge(ld_s, 16 * 5)
            v.memset(wst[64:P, :, 0:64], 0.0)
            link(v.memset(pcp[:, :, 0:META], 0.0))
            v.memset(win_a[:, :, 0:META], 0.0)
            v.memset(win_b[:, :, 0:META], 0.0).then_inc(init_done, 1)
            dve.wait_ge(ld_m, 16)
            dve.wait_ge(ld_c, 32)
            link(tt(memn, h, col_wide("g_mem", 0, KT, S), ALU.mult))
            dve.wait_ge(rooted, 1)
            link(v.reciprocal(rs[:, 0:S], rs[:, 0:S]))
            tt(memn, memn, over(rs[:, 0:S], KT), ALU.mult).then_inc(normed0, 1)
            dve.wait_ge(normed0, 1)
            dve.wait_ge(ld_x, 16)
            dve.wait_ge(sqd, 2)
            link(tt(h, xr, col_wide("g_norm", 0, KT, S), ALU.mult))
            normed_to(h, 2, S, 1)
            for r in range(2):
                nk, sc, mask = (2 * P, sc1, "att1") if r == 0 else (P, sc0, "att0")
                m = small[:, 16 + 24 * r:24 + 24 * r]
                ex = small[:, 32 + 24 * r:40 + 24 * r]
                dve.wait_ge(at_s, r + 1)
                per = 512 // nk
                for q in range(8 // per):
                    ins = stt(out=sc[:, per * q:per * q + per, :],
                              in0=ps[:, 4 + q, :].rearrange("p (a b) -> p a b", a=per), scalar=0.125,
                              in1=over(const(mask), per), op0=ALU.mult, op1=ALU.add)
                    link(ins)
                link(v.tensor_reduce(m, sc, AX_X, ALU.max))
                link(tt(m, m, sink_sb, ALU.max))
                link(tt(ex, sink_sb, m, ALU.subtract))
                ts(m, m, -1.0, None, ALU.mult).then_inc(at_m, 1)
                if r == 0:
                    dve.wait_ge(ev["qkvs"], GB + 14)
                    tt(tmp, sv, sv, ALU.mult).then_inc(sqd, 1)
                    link(tt(sv, sv, col_wide("g_sgu", 0, 4, S), ALU.mult))
            dve.wait_ge(at_t, 1)
            v.tensor_copy(vtok, ps[:, 7, 0:S].rearrange("p (a b) -> p a b", a=2)).then_inc(at_tc, 1)
            for r in range(2):
                nk, sc = (2 * P, sc1) if r == 0 else (P, sc0)
                tot = small[:, 24 + 24 * r:32 + 24 * r]
                ex = small[:, 32 + 24 * r:40 + 24 * r]
                dve.wait_ge(at_p, r + 1)
                link(tt(tot, tot, ex, ALU.add))
                link(v.reciprocal(tot, tot))
                tt(sc, sc, tot.unsqueeze(2).to_broadcast([P, 8, nk]), ALU.mult).then_inc(at_n, 1)
            dve.wait_ge(rooted, 3)
            link(v.reciprocal(rs[:, 0:S], rs[:, 0:S]))
            tt(sv, sv, over(rs[:, 0:S], 4), ALU.mult).then_inc(sg_n, 1)
            dve.wait_ge(sg_t, 1)
            v.tensor_copy(svt[:, 0, :], ps[:, 0, :])
            v.tensor_copy(svt[:, 1, :], ps[:, 1, :]).then_inc(sg_tc, 1)
            dve.wait_ge(sg_o, 1)
            for c in range(2):
                last = tt(yb[:, :, c * P:(c + 1) * P], su[:, :, c * P:(c + 1) * P],
                          ps[:, 6 + c, :].rearrange("p (a b) -> p a b", a=4), ALU.mult)
            last.then_inc(sg_y, 1)
            dve.wait_ge(at_o, 1)
            for c in range(2):
                last = v.tensor_copy(ya[:, :, c * P:(c + 1) * P],
                                     ps[:, c, :].rearrange("p (a b) -> p a b", a=4))
            last.then_inc(at_y, 1)
            for u in range(24):
                n, br = u // 3, u % 3
                if u % 2:
                    dve.wait_ge(used, FIRST["branch"] + u // 2 + 1)
                else:
                    dve.wait_ge(halves, u // 2 + 1)
                src, g = ps[:, u % GB, 0:S], gates[:, 8 * br + n, :]
                if br == 0:
                    tt(merged[:, n, :], g, src, ALU.mult).then_inc(ev["branch"], 1)
                else:
                    tt(tmp[:, br, :], g, src, ALU.mult).then_inc(ev["branch"], 1)
                    dve.wait_ge(ev["branch"], GB + u + 1)
                    ins = tt(merged[:, n, :], merged[:, n, :], tmp[:, br, :], ALU.add)
                    if u < 23:
                        link(ins)
                    else:
                        ins.then_inc(merged_done, 1)

            def take(name, b, n, dst, t, per=1):
                for j in range(n):
                    dve.wait_ge(used, b + per * (j + 1))
                    v.tensor_copy(dst[:, j, :], ps[:, j % GB, 0:t]).then_inc(ev[name], 1)

            take("out", FIRST["out"], 8, y1, S)
            residual(4, S, xr, y1, 1)
            link(tt(h, xr, col_wide("g_norm", 16, KT, S), ALU.mult))
            dve.wait_ge(used, FIRST["mem_kv"] + 8)
            normed_to(h, 5, S, 3)
            for c in range(2):
                ins = v.tensor_copy(memv[:, c, :], ps[:, c, :])
                if c == 0:
                    link(ins)
                else:
                    ins.then_inc(ev["mem_v"], 1)
            take("mem_q", FIRST["mem_q"], 4, qm, S)
            dve.wait_ge(mm_s, 1)
            for q in range(4):
                link(v.tensor_reduce(small[:, 16 + 2 * q:18 + 2 * q],
                                     ps[:, 4 + q, :].rearrange("p (a b) -> p a b", a=2), AX_X, ALU.max))
            ts(small[:, 16:24], small[:, 16:24], -(128 ** -0.5), None, ALU.mult).then_inc(mm_m, 1)
            dve.wait_ge(mm_p, 8)
            link(v.reciprocal(small[:, 24:32], small[:, 24:32]))
            tt(msc, msc, small[:, 24:32].unsqueeze(2).to_broadcast([P, 8, 2 * P]), ALU.mult).then_inc(mm_n, 1)
            dve.wait_ge(mm_t, 1)
            for c in range(2):
                v.tensor_copy(mpt[:, c, 4:8, :], ps[:, 2 * c + 1, :]).then_inc(mm_tc, 1)
            dve.wait_ge(mm_o, 1)
            v.tensor_copy(om[:, :, P:S], ps[:, 5, :].rearrange("p (a b) -> p a b", a=4)).then_inc(mm_y, 1)
            for j in range(8):
                if j % 2:
                    dve.wait_ge(used, FIRST["mem_o"] + j // 2 + 1)
                else:
                    dve.wait_ge(halves, 12 + j // 2 + 1)
                v.tensor_copy(y1[:, j, :], ps[:, j % GB, 0:S]).then_inc(ev["mem_o"], 1)
            residual(6, S, xr, y1, 2)
            link(tt(h, xr, col_wide("g_norm", 32, KT, S), ALU.mult))
            normed_to(h, 7, S, 4)
            dve.sem_inc(up_sq, 4)
            with dve.Fori(0, FF // 8) as it:
                for s in range(8):
                    dve.wait_ge(ev["up"], it * 8 + (GB + s + 1))
                    tt(act_up[:, bass.ds(it * 8 + s, 1), :], tmp[:, s % 4, :], tmp[:, s % 4, :],
                       ALU.mult).then_inc(up_sq, 1)
            b = FIRST["down"]
            with dve.Fori(0, KT // 2) as it:
                for j in range(2):
                    dve.wait_ge(used, it * 8 + (b + 4 * (j + 1)))
                    dve.sem_inc(passed, 1)
                    v.tensor_copy(y1[:, bass.ds(it * 2 + j, 1), :], ps[:, j, 0:S]).then_inc(ev["down"], 1)
            residual(8, S, xr, y1, 3)
            second_vector(dve, link, v, tt, stt, ts, inverse_root, residual, normed_to, take)

        @block.gpsimd
        def _(pool):
            link = Chain(pool, pool_chain)
            g = nc.gpsimd
            pool.wait_ge(ev["qkvs"], GB + 18)
            pool.wait_ge(init_done, 1)
            link(g.tensor_tensor(win_a[:, 0:4, META:L], pcp[:, 0:4, META:L], pcp[:, 0:4, META - 1:L - 1], ALU.add))
            link(g.tensor_tensor(win_b[:, 1:4, META:L], win_a[:, 1:4, META:L], win_a[:, 1:4, META - 2:L - 2], ALU.add))
            link(g.tensor_tensor(win_a[:, 2:4, META:L], win_b[:, 2:4, META:L], win_b[:, 2:4, META - 4:L - 4], ALU.add))
            link(g.tensor_tensor(win_b[:, 3:4, META:L], win_a[:, 3:4, META:L], win_a[:, 3:4, META - 8:L - 8], ALU.add))
            inv = const("inv_cnt").rearrange("p (a b) -> p a b", a=4)
            for k in range(4):
                src = (win_a, win_b)[k % 2]
                link(g.tensor_tensor(src[:, k, META:META + 16], src[:, k, META:META + 16], inv[:, k, :], ALU.mult))
                link(g.tensor_scalar(src[:, k, META + 16:L], src[:, k, META + 16:L], 0.5 ** (k + 1), None, ALU.mult))
                ins = g.tensor_tensor(pcp[:, k, META:L], src[:, k, META:L], pcp[:, k, META:L], ALU.subtract)
                if k < 3:
                    link(ins)
                else:
                    ins.then_inc(pl_w, 1)
            second_gpsimd(pool, link, g)


def blocks_of(w):
    k, n = w.shape
    kt = k // P
    b = w.reshape(kt, P, n // P, P).transpose(2, 1, 0, 3)
    return b.reshape(n // P, P, kt * P)


def deep_blocks(w, per):
    b = blocks_of(w)
    n = b.shape[0]
    out = np.zeros((n, P, per * BLK), w.dtype)
    out[:, :, :b.shape[2]] = b
    return out.reshape(n, P, per, BLK).transpose(0, 2, 1, 3).reshape(n * per, P, BLK)


def feature_tiles(x):
    return np.ascontiguousarray(x.T.reshape(-1, P, x.shape[0]).transpose(1, 0, 2))


def columns(*vectors):
    return [np.asarray(v).reshape(-1, P).T for v in vectors]


def kernel(**a):
    import concourse.bacc as bacc
    from concourse.bass_utils import run_bass_kernel_spmd

    a = {k: np.asarray(v) for k, v in a.items()}
    f = np.float32
    w_in = a["w_in"][0]
    heads = np.arange(512).reshape(2, 4, 64).transpose(1, 0, 2).reshape(-1)
    w_in = np.concatenate([w_in[:, :512][:, heads], w_in[:, 512:]], axis=1)
    br = a["w_branch"][0].copy()
    br[0] = br[0][heads]
    br = br.reshape(3, 4, P, 8, P).transpose(3, 0, 2, 1, 4).reshape(12, 2, P, 4 * P)
    mem_o = a["w_o_mem"][0].reshape(4, P, 8, P).transpose(2, 1, 0, 3).reshape(4, 2, P, 4 * P)
    pair = lambda w: w.reshape(w.shape[0], 2, P, 4 * P).transpose(0, 2, 1, 3).reshape(w.shape[0], P, BLK)
    both = lambda w: w.reshape(*w.shape[:-1], 2, F2, P).swapaxes(-3, -2).reshape(w.shape)
    up2 = both(a["ffn_up_2"])
    parts = {
        "in": blocks_of(w_in), "branch": pair(br), "out": blocks_of(a["w_out"][0]),
        "mem_kv": blocks_of(a["w_kv_mem"][0]), "mem_q": blocks_of(a["w_q_mem"][0]), "mem_o": pair(mem_o),
        "up": blocks_of(a["w_up"][0]), "down": deep_blocks(a["w_down"][0], 4),
        "rw_r": blocks_of(a["rw_wr_2"][0]), "rw_k": blocks_of(a["rw_wk_2"][0]),
        "rw_v": blocks_of(a["rw_wv_2"][0]), "rw_o": blocks_of(a["rw_wo_2"][0]),
        "ffa_up": blocks_of(up2[0]), "ffa_down": deep_blocks(a["ffn_down_2"][0], F2B),
        "sb_k": blocks_of(a["sb_wk_2"]), "sb_v": blocks_of(a["sb_wv_2"]),
        "sb_q": blocks_of(a["sb_wq_2"][0]), "sb_o": blocks_of(a["sb_wo_2"][0]),
        "ffb_up": blocks_of(up2[1]), "ffb_down": deep_blocks(a["ffn_down_2"][1], F2B),
    }
    stream = np.concatenate([parts[name] for name, _ in STREAM])
    cw, cb = both(a["ffn_conv_w_2"]), both(a["ffn_conv_b_2"])
    cols = np.concatenate(columns(
        a["g_norm"], a["g_mem"], a["g_sgu"], a["pool_scale"], a["norm_mix_g_2"], a["norm_ffn_g_2"],
        a["rw_mix_2"], a["rw_w0_2"], a["rw_a0_2"], a["rw_kk_2"], a["rw_ka_2"], a["rw_rk_2"],
        a["rw_lnx_g_2"], a["rw_lnx_b_2"], a["kv_norm_g_2"], a["final_norm_g_2"], cw, cb), axis=1)
    g1 = a["rw_g1_2"][0]
    wide = lambda w: np.ascontiguousarray(w.reshape(KT, P, -1).transpose(1, 0, 2))
    ins = {
        "stream": stream, "x_t": feature_tiles(a["x"][0]), "mem_t": feature_tiles(a["mem"][0]),
        "meta_t": feature_tiles(a["meta_tokens_2"]), "cols": np.ascontiguousarray(cols),
        "consts": CONSTS, "sinks": np.tile(a["attn_sinks"], (P, 1)),
        "ws_t": np.ascontiguousarray(a["w_spatial"][0].transpose(2, 0, 1)),
        "b_sp": a["b_spatial"][0].reshape(1, 512),
        "w_pool": np.ascontiguousarray(a["w_pool"][0].transpose(1, 0, 2)),
        "w1": wide(a["rw_w1_2"][0]), "a1": wide(a["rw_a1_2"][0]), "g1": wide(g1),
        "w2": a["rw_w2_2"][0], "a2": a["rw_a2_2"][0], "g2": a["rw_g2_2"][0],
    }
    nc = bacc.Bacc("TRN2", target_bir_lowering=False, num_devices=1)
    args = [nc.dram_tensor("in_" + n, v.shape, mybir.dt.from_np(v.dtype), kind="ExternalInput").ap()
            for n, v in ins.items()]
    out = nc.dram_tensor("out_t", (P, KT, S), F32, kind="ExternalOutput").ap()
    program(nc, *args, out)
    r = run_bass_kernel_spmd(nc, [{"in_" + n: v for n, v in ins.items()}], core_ids=[0])
    got = np.asarray(r.results[0]["out_t"]).reshape(P, KT, S)
    return np.ascontiguousarray(got.transpose(2, 1, 0).reshape(1, S, D))
```

```python
from contextlib import ExitStack

import numpy as np

import concourse.bass as bass
from concourse import mybir

ALU = mybir.AluOpType
ACT = mybir.ActivationFunctionType
F32 = mybir.dt.float32
AX_X = mybir.AxisListType.X

P = 128
D = 1024
KT = D // P
S = 256
META = 16
L = S + META
RING = 8
BLK = 8 * P
EPS = 1e-6
GN_EPS = 64e-5
NEG = -1e30
GB = 4

N_QKV, N_SU, N_SV, N_PC, N_GATE = 6, 4, 4, 4, 24
N_IN = N_QKV + N_SU + N_SV + N_PC + N_GATE
FF = 4096 // P
F2 = 2816 // P
F2B = 3
STREAM = [("in", N_IN), ("branch", 12), ("out", 8), ("mem_kv", 8), ("mem_q", 4), ("mem_o", 4),
          ("up", FF), ("down", 4 * KT),
          ("rw_r", 8), ("rw_k", 8), ("rw_v", 8), ("rw_o", 8),
          ("ffa_up", 2 * F2), ("ffa_down", F2B * KT),
          ("sb_k", 8), ("sb_v", 8), ("sb_q", 8), ("sb_o", 8),
          ("ffb_up", 2 * F2), ("ffb_down", F2B * KT)]
FIRST = {}
_n = 0
for _name, _count in STREAM:
    FIRST[_name] = _n
    _n += _count
N_BLOCKS = _n

COLS = {}
_n = 0
for _name, _count in [("g_norm", 48), ("g_mem", 8), ("g_sgu", 4), ("pool_scale", 4), ("mix_g", 16),
                      ("ffn_g", 16), ("rw_mix", 48), ("w0", 8), ("a0", 8), ("k_k", 8), ("k_a", 8),
                      ("r_k", 8), ("lnx_g", 8), ("lnx_b", 8), ("kv_g", 8), ("fin_g", 8),
                      ("conv_w", 2 * 3 * 2 * F2), ("conv_b", 2 * 2 * F2)]:
    COLS[_name] = _n
    _n += _count
N_COLS = _n

CH = 32
LEVELS = (1, 2, 4, 8, 16)


def shape_constants():
    i = np.arange(P)
    r, c = i[:, None], i[None, :]
    same = r // CH == c // CH
    parts = {
        "ident": r == c,
        "mean": np.full((P, P), 1.0 / D),
        "ones": np.ones((P, P)),
        "after": r >= c,
        "strict": r < c,
        "att0": np.where((r < 64) & (c >= 64), NEG, 0.0),
        "chunk_strict": same & (r < c),
        "chunk_incl": same & (r <= c),
        "level1t": (r // 2 == c // 2) & (r > c),
        "scan": np.tile((np.arange(L) % CH != 0).astype(np.float32), (P, 1)),
    }
    c2 = np.arange(2 * P)[None, :]
    parts["att1"] = np.where(((r < 64) & (c2 >= 192)) | ((r >= 64) & (c2 < 64)), NEG, 0.0)
    for m in LEVELS:
        parts[f"level{m}"] = (r // (2 * m) == c // (2 * m)) & (r % (2 * m) < m) & (c % (2 * m) >= m)
    heads = (2 * np.arange(KT)[None, :, None] + r[:, :, None] // 64) == np.arange(16)[None, None, :]
    parts["to_head"] = heads.reshape(P, KT * 16)
    back = np.zeros((P, KT, P))
    back[:16] = heads.transpose(2, 1, 0)
    parts["from_head"] = back.reshape(P, KT * P)
    parts["strict_neg"] = np.where(r < c, 0.0, NEG)
    t = np.arange(16) + 1
    parts["inv_cnt"] = np.tile(np.concatenate([1.0 / np.minimum(t, w) for w in (2, 4, 8, 16)]), (P, 1))
    at, n = {}, 0
    for k, v in parts.items():
        at[k] = (n, n + v.shape[1])
        n += v.shape[1]
    return np.concatenate([np.asarray(v, np.float32) for v in parts.values()], axis=1), at


CONSTS, CONST_AT = shape_constants()


class Chain:

    def __init__(self, eng, sem):
        self.eng, self.sem, self.n, self.loop = eng, sem, 0, None

    def __call__(self, ins):
        ins.then_inc(self.sem, 1)
        self.n += 1
        self.eng.wait_ge(self.sem, self.n if self.loop is None else self.loop * self.per + self.n)

    def enter(self, index, per):
        self.loop, self.per, self.base = index, per, self.n

    def leave(self, times):
        assert self.n - self.base == self.per, (self.n - self.base, self.per)
        self.loop, self.n = None, self.base + self.per * times


class Marks:

    def __init__(self, sem, names):
        self.sem, self.names, self.next = sem, names.split(), 0

    def reach(self, ins, name):
        assert self.names[self.next % len(self.names)] == name, (self.names[self.next], name)
        self.next += 1
        ins.then_inc(self.sem, 1)

    def wait(self, eng, name, it=None):
        n = self.names.index(name) + 1
        eng.wait_ge(self.sem, n if it is None else it * len(self.names) + n)


class Space:

    def __init__(self, tensor, width):
        self.t, self.width, self.at = tensor, width, 0

    def take(self, *dims):
        n = int(np.prod(dims))
        a = self.t[:, self.at:self.at + n]
        self.at += n
        assert self.at <= self.width, (self.at, self.width)
        if len(dims) == 2:
            return a.rearrange("p (a b) -> p a b", a=dims[0])
        if len(dims) == 4:
            return a.rearrange("p (a b c d) -> p a b c d", a=dims[0], b=dims[1], c=dims[2])
        if len(dims) == 3:
            return a.rearrange("p (a b c) -> p a b c", a=dims[0], b=dims[1])
        return a


def program(nc, stream, x_t, mem_t, meta_t, cols_d, consts_d, sinks_d, ws_t, b_sp, w_pool,
            w1_d, a1_d, g1_d, w2_d, a2_d, g2_d, out_t):
    with ExitStack() as ctx:
        def sem(name):
            return ctx.enter_context(nc.semaphore(name))

        ring = ctx.enter_context(nc.sbuf_tensor("ring", [P, RING, BLK], F32))
        consts = ctx.enter_context(nc.sbuf_tensor("consts", [P, CONSTS.shape[1]], F32))
        cols = ctx.enter_context(nc.sbuf_tensor("cols", [P, N_COLS], F32))
        res = ctx.enter_context(nc.sbuf_tensor("res", [P, KT, L], F32))
        small = ctx.enter_context(nc.sbuf_tensor("small", [P, 64], F32))
        rs = ctx.enter_context(nc.sbuf_tensor("rs", [P, L], F32))
        width = (212863 // 4) - (RING * BLK + CONSTS.shape[1] + N_COLS + KT * L + 64 + L) - 16
        width -= width % 8
        arena = ctx.enter_context(nc.sbuf_tensor("arena", [P, width], F32))
        ps = ctx.enter_context(nc.psum_tensor("ps", [P, 8, 512], F32))

        def const(name, rows=P):
            a, b = CONST_AT[name]
            return consts[0:rows, a:b]

        def col(name, k, rows=P):
            return cols[0:rows, COLS[name] + k:COLS[name] + k + 1]

        def col_wide(name, k, n, t):
            a = COLS[name] + k
            return cols[:, a:a + n].unsqueeze(2).to_broadcast([P, n, t])

        def over(a, n):
            return a.unsqueeze(1).to_broadcast([P, n, a.shape[1]])

        ident = const("ident")
        xr = res[:, :, META:L]

        one = Space(arena, width)
        eps_c = small[:, 0:1]
        gn_eps_c = small[:, 1:2]
        one_c = small[:, 2:3]
        sink_sb = small[:, 8:16]
        h = one.take(KT, S)
        qkv = one.take(N_QKV, S)
        su, sv = one.take(4, S), one.take(4, S)
        pcp = one.take(4, L)
        gates = one.take(24, S)
        sc1, sc0 = one.take(8, 2 * P), one.take(8, P)
        pt1, pt0 = one.take(2, 8, P), one.take(8, P)
        act_up = arena[:, one.at - 24 * S - 16 * P - 8 * P - 16 * P - 8 * P:one.at][:, 0:FF * S].rearrange(
            "p (a b) -> p a b", a=FF)
        vtok = one.take(2, P)
        svt = one.take(2, 512)
        lora_at = one.at
        ya, yb, yc = one.take(4, S), one.take(4, S), one.take(4, S)
        merged = one.take(KT, S)
        memn = one.take(KT, S)
        sq_at = one.at
        sq = one.take(KT, S)
        y1 = arena[:, one.at:one.at + KT * S].rearrange("p (a b) -> p a b", a=KT)
        win_a, win_b = one.take(4, L), one.take(4, L)
        memk, memv = one.take(4, S), one.take(2, 512)
        qm = one.take(4, S)
        om = su
        wst, wpl = one.take(4, P), one.take(4, P)
        bsp = one.take(512)
        tmp = one.take(4, S)
        msc = sc1
        mpt = pt1

        ld_c, ld_x, ld_m, ld_s = sem("ld_consts"), sem("ld_x"), sem("ld_mem"), sem("ld_small")
        landed = [sem(f"landed{i}") for i in range(RING)]
        used = sem("blocks_used")
        act_chain, dve_chain, pool_chain = sem("act_chain"), sem("dve_chain"), sem("pool_chain")
        init_done = sem("init_done")
        ev = {}
        for name in ("qkvs", "gate", "branch", "out", "mem_k", "mem_v", "mem_q", "mem_o", "up", "down"):
            ev[name] = sem("ev_" + name)
        sqd, summed, rooted, normed = sem("squared"), sem("summed"), sem("rooted"), sem("normed")
        at_s, at_m, at_p, at_n = sem("at_scores"), sem("at_max"), sem("at_exp"), sem("at_norm")
        at_t, at_tc, at_o, at_y = sem("at_turned"), sem("at_turned_copied"), sem("at_out"), sem("ya_done")
        sg_n, sg_t, sg_tc, sg_o, sg_y = (sem("sgu_normed"), sem("sgu_turned"), sem("sgu_turned_copied"),
                                         sem("sgu_out"), sem("yb_done"))
        pl_w, pl_o, pl_y = sem("pooled"), sem("pool_out"), sem("yc_done")
        mm_s, mm_m, mm_p, mm_n, mm_t, mm_tc, mm_o, mm_y = [sem("mem_" + s) for s in (
            "scores", "max", "exp", "norm", "turned", "turned_copied", "out", "done")]
        yg_done, res_up = sem("y_scaled"), sem("res_updated")
        sq_part, norm_part = sem("squared_slices"), sem("normed_slices")
        halves, normed0, up_sq = sem("half_blocks_used"), sem("mem_normed"), sem("up_squared")
        merged_done = sem("merged_done")
        stored, passed = sem("stored"), sem("passed")

        NORM = {n: i + 1 for i, n in enumerate(
            ["mem", "in", "sgu", "out", "hm", "ym", "hf", "yf",
             "r1", "f1", "kv", "f2", "fin"])}

        def arrived(eng, b, it=None):
            v = 16 * (b // RING + 1)
            eng.wait_ge(landed[b % RING], v if it is None else it * 16 + v)

        two = Space(arena, width)
        r_y, k2, vv, lw, bb, gg, kkn = [two.take(KT, L) for _ in range(7)]
        s16a, s16b = two.take(L), two.take(L)
        loop_at = two.at
        hnp = two.take(KT, L + 1)
        tw, ta, tg0, tg1 = two.take(L), two.take(L), two.take(L), two.take(L)
        two.at = lora_at
        w1s, a1s, g1s = two.take(KT, 64), two.take(KT, 64), two.take(KT, 160)
        w2s, a2s = two.take(D), two.take(D)
        g2s, g2t = two.take(D), two.take(D)
        assert two.at <= sq_at
        xx = two.take(KT, L)
        xm = [two.take(KT, L) for _ in range(3)]
        two.at = loop_at
        TW = [P, P, META]
        AW = 4 * L

        def sq_blocks(buf, n):
            w = TW[n]
            return buf[0:w, 512 * n:512 * n + 4 * w].rearrange("p (a b) -> p a b", a=4)

        ar = two.take(2, 2, L)
        yy_at = two.at
        bt, kt_ = two.take(2, L), two.take(2, L)
        yy = arena[:, yy_at:yy_at + AW]
        cum, ep, en, epre = two.take(2, L), two.take(2, L), two.take(2, L), two.take(2, L)
        eh = two.take(2, S)
        wu_at = two.at
        bh, kh, vst = two.take(2, S), two.take(2, S), two.take(2, L)
        wu = arena[:, wu_at:wu_at + 12 * P].rearrange("p (n e j) -> p n e j", n=3, e=4)
        lev_at = two.at
        levs = [two.take(AW) for _ in LEVELS[1:]]
        bhx, khx = [arena[:, lev_at + 2048 * i:lev_at + 2048 * (i + 1)].rearrange(
            "p (n f c j) -> p n f c j", n=2, f=4, c=4) for i in range(2)]
        s_at = two.at
        ab, tm, _ = two.take(AW), two.take(AW), two.take(9 * 256 - 2 * AW)
        states = arena[:, s_at:s_at + 9 * 256].rearrange("p (c e j) -> p c e j", c=9, e=4)
        tmt, rb, ak, rk = two.take(AW), two.take(AW), two.take(AW), two.take(AW)
        qq = ak
        vtk, bhk, khk = two.take(3, 2, P), two.take(2, 2, P), two.take(2, 2, P)
        rhs_at = two.at
        rhs_ = two.take(3, 4, P)
        maps = [arena[:, at:at + 1024].rearrange("p (c e j) -> p c e j", c=4, e=4) for at in (rhs_at, yy_at)]
        ecs = two.take(4, 8)
        v_low = two.take(2, 4, P)

        three = Space(arena, width)
        hf = three.take(KT, L)
        sqb = three.take(KT, L)
        cu = three.take(4, L)
        act2 = three.take(F2, L)
        hq = three.take(KT, L)
        kT, vT, qT, oT = [three.take(KT, L) for _ in range(4)]
        four = Space(arena, width)
        ZW = L + (L - P) + META
        kst, vs2, qst = four.take(2, 384), four.take(2, 384), four.take(2, L)
        zs, ll, ee = [[four.take(2, ZW) for _ in range(2)] for _ in range(3)]
        vk2 = four.take(2, 3, P)
        assert four.at <= KT * L * 2 + 4 * L + F2 * L
        ZC = [0, L, L + L - P]

        for name in ("rw_r", "rw_k", "rw_v", "lora", "exp_kk", "exp_rk", "rw_o", "ffa_up", "ffa_down",
                     "sb_k", "sb_v", "sb_q", "sb_o", "ffb_up", "ffb_down"):
            ev[name] = sem("ev_" + name)
        ld_l = sem("ld_lora")
        mixed, mix_part, gated, centred_sq = sem("mixed"), sem("mixed_slices"), sem("gated"), sem("centred_squares")
        lora_mm, head_mm, lnx, y_root = sem("lora_mm"), sem("head_mm"), sem("lnx"), sem("y_root")
        pe2 = Marks(sem("time_mix_pe"), "w1 a1 g1 kk_sum rk_sum y_sum yv_sum")
        act2m = Marks(sem("time_mix_act"), "tw ta tg tg1 kk_root")
        dve2 = Marks(sem("time_mix_dve"), "kk_sq rk kk_floor kk_inv kkn mu var y_inv")

        def tiles_of(m):
            return range(3) if 2 * m <= META else range(2)

        def top(n):
            return LEVELS[-1] if n < 2 else META // 2

        def per_level(*kinds):
            return " " + " ".join(f"{k}{m}_{n}" for m in LEVELS[1:] for k in kinds for n in tiles_of(m)) + " "
        STAGES_A = "a0_0 a0_1 a1_0 a1_1 a2_0 a2_1"
        rp = Marks(sem("chunk_pe"), "turned ends " + STAGES_A + per_level("y", "u") +
                   "akv_0 akv_1 akv_2 wu_0 wu_1 wu_2 pg_0 pg_1 "
                   "s1 s2 q_0 s3 q_1 s4 q_2 s5 s6 s7 s8 yo_0 yo_1 yo_2")
        ra = Marks(sem("chunk_act"), "vturned turned " + STAGES_A.replace("a", "ab") + per_level("y") +
                   "eye wu_0 wu_1 wu_2 q_0 q_1 q_2")
        rd = Marks(sem("chunk_dve"), "ar bk hats turned ends a0_0 a0_1 t0_0 a1_0 a1_1 t0_1 a2_0 a2_1 t0_2" + per_level("t") +
                   "akv_0 akv_1 akv_2 p_0 p_1 s1 s2 s3 s4 s5 s6 s7 s8 yo_0 yo_1 yo_2")
        rl = Marks(sem("chunk_pool"), "v " + per_level("x") + "bhx khx")
        decays_summed, decays_up = sem("decays_summed"), sem("decays_up")
        ffc, ffs, ffm = sem("conv_tap"), sem("conv_silu"), sem("conv_product")
        k_staged, k_z, k_vt, k_vk, k_abs, k_exp, k_ln, k_zr, k_l1, k_l, k_sfx, k_arg, k_w, k_o, k_od = [
            sem("stick_" + x) for x in ("staged z vt vk abs exp ln zr l1 l sfx arg w o od").split()]
        zeroed = sem("pads_zeroed")
        CHUNK_LINKS = 6

        def take_wait(eng):
            eng.sem_inc(passed, 1)

        def gps(n, w=L):
            return ps[:, n, 0:w]

        def second_sync(sp):
            for i in range(4):
                if i < 3:
                    sp.wait_ge(norm_part, 3 * 7 + i + 1)
                else:
                    sp.wait_ge(normed, 9)
                sp.dma_start(out_t[:, 2 * i:2 * i + 2, :], hf[:, 2 * i:2 * i + 2, META:L]).then_inc(stored, 16)
            sp.wait_ge(stored, 16 * 4)

        def second_tensor(pe, mm, tiles, total):
            total(6, xm[0], KT, L, "r1", squares=(2, 9))
            pe.wait_ge(ld_l, 16 * 7)

            def lora_in(buf, w, m0, m1, bank, mark, k_mix):
                if k_mix > 1:
                    pe.wait_ge(mixed, k_mix)
                for k in range(KT):
                    if k_mix == 1 and k % 2 == 0:
                        pe.wait_ge(mix_part, k // 2 + 1)
                    last = mm(ps[0:m1 - m0, bank, 0:L], w[:, k, m0:m1], buf[:, k, :], k == 0, k == KT - 1)
                if mark:
                    pe2.reach(last, mark)
            lora_in(xm[0], w1s, 0, 64, 4, "w1", 1)
            lora_in(xm[1], a1s, 0, 64, 5, "a1", 2)
            pe.wait_ge(rooted, 9)
            lora_in(xm[2], g1s, 0, P, 6, None, 3)
            lora_in(xm[2], g1s, P, 160, 7, "g1", 3)
            pe.sem_inc(ev["rw_r"], GB)
            pe.sem_inc(ev["rw_k"], GB)
            pe.sem_inc(ev["rw_v"], GB)
            pe.sem_inc(ev["lora"], GB)
            pe.wait_ge(mixed, 4)
            tiles("rw_r", FIRST["rw_r"], 8, xm[0], L)

            def lora_out(w, src, j0, w_b=None, src_b=None):
                for n in range(KT):
                    j = j0 + n
                    pe.wait_ge(ev["lora"], j + 1)
                    o = gps(4 + j % GB)
                    last = mm(o, w[0:src.shape[0], n * P:(n + 1) * P], src, True, w_b is None)
                    if w_b is not None:
                        last = mm(o, w_b[0:32, n * P:(n + 1) * P], src_b, False, True)
                    last.then_inc(lora_mm, 1)
            act2m.wait(pe, "tg1")
            lora_out(w2s, tw[0:64, :], 0)
            pe.wait_ge(ev["rw_r"], GB + 8)
            pe.wait_ge(mixed, 5)
            tiles("rw_k", FIRST["rw_k"], 8, xm[1], L)
            lora_out(a2s, ta[0:64, :], 8)
            lora_out(g2s, tg0[:, :], 16, g2t, tg1[0:32, :])
            pe.wait_ge(ev["rw_k"], GB + 8)
            pe.wait_ge(mixed, 6)
            tiles("rw_v", FIRST["rw_v"], 8, xm[2], L)

            def to_heads(src, bank, mark, done=None):
                for n in range(KT):
                    if done is not None:
                        pe.wait_ge(done, n + 1)
                    last = mm(ps[0:16, bank, 0:L], const("to_head")[:, n * 16:(n + 1) * 16], src[:, n, :],
                              n == 0, n == KT - 1)
                pe2.reach(last, mark)

            def from_heads(src, name, j0=0):
                for n in range(KT):
                    pe.wait_ge(ev[name], j0 + n + 1)
                    mm(gps(4 + n % GB), const("from_head")[0:16, n * P:(n + 1) * P], src[0:16, :]
                       ).then_inc(head_mm, 1)
            dve2.wait(pe, "kk_sq")
            pe.wait_ge(ev["lora"], GB + 24)
            to_heads(xx, 4, "kk_sum")
            dve2.wait(pe, "rk")
            to_heads(hnp[:, :, 0:L], 5, "rk_sum")
            dve2.wait(pe, "kk_inv")
            pe.sem_inc(ev["exp_kk"], GB)
            from_heads(s16a, "exp_kk")
            dve2.wait(pe, "kkn")

            with pe.Fori(0, 4) as it:
                chunk_tensor(pe, mm, it)

            rd.wait(pe, "yo_2", 3)
            to_heads(r_y, 4, "y_sum")
            dve2.wait(pe, "mu")
            from_heads(s16a, "exp_kk", 8)
            to_heads(lw, 0, "yv_sum", centred_sq)
            dve2.wait(pe, "y_inv")
            from_heads(s16a, "exp_kk", 16)
            pe.wait_ge(ev["exp_kk"], GB + 24)
            pe.sem_inc(ev["exp_rk"], GB)
            from_heads(s16b, "exp_rk")
            pe.sem_inc(ev["rw_o"], GB)

            def gated_slice(k):
                if k % 2 == 0:
                    pe.wait_ge(gated, k // 2 + 1)
            tiles("rw_o", FIRST["rw_o"], 8, bb, L, norm=gated_slice)
            ffn_tensor(pe, mm, tiles, total, "ffa", (3, 10), (4, 5))
            total(6, sqb, KT, L, "kv", squares=(4, 11))
            pe.sem_inc(ev["sb_k"], GB)
            tiles("sb_k", FIRST["sb_k"], 8, hf, L, norm=(5, 6))
            pe.wait_ge(ev["sb_k"], GB + 8)
            pe.sem_inc(ev["sb_v"], GB)
            tiles("sb_v", FIRST["sb_v"], 8, hf, L)
            pe.wait_ge(ev["sb_v"], GB + 8)
            pe.wait_ge(normed, 7)
            pe.sem_inc(ev["sb_q"], GB)
            tiles("sb_q", FIRST["sb_q"], 8, hq, L)
            pe.wait_ge(ev["sb_q"], GB + 8)
            stick_units(pe, lambda t, it: stick_tensor(pe, mm, t, it))
            pe.wait_ge(k_od, KT)
            pe.sem_inc(ev["sb_o"], GB)
            tiles("sb_o", FIRST["sb_o"], 8, oT, L)
            ffn_tensor(pe, mm, tiles, total, "ffb", (5, 12), (6, 8))
            total(6, sqb, KT, L, "fin", squares=(6, 13))

        def ffn_tensor(pe, mm, tiles, total, name, squares, norm):
            total(6, sqb, KT, L, name, squares=squares)
            up, down = name + "_up", name + "_down"
            pe.sem_inc(ev[up], GB)
            tiles(up, FIRST[up], 2 * F2, hf, L, norm=norm)
            pe.wait_ge(ev[up], GB + 2 * F2)
            pe.wait_ge(ffm, 2 + F2 if name == "ffa" else 4 + 2 * F2)
            pe.sem_inc(ev[down], GB)
            for n in range(KT):
                pe.wait_ge(ev[down], n + 1)
                for q in range(F2B):
                    b = FIRST[down] + n * F2B + q
                    arrived(pe, b)
                    for k in range(8 * q, min(F2, 8 * q + 8)):
                        last = mm(gps(n % GB), ring[:, b % RING, (k - 8 * q) * P:(k - 8 * q + 1) * P],
                                  act2[:, k, :], k == 0, k == F2 - 1)
                    last.then_inc(used, 1)

        def chunk_tensor(pe, mm, it):
            tr = nc.tensor.transpose

            def head(e):
                p, q = e // 2, e % 2
                return p, q, slice(64 * p, 64 * p + 64)
            rd.wait(pe, "ar", it)
            for n in range(2):
                for q in range(2):
                    tr(ps[:, 0, (2 * n + q) * P:(2 * n + q + 1) * P], ar[:, 0, q, n * P:(n + 1) * P], ident)
            rl.wait(pe, "v", it)
            for n in range(2):
                for q in range(2):
                    tr(ps[:, 1, (2 * n + q) * P:(2 * n + q + 1) * P], vst[:, q, n * P:(n + 1) * P], ident)
            for q in range(2):
                tr(ps[0:META, 5, q * P:(q + 1) * P], ar[:, 0, q, S:L], ident)
                tr(ps[0:META, 5, (2 + q) * P:(3 + q) * P], vst[:, q, S:L], ident)
            rd.wait(pe, "hats", it)
            for n in range(2):
                for q in range(2):
                    tr(ps[:, 2, (2 * n + q) * P:(2 * n + q + 1) * P], bh[:, q, n * P:(n + 1) * P], ident)
                    last = tr(ps[:, 3, (2 * n + q) * P:(2 * n + q + 1) * P], kh[:, q, n * P:(n + 1) * P], ident)
            rp.reach(last, "turned")
            for e in range(4):
                p, q, r = head(e)
                last = mm(ps[0:64, 4, 8 * e:8 * e + 8], const("ident")[:, r], ep[:, q, CH - 1:S:CH])
            rp.reach(last, "ends")
            for n in range(3):
                t0, w = n * P, TW[n]
                for p in range(2):
                    if n == 0 and p == 0:
                        ra.wait(pe, "turned", it)
                        rd.wait(pe, "ends", it)
                    elif n:
                        rd.wait(pe, f"a{n - 1}_{p}", it)
                        ra.wait(pe, f"ab{n - 1}_{p}", it)
                    if n == 2:
                        take_wait(pe)
                    r = slice(64 * p, 64 * p + 64)
                    for q in range(2):
                        both = ar[r, :, q, t0:t0 + w]
                        mm(ps[0:w, p, q * 2 * w:(q + 1) * 2 * w], bt[r, q, t0:t0 + w], both)
                        mm(ps[0:w, 2 + p, q * 2 * w:(q + 1) * 2 * w], kt_[r, q, t0:t0 + w], both)
                        last = mm(ps[0:w, 4 + p, q * w:(q + 1) * w], ar[r, 0, q, t0:t0 + w],
                                  bt[r, q, t0:t0 + w])
                    rp.reach(last, f"a{n}_{p}")
            ybank, uabank, ubbank = [6, 7, 0], [2, 4, 1], [3, 5, 1]
            prev = "t0"
            for li, m in enumerate(LEVELS[1:]):
                for n in tiles_of(m):
                    w = TW[n]
                    rd.wait(pe, f"{prev}_{n}", it)
                    rl.wait(pe, f"x{m}_{n}", it)
                    if n == 2:
                        take_wait(pe)
                    for e in range(4):
                        last = mm(ps[0:w, ybank[n], e * w:(e + 1) * w], sq_blocks(levs[li], n)[:, e, :],
                                  sq_blocks(tm, n)[:, e, :])
                    rp.reach(last, f"y{m}_{n}")
                for n in tiles_of(m):
                    w = TW[n]
                    ra.wait(pe, f"y{m}_{n}", it)
                    o2 = 64 if n == 2 else 0
                    if n == 2:
                        take_wait(pe)
                    for e in range(4):
                        y_e, tt_e = sq_blocks(yy, n)[:, e, :], sq_blocks(tmt, n)[:, e, :]
                        if m != top(n):
                            mm(ps[0:w, uabank[n], e * w:(e + 1) * w], tt_e, y_e)
                        last = mm(ps[0:w, ubbank[n], o2 + e * w:o2 + (e + 1) * w], y_e, tt_e)
                    rp.reach(last, f"u{m}_{n}")
                prev = f"t{m}"
            for n in range(3):
                w = TW[n]
                rd.wait(pe, f"t{top(n)}_{n}", it)
                if n == 2:
                    take_wait(pe)
                for e in range(4):
                    p, q, r = head(e)
                    last = mm(ps[0:w, n, e * 64:(e + 1) * 64], sq_blocks(ak, n)[:, e, :], vtk[0:w, n, q, r])
                rp.reach(last, f"akv_{n}")
            for n in range(3):
                w = TW[n]
                rd.wait(pe, f"akv_{n}", it)
                if n == 2:
                    take_wait(pe)
                for e in range(4):
                    last = mm(ps[0:w, 3 + n, e * P:(e + 1) * P], sq_blocks(tmt, n)[:, e, :], rhs_[0:w, n, e, :])
                rp.reach(last, f"wu_{n}")
            ra.wait(pe, "wu_2", it)
            rl.wait(pe, "khx", it)
            for n in range(2):
                for e in range(4):
                    p, q, r = head(e)
                    mm(ps[:, 4 * n + e, 0:256], wu[:, n, e, :],
                       bhx[:, n, 2 * q + p].rearrange("p c j -> p (c j)"), True, False)
                    last = mm(ps[:, 4 * n + e, 0:256], v_low[:, n, 2 * q + p, :],
                              khx[:, n, 2 * q + p].rearrange("p c j -> p (c j)"), False, True)
                rp.reach(last, f"pg_{n}")

            def state(c):
                rd.wait(pe, f"s{c - 1}" if c > 1 else "p_1", it)
                take_wait(pe)
                rows = slice(64, P) if c == 1 else slice(0, P)
                for e in range(4):
                    last = mm(ps[0:64, 0, 64 * e:64 * e + 64], maps[(c - 1) // 4][rows, (c - 1) % 4, e, :],
                              states[rows, c - 1, e, :])
                rp.reach(last, f"s{c}")

            def queries(n):
                w = TW[n]
                for e in range(4):
                    p, q, r = head(e)
                    o = ps[0:64, 1 + n, e * w:(e + 1) * w]
                    mm(o, wu[0:w, n, e, 0:64], sq_blocks(rb, n)[:, e, :], True, False)
                    last = mm(o, const("ident")[:, r], ar[:, 1, q, n * P:n * P + w], False, True)
                rp.reach(last, f"q_{n}")
            state(1)
            for c in range(2, 9):
                state(c)
                if c < 5:
                    queries(c - 2)
            rd.wait(pe, "s8", it)
            for n in range(3):
                w = TW[n]
                ra.wait(pe, f"q_{n}", it)
                for e in range(4):
                    p, q, r = head(e)
                    o = ps[r, 5 + n, q * w:(q + 1) * w]
                    mm(o, wu[0:w, n, e, 64:P], sq_blocks(rb, n)[:, e, :], True, False)
                    chunks = [c for c in range(4 * n, min(4 * n + 4, 9)) if c]
                    last = mm(o, vtk[0:w, n, q, r], sq_blocks(rk, n)[:, e, :], False, False)
                    for c in chunks:
                        a0 = (c - 4 * n) * CH
                        a1 = min(a0 + CH, w)
                        last = mm(ps[r, 5 + n, q * w + a0:q * w + a1], states[0:64, c, e, :],
                                  qb(n)[0:64, e, a0:a1], False, c == chunks[-1])
                rp.reach(last, f"yo_{n}")

        def qb(n):
            w = TW[n]
            return qq[:, 512 * n:512 * n + 4 * w].rearrange("p (a b) -> p a b", a=4)

        def stick_units(eng, turn):
            turn(0, None)
            turn(1, None)
            with eng.Fori(0, 2) as it:
                turn(2, it)
                turn(3, it)
            for t in range(6, 10):
                turn(t, None)

        def unit(eng, s, u, it):
            if u >= 0:
                eng.wait_ge(s, u + 1 if it is None else it * 2 + (u + 1))

        def z_products(pe, mm, u, it):
            b = u % 2
            unit(pe, k_staged, u, it)
            unit(pe, k_vk, u - 1, it)
            unit(pe, k_zr, u - 2, it)
            for n in range(3):
                last = nc.tensor.transpose(ps[:, 7, n * P:(n + 1) * P], vs2[:, b, n * P:(n + 1) * P], ident)
            last.then_inc(k_vt, 1)
            for p in range(2):
                r = slice(64 * p, 64 * p + 64)
                for i in range(3):
                    last = mm(ps[:, 2 * b + p, ZC[i]:ZC[i] + L - i * P], kst[r, b, i * P:(i + 1) * P],
                              qst[r, b, i * P:L])
            last.then_inc(k_z, 1)

        def stick_tensor(pe, mm, t, it):
            if t == 0:
                z_products(pe, mm, 0, it)
            if 1 <= t <= 8:
                u, b = t - 1, (t - 1) % 2
                unit(pe, k_l, u, it)
                unit(pe, k_arg, u - 1, it)
                for e in range(2):
                    for i in range(3):
                        last = mm(ps[:, 4 + e, ZC[i]:ZC[i] + L - i * P], const("after"),
                                  ll[b][:, e, ZC[i]:ZC[i] + L - i * P], True, i == 2)
                        for j in range(i + 1, 3):
                            w = L - j * P
                            last = mm(ps[:, 4 + e, ZC[i] + (j - i) * P:ZC[i] + (j - i) * P + w],
                                      const("ones"), ll[b][:, e, ZC[j]:ZC[j] + w], False, j == 2)
                last.then_inc(k_sfx, 1)
            if t + 1 <= 7:
                z_products(pe, mm, t + 1, it)
            if 1 <= t <= 8:
                unit(pe, k_w, u, it)
                unit(pe, k_vk, u, it)
                unit(pe, k_od, u - 1, it)
                for p in range(2):
                    r = slice(64 * p, 64 * p + 64)
                    for i in range(3):
                        last = mm(ps[r, 6, i * P:L], vk2[:, b, i, r], ee[b][:, p, ZC[i]:ZC[i] + L - i * P],
                                  i == 0, i == 2)
                last.then_inc(k_o, 1)

        def load_lora(act):
            for dst, src in ((w1s, w1_d), (a1s, a1_d), (g1s, g1_d), (w2s[0:64, :], w2_d), (a2s[0:64, :], a2_d),
                             (g2s, g2_d[0:P, :]), (g2t[0:32, :], g2_d[P:160, :])):
                act.dma_start(dst, src).then_inc(ld_l, 16)

        def second_scalar(act, link, f, root, squares_of_res):
            cp = nc.scalar.copy
            squares_of_res(xm[0], res, res_up, 8)
            root(6, L, which=9)
            pe2.wait(act, "w1")
            act2m.reach(f(tw[0:64, :], ps[0:64, 4, 0:L], ACT.Tanh), "tw")
            pe2.wait(act, "a1")
            act2m.reach(cp(ta[0:64, :], ps[0:64, 5, 0:L]), "ta")
            pe2.wait(act, "g1")
            act2m.reach(f(tg0, ps[:, 6, 0:L], ACT.Sigmoid), "tg")
            act2m.reach(f(tg1[0:32, :], ps[0:32, 7, 0:L], ACT.Sigmoid), "tg1")
            for j in range(24):
                act.wait_ge(lora_mm, j + 1)
                n, src = j % 8, gps(4 + j % GB)
                if j < 8:
                    ins = f(lw[:, n, :], src, ACT.Sigmoid, bias=col("w0", n))
                elif j < 16:
                    ins = f(bb[:, n, :], src, ACT.Sigmoid, bias=col("a0", n))
                else:
                    ins = cp(gg[:, n, :], src)
                ins.then_inc(ev["lora"], 1)
            dve2.wait(act, "kk_floor")
            act2m.reach(f(s16a[0:16, :], s16a[0:16, :], ACT.Sqrt), "kk_root")
            decays_scalar(act, 0)
            with act.Fori(0, 3) as it:
                chunk_scalar(act, it)
            chunk_scalar(act, 3, True)
            dve2.wait(act, "var")
            f(s16a[0:16, :], s16a[0:16, :], ACT.Sqrt).then_inc(y_root, 1)
            for n in range(KT):
                act.wait_ge(ev["exp_kk"], GB + 16 + n + 1)
                ins = f(kkn[:, n, :], kkn[:, n, :], ACT.Identity, scale=col("lnx_g", n), bias=col("lnx_b", n))
                ins.then_inc(lnx, 1)
            squares_of_res(sqb, res, ev["rw_o"], GB, 2)
            ffn_scalar(act, f, root, "ffa", 0, 10)
            squares_of_res(sqb, res, ev["ffa_down"], GB, 2)
            root(6, L, which=11)
            stick_units(act, lambda t, it: stick_scalar(act, f, t, it))
            squares_of_res(sqb, res, ev["sb_o"], GB, 2)
            ffn_scalar(act, f, root, "ffb", 1, 12)
            squares_of_res(sqb, res, ev["ffb_down"], GB, 2)
            root(6, L, which=13)

        def ffn_scalar(act, f, root, name, layer, which):
            root(6, L, which=which)
            b = FIRST[name + "_up"]
            wc = COLS["conv_w"] + layer * 3 * 2 * F2 + 2 * 2 * F2
            bc = COLS["conv_b"] + layer * 2 * F2
            m0 = layer * (2 + F2)

            def pair(m, it=None):
                for s in (2 * m, 2 * m + 1):
                    add = (lambda v: v) if it is None else (lambda v: it * 8 + v)
                    addp = (lambda v: v) if it is None else (lambda v: it * 4 + v)
                    act.wait_ge(used, add(b + s + 1))
                    act.wait_ge(ffm, addp(m0 + m + 1))
                    if it is None:
                        sc, bi = cols[:, wc + s:wc + s + 1], cols[:, bc + s:bc + s + 1]
                    else:
                        sc, bi = cols[:, bass.ds(it * 8 + (wc + s), 1)], cols[:, bass.ds(it * 8 + (bc + s), 1)]
                    f(cu[:, s % 4, :], gps(s % GB), ACT.Identity, scale=sc, bias=bi).then_inc(ffc, 1)
                act.wait_ge(ev[name + "_up"], add(GB + 2 * m + 1))
                f(cu[:, (2 * m) % 4, :], cu[:, (2 * m) % 4, :], ACT.Silu).then_inc(ffs, 1)
            with act.Fori(0, 5) as it:
                for m in range(4):
                    pair(m, it)
            for m in (20, 21):
                pair(m)

        def decays_scalar(act, t):
            f = nc.scalar.activation
            act.wait_ge(decays_summed, t + 1)
            f(ep, cum, ACT.Exp)
            f(epre, epre, ACT.Exp)
            f(en, cum, ACT.Exp, scale=-1.0)
            f(eh, eh, ACT.Exp).then_inc(decays_up, 1)

        def chunk_scalar(act, it, last_turn=False):
            f, cp = nc.scalar.activation, nc.scalar.copy
            rp.wait(act, "turned", it)
            src = ps[:, 0, :].rearrange("p (n q r j) -> p n q r j", n=2, q=2, r=2)
            for n in range(2):
                for r in range(2):
                    cp(rhs_[:, n, 2 * r:2 * r + 2, 0:64], src[:, n, :, r, :])
            ra.reach(cp(vtk[:, 0:2], ps[:, 1, :].rearrange("p (n q j) -> p n q j", n=2, q=2)), "vturned")
            ra.reach(cp(bhk, ps[:, 2, :].rearrange("p (n q j) -> p n q j", n=2, q=2)), "turned")
            for n in range(3):
                w = TW[n]
                for p in range(2):
                    rp.wait(act, f"a{n}_{p}", it)
                    ra.reach(cp(sq_blocks(ab, n)[:, 2 * p:2 * p + 2, :],
                                ps[0:w, p, 0:4 * w].rearrange("p (q k t) -> p q k t", q=2, k=2)[:, :, 0, :]),
                             f"ab{n}_{p}")
            ybank = [6, 7, 0]
            for m in LEVELS[1:]:
                for n in tiles_of(m):
                    w = TW[n]
                    rp.wait(act, f"y{m}_{n}", it)
                    ra.reach(cp(sq_blocks(yy, n), ps[0:w, ybank[n], 0:4 * w].rearrange(
                        "p (a b) -> p a b", a=4)), f"y{m}_{n}")
            ra.reach(cp(states[64:P, 0:8].rearrange("p c e j -> p (c e) j"),
                        const("ident")[64:P, 64:P].unsqueeze(1).to_broadcast([64, 32, 64])), "eye")
            for n in range(3):
                w = TW[n]
                rp.wait(act, f"wu_{n}", it)
                ra.reach(cp(wu[0:w, n], ps[0:w, 3 + n, :].rearrange("p (a b) -> p a b", a=4)), f"wu_{n}")
            if not last_turn:
                decays_scalar(act, it + 1)
            for n in range(3):
                w = TW[n]
                rp.wait(act, f"q_{n}", it)
                ra.reach(cp(qb(n)[0:64], ps[0:64, 1 + n, 0:4 * w].rearrange("p (a b) -> p a b", a=4)), f"q_{n}")

        def stick_scalar(act, f, t, it):
            if t <= 7:
                u, b = t, t % 2
                unit(act, k_vt, u, it)
                unit(act, k_o, u - 2, it)
                nc.scalar.copy(vk2[:, b], ps[:, 7, 0:3 * P].rearrange("p (a b) -> p a b", a=3)).then_inc(k_vk, 1)
                unit(act, k_z, u, it)
                f(ee[b], ps[:, 2 * b:2 * b + 2, 0:ZW], ACT.Abs, scale=0.125).then_inc(k_abs, 1)
                unit(act, k_abs, u, it)
                f(ee[b], ee[b], ACT.Exp, scale=-1.0).then_inc(k_exp, 1)
                unit(act, k_exp, u, it)
                f(ee[b], ee[b], ACT.Ln, bias=one_c).then_inc(k_ln, 1)
            if 1 <= t <= 8:
                u, b = t - 1, (t - 1) % 2
                unit(act, k_arg, u, it)
                f(ee[b], zs[b], ACT.Exp).then_inc(k_w, 1)

        def second_vector(dve, link, v, tt, stt, ts, inverse_root, residual, normed_to, take):
            cpv = v.tensor_copy
            dve.wait_ge(sqd, 9)
            link(v.memset(hnp[:, :, 0:1], 0.0))
            hn = hnp[:, :, 1:L + 1]
            link(tt(hn, res[:], col_wide("mix_g", 0, KT, L), ALU.mult))
            normed_to(hn, 9, L, 4)
            dve.wait_ge(normed, 4)
            for i in range(4):
                c = slice(2 * i, 2 * i + 2)
                link(tt(xx[:, c, :], hnp[:, c, 0:L], hn[:, c, :], ALU.subtract))
                for k in (2 * i, 2 * i + 1):
                    last = stt(out=xm[0][:, k, :], in0=xx[:, k, :], scalar=col("rw_mix", 8 + k), in1=hn[:, k, :],
                               op0=ALU.mult, op1=ALU.add)
                last.then_inc(mix_part, 1)
            dve.sem_inc(mixed, 1)
            for j, (which, buf) in enumerate(((4, 1), (5, 2), (0, 0), (2, 1), (3, 2)), 1):
                if j >= 3:
                    pe2.wait(dve, ("w1", "a1", "g1")[j - 3])
                for k in range(KT):
                    last = stt(out=xm[buf][:, k, :], in0=xx[:, k, :], scalar=col("rw_mix", 8 * which + k),
                               in1=hn[:, k, :], op0=ALU.mult, op1=ALU.add)
                last.then_inc(mixed, 1)
            dve.wait_ge(mixed, 6)
            take("rw_r", FIRST["rw_r"], 8, r_y, L)
            take("rw_k", FIRST["rw_k"], 8, k2, L)
            dve.wait_ge(ev["rw_k"], GB + 8)
            link(tt(kkn, k2, col_wide("k_k", 0, KT, L), ALU.mult))
            dve2.reach(tt(xx, kkn, kkn, ALU.mult), "kk_sq")
            dve.wait_ge(ev["lora"], GB + 16)
            link(stt(out=hnp[:, :, 0:L], in0=bb, scalar=-1.0, in1=col_wide("k_a", 0, KT, L), op0=ALU.add,
                     op1=ALU.mult))
            link(stt(out=k2, in0=hnp[:, :, 0:L], scalar=1.0, in1=k2, op0=ALU.add, op1=ALU.mult))
            link(tt(hnp[:, :, 0:L], r_y, k2, ALU.mult))
            dve2.reach(tt(hnp[:, :, 0:L], hnp[:, :, 0:L], col_wide("r_k", 0, KT, L), ALU.mult), "rk")
            link(ts(lw, lw, -float(np.exp(-0.5)), None, ALU.mult))
            take("rw_v", FIRST["rw_v"], 8, vv, L)
            pe2.wait(dve, "kk_sum")
            dve2.reach(ts(s16a[0:16, :], ps[0:16, 4, 0:L], 1e-24, None, ALU.max), "kk_floor")
            pe2.wait(dve, "rk_sum")
            link(cpv(s16b[0:16, :], ps[0:16, 5, 0:L]))
            act2m.wait(dve, "kk_root")
            dve2.reach(v.reciprocal(s16a[0:16, :], s16a[0:16, :]), "kk_inv")
            decays_vector(dve, link, 0, v, tt)
            v.memset(ecs, 0.0)
            link(v.memset(v_low, 0.0))

            def heads_times(dst, src, name, mm0, op=ALU.mult, ext=None):
                for n in range(KT):
                    dve.wait_ge(head_mm, mm0 + n + 1)
                    tt(dst[:, n, :], src[:, n, :], gps(4 + n % GB), op).then_inc(ev[name], 1)
                    if ext is not None:
                        ext(n)
            heads_times(kkn, kkn, "exp_kk", 0)
            dve.wait_ge(ev["exp_kk"], GB + 8)
            dve2.reach(tt(bb, kkn, bb, ALU.mult), "kkn")
            dve2.wait(dve, "kkn")
            with dve.Fori(0, 3) as it:
                link.enter(it, CHUNK_LINKS)
                chunk_vector(dve, link, it, v, tt, stt, cpv)
                link.leave(3)
            chunk_vector(dve, link, 3, v, tt, stt, cpv, True)
            rd.wait(dve, "yo_2", 3)
            pe2.wait(dve, "y_sum")
            dve2.reach(ts(s16a[0:16, :], ps[0:16, 4, 0:L], 1.0 / 64, None, ALU.mult), "mu")
            def square(n):
                dve.wait_ge(ev["exp_kk"], GB + 8 + n + 1)
                tt(lw[:, n, :], kkn[:, n, :], kkn[:, n, :], ALU.mult).then_inc(centred_sq, 1)
            heads_times(kkn, r_y, "exp_kk", 8, ALU.subtract, square)
            pe2.wait(dve, "yv_sum")
            dve2.reach(ts(s16a[0:16, :], ps[0:16, 0, 0:L], 1.0 / 64, GN_EPS, ALU.mult, ALU.add), "var")
            dve.wait_ge(y_root, 1)
            dve2.reach(v.reciprocal(s16a[0:16, :], s16a[0:16, :]), "y_inv")
            heads_times(kkn, kkn, "exp_kk", 16)
            heads_times(r_y, vv, "exp_rk", 24)
            dve.wait_ge(lnx, 8)
            dve.wait_ge(ev["exp_rk"], GB + 8)
            for i in range(4):
                c = slice(2 * i, 2 * i + 2)
                link(tt(kkn[:, c, :], kkn[:, c, :], r_y[:, c, :], ALU.add))
                tt(bb[:, c, :], kkn[:, c, :], gg[:, c, :], ALU.mult).then_inc(gated, 1)

            def add_to_res(name, per):
                for j in range(KT):
                    dve.wait_ge(used, FIRST[name] + per * (j + 1))
                    tt(res[:, j, :], res[:, j, :], gps(j % GB), ALU.add).then_inc(ev[name], 1)
            add_to_res("rw_o", 1)
            ffn_vector(dve, link, tt, stt, normed_to, add_to_res, "ffa", 0, 10)
            dve.wait_ge(ev["ffa_down"], GB + 8)
            link(tt(hf, res[:], col_wide("kv_g", 0, KT, L), ALU.mult))
            link(tt(hq, res[:], col_wide("mix_g", 8, KT, L), ALU.mult))
            normed_to(hf, 11, L, 6)
            tt(hq, hq, over(rs[:, 0:L], KT), ALU.mult).then_inc(normed, 1)
            take("sb_k", FIRST["sb_k"], 8, kT, L)
            take("sb_v", FIRST["sb_v"], 8, vT, L)
            v.memset(kst[:, :, L:384], 0.0)
            v.memset(vs2[:, :, L:384], 0.0).then_inc(zeroed, 1)
            take("sb_q", FIRST["sb_q"], 8, qT, L)
            stick_units(dve, lambda t, it: stick_vector(dve, t, it, v, tt, stt, ts, cpv))
            add_to_res("sb_o", 1)
            ffn_vector(dve, link, tt, stt, normed_to, add_to_res, "ffb", 1, 12)
            dve.wait_ge(ev["ffb_down"], GB + 8)
            link(tt(hf, res[:], col_wide("fin_g", 0, KT, L), ALU.mult))
            normed_to(hf, 13, L, 9)

        def ffn_vector(dve, link, tt, stt, normed_to, add_to_res, name, layer, which):
            dve.wait_ge(ev["rw_o" if layer == 0 else "sb_o"], GB + 8)
            link(tt(hf, res[:], col_wide("ffn_g", 8 * layer, KT, L), ALU.mult))
            normed_to(hf, which, L, 0)
            wc = COLS["conv_w"] + layer * 3 * 2 * F2
            dve.sem_inc(ffm, 2)

            def pair(m, it=None):
                add = (lambda x: x) if it is None else (lambda x: it * 8 + x)
                addp = (lambda x: x) if it is None else (lambda x: it * 4 + x)
                for s in (2 * m, 2 * m + 1):
                    dve.wait_ge(ffc, add(layer * 2 * F2 + s + 1))
                    for back, tap in ((1, 1), (2, 0)):
                        at = wc + tap * 2 * F2 + s
                        w = cols[:, at:at + 1] if it is None else cols[:, bass.ds(it * 8 + at, 1)]
                        c = cu[:, s % 4, back:L]
                        ins = stt(out=c, in0=ps[:, s % GB, 0:L - back], scalar=w, in1=c, op0=ALU.mult,
                                  op1=ALU.add)
                        if back == 1:
                            link(ins)
                        else:
                            ins.then_inc(ev[name + "_up"], 1)
                dve.wait_ge(ev[name + "_up"], add(GB + 2 * m + 2))
                dve.wait_ge(ffs, addp(layer * F2 + m + 1))
                dst = act2[:, m, :] if it is None else act2[:, bass.ds(it * 4 + m, 1), :]
                tt(dst, cu[:, (2 * m) % 4, :], cu[:, (2 * m + 1) % 4, :], ALU.mult).then_inc(ffm, 1)
            with dve.Fori(0, 5) as it:
                link.enter(it, 8)
                for m in range(4):
                    pair(m, it)
                link.leave(5)
            for m in (20, 21):
                pair(m)
            add_to_res(name + "_down", F2B)

        def masks(name, w, n):
            return const(name, w)[:, 0:w].unsqueeze(1).to_broadcast([w, n, w])

        def decays_vector(dve, link, t, v, tt):
            for q in range(2):
                link(v.tensor_tensor_scan(cum[:, q, :], const("scan"),
                                          lw[:, bass.ds(t * 2 + q, 1), :].rearrange("p a b -> p (a b)"),
                                          0.0, ALU.mult, ALU.add))
            tt(epre, cum, lw[:, bass.ds(t * 2, 2), :], ALU.subtract)
            c4 = cum[:, :, 0:S].rearrange("p q (c t) -> p q c t", c=8)
            tt(eh.rearrange("p q (c t) -> p q c t", c=8), c4[:, :, :, CH - 1:CH].to_broadcast([P, 2, 8, CH]),
               c4, ALU.subtract).then_inc(decays_summed, 1)

        def chunk_vector(dve, link, it, v, tt, stt, cpv, last_turn=False):
            two_ = bass.ds(it * 2, 2)
            dve.wait_ge(decays_up, it + 1)
            stt(out=ar[:, 0], in0=kkn[:, two_, :], scalar=-1.0, in1=epre, op0=ALU.mult, op1=ALU.mult)
            rd.reach(tt(ar[:, 1], r_y[:, two_, :], ep, ALU.mult), "ar")
            tt(bt, bb[:, two_, :], en, ALU.mult)
            rd.reach(tt(kt_, k2[:, two_, :], en, ALU.mult), "bk")
            tt(bh, bb[:, two_, 0:S], eh, ALU.mult)
            rd.reach(tt(kh, k2[:, two_, 0:S], eh, ALU.mult), "hats")
            rp.wait(dve, "turned", it)
            cpv(khk, ps[:, 3, :].rearrange("p (n q j) -> p n q j", n=2, q=2))
            last = ps[0:META, 5, :].rearrange("p (k q r j) -> p k q r j", k=2, q=2, r=2)
            for r in range(2):
                cpv(rhs_[0:META, 2, 2 * r:2 * r + 2, 0:64], last[:, 0, :, r, :])
            rd.reach(cpv(vtk[0:META, 2], ps[0:META, 5, 256:512].rearrange("p (q j) -> p q j", q=2)), "turned")
            rp.wait(dve, "ends", it)
            rd.reach(cpv(ecs[0:64], ps[0:64, 4, 0:32].rearrange("p (e c) -> p e c", e=4)), "ends")
            for n in range(3):
                w = TW[n]
                for p in range(2):
                    rp.wait(dve, f"a{n}_{p}", it)
                    ab_rb = ps[0:w, p, 0:4 * w].rearrange("p (q k t) -> p q k t", q=2, k=2)
                    ak_rk = ps[0:w, 2 + p, 0:4 * w].rearrange("p (q k t) -> p q k t", q=2, k=2)

                    def half(buf):
                        return sq_blocks(buf, n)[:, 2 * p:2 * p + 2, :]
                    tt(half(ak), ak_rk[:, :, 0, :], masks("chunk_strict", w, 2), ALU.mult)
                    tt(half(rk), ak_rk[:, :, 1, :], masks("chunk_incl", w, 2), ALU.mult)
                    tt(half(tm), ps[0:w, 4 + p, 0:2 * w].rearrange("p (q t) -> p q t", q=2),
                       masks("level1t", w, 2), ALU.mult)
                    ra.wait(dve, f"ab{n}_{p}", it)
                    rd.reach(tt(half(rb), ab_rb[:, :, 1, :], masks("chunk_incl", w, 2), ALU.mult), f"a{n}_{p}")
                link(tt(sq_blocks(tmt, n), sq_blocks(ab, n), masks("level1", w, 4), ALU.mult))
                tt(sq_blocks(tm, n), sq_blocks(tm, n), masks("ident", w, 4), ALU.add)
                rd.reach(tt(sq_blocks(tmt, n), sq_blocks(tmt, n), masks("ident", w, 4), ALU.add), f"t0_{n}")
            uabank, ubbank = [2, 4, 1], [3, 5, 1]
            for m in LEVELS[1:]:
                for n in tiles_of(m):
                    w = TW[n]
                    o2 = 64 if n == 2 else 0
                    rp.wait(dve, f"u{m}_{n}", it)
                    if m != top(n):
                        tt(sq_blocks(tm, n), sq_blocks(tm, n),
                           ps[0:w, uabank[n], 0:4 * w].rearrange("p (a b) -> p a b", a=4), ALU.add)
                    rd.reach(tt(sq_blocks(tmt, n), sq_blocks(tmt, n),
                                ps[0:w, ubbank[n], o2:o2 + 4 * w].rearrange("p (a b) -> p a b", a=4),
                                ALU.add), f"t{m}_{n}")
            for n in range(3):
                w = TW[n]
                rp.wait(dve, f"akv_{n}", it)
                rd.reach(cpv(rhs_[0:w, n, :, 64:P], ps[0:w, n, 0:256].rearrange("p (a b) -> p a b", a=4)),
                         f"akv_{n}")
            rp.wait(dve, "wu_2", it)
            for n in range(2):
                last = tt(maps[n], const("ident")[:, 0:64].unsqueeze(1).unsqueeze(1).to_broadcast([P, 4, 4, 64]),
                   ecs[:, :, 4 * n:4 * n + 4].rearrange("p e c -> p c e").unsqueeze(3).to_broadcast(
                       [P, 4, 4, 64]), ALU.mult)
            link(last)
            for n in range(2):
                if n == 1 and not last_turn:
                    decays_vector(dve, link, it + 1, v, tt)
                rp.wait(dve, f"pg_{n}", it)
                at = maps[n].rearrange("p c e j -> p e c j")
                rd.reach(tt(at, at, ps[:, 4 * n:4 * n + 4, 0:256].rearrange("p e (c j) -> p e c j", c=4), ALU.add),
                         f"p_{n}")
            for c in range(1, 9):
                rp.wait(dve, f"s{c}", it)
                rd.reach(cpv(states[0:64, c], ps[0:64, 0, 0:256].rearrange("p (e j) -> p e j", e=4)), f"s{c}")
            for n in range(3):
                w = TW[n]
                rp.wait(dve, f"yo_{n}", it)
                take_wait(dve)
                rd.reach(cpv(r_y[:, two_, n * P:n * P + w],
                             ps[:, 5 + n, 0:2 * w].rearrange("p (q t) -> p q t", q=2)), f"yo_{n}")

        def stick_vector(dve, t, it, v, tt, stt, ts, cpv):
            diag = [(ZC[i], min(P, L - i * P)) for i in range(3)]
            rest = [(P, L), (L + P, L + P + META)]
            if t <= 7:
                b = t % 2
                unit(dve, k_abs, t, it)
                unit(dve, k_w, t - 2, it)
                z = ps[:, 2 * b:2 * b + 2, 0:ZW]
                for a, w in diag:
                    stt(out=zs[b][:, :, a:a + w], in0=z[:, :, a:a + w], scalar=0.125,
                        in1=over(const("strict_neg")[:, 0:w], 2), op0=ALU.mult, op1=ALU.add)
                for a, e in rest:
                    ts(zs[b][:, :, a:e], z[:, :, a:e], 0.125, None, ALU.mult)
                ts(ll[b], z, 0.125, 0.0, ALU.mult, ALU.max).then_inc(k_zr, 1)
            if 1 <= t <= 8:
                unit(dve, k_sfx, t - 1, it)
                c = (t - 1) % 2
                tt(zs[c], zs[c], ps[:, 4:6, 0:ZW], ALU.add).then_inc(k_arg, 1)
            if t <= 7:
                unit(dve, k_ln, t, it)
                unit(dve, k_zr, t, it)
                stt(out=ll[b], in0=ll[b], scalar=-1.0, in1=ee[b], op0=ALU.mult,
                    op1=ALU.subtract).then_inc(k_l1, 1)
                unit(dve, k_l1, t, it)
                for a, w in diag:
                    last = tt(ll[b][:, :, a:a + w], ll[b][:, :, a:a + w], over(const("strict")[:, 0:w], 2),
                              ALU.mult)
                last.then_inc(k_l, 1)
            if t >= 2:
                u = t - 2
                unit(dve, k_o, u, it)
                dst = oT[:, u, :] if it is None else oT[:, bass.ds(it * 2 + u, 1), :]
                if it is not None:
                    take_wait(dve)
                cpv(dst, ps[:, 6, 0:L]).then_inc(k_od, 1)

        def second_gpsimd(pool, link, g):
            with pool.Fori(0, 4) as it:
                pool.wait_ge(decays_summed, it + 1)
                pool.wait_ge(rp.sem, it * len(rp.names))
                rl.reach(g.tensor_copy(vst, vv[:, bass.ds(it * 2, 2), :]), "v")
                for li, m in enumerate(LEVELS[1:]):
                    for n in tiles_of(m):
                        w = TW[n]
                        if li == 0:
                            ra.wait(pool, f"ab{n}_1", it)
                        rl.reach(g.tensor_tensor(sq_blocks(levs[li], n), sq_blocks(ab, n),
                                                 const(f"level{m}", w)[:, 0:w].unsqueeze(1).to_broadcast(
                                                     [w, 4, w]), ALU.mult), f"x{m}_{n}")
                g.tensor_copy(v_low[:, :, :, 64:P], vtk[:, 0:2].rearrange("p n q (r j) -> p n (q r) j", r=2))
                chunk_of = const("chunk_incl")[:, CH - 1:P:CH].unsqueeze(1).unsqueeze(3)
                rp.wait(pool, "y16_1", it)
                ra.wait(pool, "turned", it)
                for dst, src, mark in ((bhx, bhk, "bhx"), (khx, khk, "khx")):
                    for n in range(2):
                        last = g.tensor_tensor(
                            dst[:, n], src[:, n].rearrange("p q (r j) -> p (q r) j", r=2).unsqueeze(2)
                            .to_broadcast([P, 4, 4, 64]), chunk_of.to_broadcast([P, 4, 4, 64]), ALU.mult)
                    rl.reach(last, mark)
            pool.wait_ge(zeroed, 1)
            pool.wait_ge(ev["sb_v"], GB + KT)
            for u in range(2):
                stage_keys(g, u, slice(u, u + 1))
            pool.wait_ge(ev["sb_q"], GB + KT)
            for u in range(2):
                stage_queries(g, u, slice(u, u + 1))
            with pool.Fori(0, 3) as it:
                for u in (2, 3):
                    stage_unit(pool, g, u, it)

        def stage_keys(g, b, at):
            g.tensor_copy(kst[:, b:b + 1, 0:L], kT[:, at, :])
            g.tensor_copy(vs2[:, b:b + 1, 0:L], vT[:, at, :])

        def stage_queries(g, b, at):
            g.tensor_copy(qst[:, b:b + 1, :], qT[:, at, :]).then_inc(k_staged, 1)

        def stage_unit(pool, g, u, it):
            unit(pool, k_z, u - 2, it)
            take_wait(pool)
            at = bass.ds(it * 2 + u, 1)
            stage_keys(g, u % 2, at)
            stage_queries(g, u % 2, at)
        block = ctx.enter_context(nc.Block())

        @block.sync
        def _(sp):
            sp.dma_start(xr, x_t).then_inc(ld_x, 16)
            sp.dma_start(consts[:], consts_d).then_inc(ld_c, 16)
            sp.dma_start(cols[:], cols_d).then_inc(ld_c, 16)
            for b in range(RING):
                sp.dma_start(ring[:, b, :], stream[b]).then_inc(landed[b], 16)
            turns = (N_BLOCKS - RING) // RING
            with sp.Fori(0, turns) as i:
                for s in range(RING):
                    sp.wait_ge(used, i * RING + (s + 1))
                    sp.dma_start(ring[:, s, :], stream[bass.ds(i * RING + (RING + s), 1)].rearrange(
                        "o p c -> p (o c)")).then_inc(landed[s], 16)
            for b in range(RING + turns * RING, N_BLOCKS):
                sp.wait_ge(used, b - RING + 1)
                sp.dma_start(ring[:, b % RING, :], stream[b]).then_inc(landed[b % RING], 16)
            second_sync(sp)

        @block.tensor
        def _(pe):
            def mm(out, lhs, rhs, start=True, stop=True):
                return nc.tensor.matmul(out, lhs, rhs, start=start, stop=stop)

            def tiles(name, b0, n, rhs, t, j0=0, ev_sem=None, norm=None):
                e = ev_sem or ev[name]

                def body(s, it=None):
                    b, j = b0 + s, j0 + s
                    arrived(pe, b, it)
                    pe.wait_ge(e, j + 1 if it is None else it * RING + (j + 1))
                    for k in range(KT):
                        if callable(norm) and s == 0:
                            norm(k)
                        elif norm and s == 0:
                            slice_done(norm_part, normed, norm, k)
                        last = mm(ps[:, j % GB, 0:t], ring[:, b % RING, k * P:(k + 1) * P], rhs[:, k, :],
                                  k == 0, k == KT - 1)
                    last.then_inc(used, 1)
                turns = n // RING if n >= 2 * RING else 0
                if turns:
                    with pe.Fori(0, turns) as it:
                        for s in range(RING):
                            body(s, it)
                for s in range(turns * RING, n):
                    body(s)

            def slice_done(part, whole, which, k):
                if k in (0, 2, 4):
                    pe.wait_ge(part, 3 * which[0] + k // 2 + 1)
                elif k == 6:
                    pe.wait_ge(whole, which[1])

            def total(bank, src, n, t, which, matrix="mean", squares=None):
                for k in range(n):
                    if squares:
                        slice_done(sq_part, sqd, squares, k)
                    last = mm(ps[:, bank, 0:t], const(matrix), src[:, k, :], k == 0, k == n - 1)
                last.then_inc(summed, 1)

            pe.wait_ge(ld_c, 32)
            pe.wait_ge(sqd, 1)
            total(4, sq, KT, S, "mem")
            pe.wait_ge(sqd, 2)
            total(5, merged, KT, S, "in")
            pe.sem_inc(ev["qkvs"], GB)
            tiles("qkvs", FIRST["in"], 18, h, S, norm=(0, 1))
            pe.wait_ge(ev["qkvs"], GB + N_QKV)
            pe.wait_ge(summed, 2)
            pe.wait_ge(rooted, 2)
            for kv in range(2):
                r = slice(64 * kv, 64 * kv + 64)
                for t in range(4):
                    last = mm(ps[:, 4 + 2 * kv + t // 2, (t % 2) * 256:(t % 2) * 256 + 256],
                              qkv[r, t, P:S], qkv[r, 4, :])
            last.then_inc(at_s, 1)
            pe.wait_ge(ev["qkvs"], GB + 18)
            pe.sem_inc(ev["gate"], GB)
            tiles("gate", FIRST["in"] + 18, 8, h, S)
            pe.wait_ge(at_m, 1)
            for kv in range(2):
                r = slice(64 * kv, 64 * kv + 64)
                for t in range(4):
                    last = mm(ps[:, 4 + kv, t * P:(t + 1) * P], qkv[r, t, 0:P], qkv[r, 4, 0:P])
            last.then_inc(at_s, 1)
            pe.wait_ge(sqd, 3)
            total(6, tmp, 4, S, "sgu")
            for c in range(2):
                last = nc.tensor.transpose(ps[:, 7, c * P:(c + 1) * P], qkv[:, 5, c * P:(c + 1) * P], ident)
            last.then_inc(at_t, 1)
            tiles("gate", FIRST["in"] + 26, 16, h, S, j0=8)
            pe.wait_ge(at_n, 1)
            pe.wait_ge(at_m, 2)
            pe.wait_ge(rooted, 3)
            pe.wait_ge(at_tc, 1)
            for c in range(2):
                for e in range(8):
                    last = nc.tensor.transpose(ps[:, 4 + 2 * c + e // 4, (e % 4) * P:(e % 4 + 1) * P],
                                               sc1[:, e, c * P:(c + 1) * P], ident)
            last.then_inc(at_t, 1)
            pe.wait_ge(ev["gate"], GB + 24)
            pe.wait_ge(sg_n, 1)
            for c in range(2):
                for g in range(4):
                    last = nc.tensor.transpose(ps[:, c, g * P:(g + 1) * P], sv[:, g, c * P:(c + 1) * P], ident)
            last.then_inc(sg_t, 1)
            pe.wait_ge(pl_w, 1)
            pe.wait_ge(ld_s, 16 * 5)
            for g in range(4):
                last = mm(ps[:, 2 + g // 2, (g % 2) * S:(g % 2 + 1) * S], wpl[:, g, :], pcp[:, g, META:L])
            last.then_inc(pl_o, 1)
            pe.wait_ge(at_tc, 2)
            pe.wait_ge(at_n, 2)
            for e in range(8):
                last = nc.tensor.transpose(ps[:, 4 + e // 4, (e % 4) * P:(e % 4 + 1) * P], sc0[:, e, :], ident)
            last.then_inc(at_t, 1)
            pe.wait_ge(sg_tc, 1)
            pe.wait_ge(init_done, 1)
            for c in range(2):
                for g in range(4):
                    o = ps[:, 6 + c, g * P:(g + 1) * P]
                    mm(o, svt[:, c, g * P:(g + 1) * P], wst[:, g, :], True, False)
                    last = mm(o, const("ones", 1), bsp[0:1, g * P:(g + 1) * P], False, True)
            last.then_inc(sg_o, 1)
            pe.wait_ge(at_tc, 3)
            for kv in range(2):
                o = ps[64 * kv:64 * kv + 64, 0, :]
                vs = slice(64 * kv, 64 * kv + 64)
                mm(o, vtok[:, 0, vs], pt0[:, 4 * kv:4 * kv + 4, :])
                o = ps[64 * kv:64 * kv + 64, 1, :]
                mm(o, vtok[:, 0, vs], pt1[:, 0, 4 * kv:4 * kv + 4, :], True, False)
                last = mm(o, vtok[:, 1, vs], pt1[:, 1, 4 * kv:4 * kv + 4, :], False, True)
            last.then_inc(at_o, 1)
            pe.wait_ge(at_y, 1)
            pe.wait_ge(sg_y, 1)
            pe.wait_ge(pl_y, 1)
            pe.sem_inc(ev["branch"], GB)
            for u in range(24):
                b = FIRST["branch"] + u // 2
                if u % 2 == 0:
                    arrived(pe, b)
                pe.wait_ge(ev["branch"], u + 1)
                src = (ya, yb, yc)[u % 3]
                for k in range(4):
                    kk = (u % 2) * 4 + k
                    last = mm(ps[:, u % GB, 0:S], ring[:, b % RING, kk * P:(kk + 1) * P], src[:, k, :],
                              k == 0, k == 3)
                last.then_inc(used if u % 2 else halves, 1)
            pe.wait_ge(ev["branch"], GB + 24)
            pe.wait_ge(merged_done, 1)
            pe.sem_inc(ev["out"], GB)
            tiles("out", FIRST["out"], 8, merged, S)
            pe.wait_ge(sqd, 4)
            pe.wait_ge(sg_y, 1)
            total(6, sq, KT, S, "out")
            pe.wait_ge(ev["out"], GB + 8)
            pe.wait_ge(normed0, 1)
            pe.sem_inc(ev["mem_k"], GB)
            tiles("mem_k", FIRST["mem_kv"], 4, memn, S)
            total(7, sq, KT, S, "hm", squares=(0, 5))
            pe.wait_ge(ev["mem_k"], GB + 4)
            for j in range(4):
                b = FIRST["mem_kv"] + 4 + j
                arrived(pe, b)
                for c in range(2):
                    for k in range(KT):
                        last = mm(ps[:, c, j * P:(j + 1) * P], memn[:, k, c * P:(c + 1) * P],
                                  ring[:, b % RING, k * P:(k + 1) * P], k == 0, k == KT - 1)
                last.then_inc(used, 1)
            pe.wait_ge(ev["mem_v"], 1)
            pe.wait_ge(normed, 2)
            pe.sem_inc(ev["mem_q"], GB)
            tiles("mem_q", FIRST["mem_q"], 4, h, S)
            pe.wait_ge(ev["mem_q"], GB + 4)
            for c in range(2):
                for e in range(4):
                    last = mm(ps[:, 4 + 2 * c + e // 2, (e % 2) * 256:(e % 2) * 256 + 256],
                              qm[:, e, c * P:(c + 1) * P], memk[:, e, :])
            last.then_inc(mm_s, 1)
            pe.wait_ge(mm_n, 1)
            for c in range(2):
                for m in range(2):
                    for e in range(4):
                        last = nc.tensor.transpose(ps[:, 2 * m + c, e * P:(e + 1) * P],
                                                   msc[:, 4 * c + e, m * P:(m + 1) * P], ident)
            last.then_inc(mm_t, 1)
            pe.wait_ge(mm_tc, 4)
            for c in range(2):
                for e in range(4):
                    o = ps[:, 4 + c, e * P:(e + 1) * P]
                    for m in range(2):
                        last = mm(o, memv[:, m, e * P:(e + 1) * P], mpt[:, m, 4 * c + e, :], m == 0, m == 1)
            last.then_inc(mm_o, 1)
            pe.wait_ge(mm_y, 2)
            pe.sem_inc(ev["mem_o"], GB)
            for j in range(8):
                b = FIRST["mem_o"] + j // 2
                if j % 2 == 0:
                    arrived(pe, b)
                pe.wait_ge(ev["mem_o"], j + 1)
                for k in range(4):
                    kk = (j % 2) * 4 + k
                    last = mm(ps[:, j % GB, 0:S], ring[:, b % RING, kk * P:(kk + 1) * P], om[:, k, :],
                              k == 0, k == 3)
                last.then_inc(used if j % 2 else halves, 1)
            pe.wait_ge(sqd, 6)
            total(6, sq, KT, S, "ym")
            total(7, sq, KT, S, "hf", squares=(1, 7))
            pe.wait_ge(ev["mem_o"], GB + 8)
            pe.sem_inc(ev["up"], GB)
            tiles("up", FIRST["up"], FF, h, S, norm=(2, 3))
            pe.wait_ge(ev["up"], GB + FF)
            pe.wait_ge(up_sq, GB + FF)
            pe.sem_inc(ev["down"], GB)
            with pe.Fori(0, KT // 2) as it:
                for j in range(2):
                    pe.wait_ge(ev["down"], it * 2 + (j + 1 + GB - 2))
                    for q in range(4):
                        b = FIRST["down"] + 4 * j + q
                        arrived(pe, b, it)
                        for k in range(8):
                            last = mm(ps[:, j, 0:S], ring[:, b % RING, k * P:(k + 1) * P],
                                      act_up[:, 8 * q + k, :], q == 0 and k == 0, q == 3 and k == 7)
                        last.then_inc(used, 1)
            pe.wait_ge(sqd, 8)
            total(6, sq, KT, S, "yf")
            second_tensor(pe, mm, tiles, total)

        @block.scalar
        def _(act):
            link = Chain(act, act_chain)
            f = nc.scalar.activation

            def root(bank, t, scale=1.0, which=0):
                act.wait_ge(summed, which)
                f(rs[:, 0:t], ps[:, bank, 0:t], ACT.Sqrt, bias=eps_c, scale=scale).then_inc(rooted, 1)

            act.dma_start(h, mem_t).then_inc(ld_m, 16)
            for dst, src in ((sink_sb, sinks_d), (wst, ws_t), (wpl, w_pool), (bsp[0:1, :], b_sp),
                             (res[:, :, 0:META], meta_t)):
                act.dma_start(dst, src).then_inc(ld_s, 16)
            act.wait_ge(ld_m, 16)
            f(sq, h, ACT.Square).then_inc(sqd, 1)
            act.wait_ge(ld_x, 16)
            f(merged, xr, ACT.Square).then_inc(sqd, 1)
            act.wait_ge(init_done, 1)
            root(5, S, which=2)
            act.wait_ge(normed, 1)
            root(4, S, which=2)
            b = FIRST["in"]
            for j in range(18):
                act.wait_ge(used, b + j + 1)
                src = ps[:, j % GB, 0:S]
                if j < 6:
                    f(qkv[:, j, :], src, ACT.Copy).then_inc(ev["qkvs"], 1)
                elif j < 14:
                    f((su if j < 10 else sv)[:, (j - 6) % 4, :], src, ACT.Gelu_apprx_tanh).then_inc(ev["qkvs"], 1)
                else:
                    f(pcp[:, j - 14, META:L], src, ACT.Copy).then_inc(ev["qkvs"], 1)
            for j in range(8):
                act.wait_ge(used, b + 18 + j + 1)
                f(gates[:, j, :], ps[:, j % GB, 0:S], ACT.Sigmoid).then_inc(ev["gate"], 1)
            act.wait_ge(at_m, 1)
            for e in range(8):
                link(f(sc1[:, e, :], sc1[:, e, :], ACT.Exp, bias=small[:, 16 + e:17 + e],
                       accum_out=small[:, 24 + e:25 + e]))
            f(small[:, 32:40], small[:, 32:40], ACT.Exp).then_inc(at_p, 1)
            act.wait_ge(at_m, 2)
            for e in range(8):
                link(f(sc0[:, e, :], sc0[:, e, :], ACT.Exp, bias=small[:, 40 + e:41 + e],
                       accum_out=small[:, 48 + e:49 + e]))
            f(small[:, 56:64], small[:, 56:64], ACT.Exp).then_inc(at_p, 1)
            root(6, S, scale=2.0, which=3)
            with act.Fori(0, 2) as it:
                for s in range(8):
                    act.wait_ge(used, it * 8 + (b + 26 + s + 1))
                    f(gates[:, bass.ds(it * 8 + (8 + s), 1), :], ps[:, s % GB, 0:S],
                      ACT.Sigmoid).then_inc(ev["gate"], 1)
            act.wait_ge(at_t, 2)
            for c in range(2):
                for q in range(2):
                    last = nc.scalar.copy(pt1[:, c, 4 * q:4 * q + 4, :], ps[:, 4 + 2 * c + q, :])
            last.then_inc(at_tc, 1)
            act.wait_ge(pl_o, 1)
            for g in range(4):
                last = f(yc[:, g, :], ps[:, 2 + g // 2, (g % 2) * S:(g % 2 + 1) * S], ACT.Copy,
                         scale=col("pool_scale", g))
            last.then_inc(pl_y, 1)
            act.wait_ge(at_t, 3)
            for q in range(2):
                last = nc.scalar.copy(pt0[:, 4 * q:4 * q + 4, :], ps[:, 4 + q, :])
            last.then_inc(at_tc, 1)

            def squares_of_y(name, n, t, g, sc, sqv=None, ybuf=None, n0=0):
                for j in range(n):
                    act.wait_ge(ev[name], GB + j + 1)
                    ins = f(sq2(sqv)[:, j, :], sq2(ybuf, 1)[:, j, :], ACT.Square)
                    if j < n - 1:
                        link(ins)
                    else:
                        ins.then_inc(sqd, 1)
                        act.wait_ge(sqd, sc)
                for j in range(n):
                    last = f(sq2(ybuf, 1)[:, j, :], sq2(ybuf, 1)[:, j, :], ACT.Copy, scale=col(g[0], g[1] + j))
                last.then_inc(yg_done, 1)

            def squares_of_res(dst, src, done, n0, per=1):
                for i in range(4):
                    act.wait_ge(done, n0 + per * (i + 1))
                    f(dst[:, 2 * i:2 * i + 2, :], src[:, 2 * i:2 * i + 2, :], ACT.Square).then_inc(
                        sq_part if i < 3 else sqd, 1)

            def sq2(x, d=0):
                return x if x is not None else (y1 if d else sq)

            squares_of_y("out", 8, S, ("g_norm", 8), 4)
            root(6, S, which=4)
            squares_of_res(sq, xr, res_up, 0)
            b = FIRST["mem_kv"]
            for j in range(4):
                act.wait_ge(used, b + j + 1)
                f(memk[:, j, :], ps[:, j % GB, 0:S], ACT.Copy).then_inc(ev["mem_k"], 1)
            root(7, S, which=5)
            act.wait_ge(mm_m, 1)
            for e in range(8):
                ins = f(msc[:, e, :], ps[:, 4 + e // 2, (e % 2) * 256:(e % 2) * 256 + 256], ACT.Exp,
                        bias=small[:, 16 + e:17 + e], scale=128 ** -0.5, accum_out=small[:, 24 + e:25 + e])
                ins.then_inc(mm_p, 1)
            act.wait_ge(mm_t, 1)
            for c in range(2):
                nc.scalar.copy(mpt[:, c, 0:4, :], ps[:, 2 * c, :]).then_inc(mm_tc, 1)
            act.wait_ge(mm_o, 1)
            nc.scalar.copy(om[:, :, 0:P], ps[:, 4, :].rearrange("p (a b) -> p a b", a=4)).then_inc(mm_y, 1)
            squares_of_y("mem_o", 8, S, ("g_norm", 24), 6)
            load_lora(act)
            root(6, S, which=6)
            squares_of_res(sq, xr, res_up, 4)
            root(7, S, which=7)
            b = FIRST["up"]
            with act.Fori(0, FF // 8) as it:
                for s in range(8):
                    act.wait_ge(used, it * 8 + (b + s + 1))
                    act.wait_ge(up_sq, it * 8 + (s + 1))
                    f(tmp[:, s % 4, :], ps[:, s % GB, 0:S], ACT.Relu).then_inc(ev["up"], 1)
            squares_of_y("down", 8, S, ("g_norm", 40), 8)
            root(6, S, which=8)
            second_scalar(act, link, f, root, squares_of_res)

        @block.vector
        def _(dve):
            link = Chain(dve, dve_chain)
            v = nc.vector
            tt, stt, ts = v.tensor_tensor, v.scalar_tensor_tensor, v.tensor_scalar

            def inverse_root(which, t):
                dve.wait_ge(rooted, which)
                link(v.reciprocal(rs[:, 0:t], rs[:, 0:t]))

            def residual(which, t, x, yv, up=None):
                dve.wait_ge(yg_done, up)
                inverse_root(which, t)
                for i in range(4):
                    c = slice(2 * i, 2 * i + 2)
                    link(tt(yv[:, c, :], yv[:, c, :], over(rs[:, 0:t], 2), ALU.mult))
                    tt(x[:, c, :], x[:, c, :], yv[:, c, :], ALU.add).then_inc(res_up, 1)
                dve.wait_ge(res_up, 4 * up)

            def normed_to(dst, which, t, n):
                inverse_root(which, t)
                for i in range(4):
                    part = dst[:, 2 * i:2 * i + 2, :]
                    tt(part, part, over(rs[:, 0:t], 2), ALU.mult).then_inc(norm_part if i < 3 else normed, 1)

            v.memset(small[:, 0:1], EPS)
            v.memset(small[:, 1:2], GN_EPS)
            v.memset(small[:, 2:3], 1.0)
            dve.wait_ge(ld_s, 16 * 5)
            v.memset(wst[64:P, :, 0:64], 0.0)
            link(v.memset(pcp[:, :, 0:META], 0.0))
            v.memset(win_a[:, :, 0:META], 0.0)
            v.memset(win_b[:, :, 0:META], 0.0).then_inc(init_done, 1)
            dve.wait_ge(ld_m, 16)
            dve.wait_ge(ld_c, 32)
            link(tt(memn, h, col_wide("g_mem", 0, KT, S), ALU.mult))
            dve.wait_ge(ld_x, 16)
            dve.wait_ge(sqd, 2)
            link(tt(h, xr, col_wide("g_norm", 0, KT, S), ALU.mult))
            normed_to(h, 1, S, 1)
            inverse_root(2, S)
            tt(memn, memn, over(rs[:, 0:S], KT), ALU.mult).then_inc(normed0, 1)
            for r in range(2):
                nk, sc, mask = (2 * P, sc1, "att1") if r == 0 else (P, sc0, "att0")
                m = small[:, 16 + 24 * r:24 + 24 * r]
                ex = small[:, 32 + 24 * r:40 + 24 * r]
                dve.wait_ge(at_s, r + 1)
                per = 512 // nk
                for q in range(8 // per):
                    ins = stt(out=sc[:, per * q:per * q + per, :],
                              in0=ps[:, 4 + q, :].rearrange("p (a b) -> p a b", a=per), scalar=0.125,
                              in1=over(const(mask), per), op0=ALU.mult, op1=ALU.add)
                    link(ins)
                link(v.tensor_reduce(m, sc, AX_X, ALU.max))
                link(tt(m, m, sink_sb, ALU.max))
                link(tt(ex, sink_sb, m, ALU.subtract))
                ts(m, m, -1.0, None, ALU.mult).then_inc(at_m, 1)
                if r == 0:
                    dve.wait_ge(ev["qkvs"], GB + 14)
                    tt(tmp, sv, sv, ALU.mult).then_inc(sqd, 1)
                    link(tt(sv, sv, col_wide("g_sgu", 0, 4, S), ALU.mult))
            dve.wait_ge(at_t, 1)
            v.tensor_copy(vtok, ps[:, 7, 0:S].rearrange("p (a b) -> p a b", a=2)).then_inc(at_tc, 1)
            for r in range(2):
                nk, sc = (2 * P, sc1) if r == 0 else (P, sc0)
                tot = small[:, 24 + 24 * r:32 + 24 * r]
                ex = small[:, 32 + 24 * r:40 + 24 * r]
                dve.wait_ge(at_p, r + 1)
                link(tt(tot, tot, ex, ALU.add))
                link(v.reciprocal(tot, tot))
                tt(sc, sc, tot.unsqueeze(2).to_broadcast([P, 8, nk]), ALU.mult).then_inc(at_n, 1)
            dve.wait_ge(rooted, 3)
            link(v.reciprocal(rs[:, 0:S], rs[:, 0:S]))
            tt(sv, sv, over(rs[:, 0:S], 4), ALU.mult).then_inc(sg_n, 1)
            dve.wait_ge(sg_t, 1)
            v.tensor_copy(svt[:, 0, :], ps[:, 0, :])
            v.tensor_copy(svt[:, 1, :], ps[:, 1, :]).then_inc(sg_tc, 1)
            dve.wait_ge(sg_o, 1)
            for c in range(2):
                last = tt(yb[:, :, c * P:(c + 1) * P], su[:, :, c * P:(c + 1) * P],
                          ps[:, 6 + c, :].rearrange("p (a b) -> p a b", a=4), ALU.mult)
            last.then_inc(sg_y, 1)
            dve.wait_ge(at_o, 1)
            for c in range(2):
                last = v.tensor_copy(ya[:, :, c * P:(c + 1) * P],
                                     ps[:, c, :].rearrange("p (a b) -> p a b", a=4))
            last.then_inc(at_y, 1)
            for u in range(24):
                n, br = u // 3, u % 3
                if u % 2:
                    dve.wait_ge(used, FIRST["branch"] + u // 2 + 1)
                else:
                    dve.wait_ge(halves, u // 2 + 1)
                src, g = ps[:, u % GB, 0:S], gates[:, 8 * br + n, :]
                if br == 0:
                    tt(merged[:, n, :], g, src, ALU.mult).then_inc(ev["branch"], 1)
                else:
                    tt(tmp[:, br, :], g, src, ALU.mult).then_inc(ev["branch"], 1)
                    dve.wait_ge(ev["branch"], GB + u + 1)
                    ins = tt(merged[:, n, :], merged[:, n, :], tmp[:, br, :], ALU.add)
                    if u < 23:
                        link(ins)
                    else:
                        ins.then_inc(merged_done, 1)

            def take(name, b, n, dst, t, per=1):
                for j in range(n):
                    dve.wait_ge(used, b + per * (j + 1))
                    v.tensor_copy(dst[:, j, :], ps[:, j % GB, 0:t]).then_inc(ev[name], 1)

            take("out", FIRST["out"], 8, y1, S)
            residual(4, S, xr, y1, 1)
            link(tt(h, xr, col_wide("g_norm", 16, KT, S), ALU.mult))
            dve.wait_ge(used, FIRST["mem_kv"] + 8)
            normed_to(h, 5, S, 3)
            for c in range(2):
                ins = v.tensor_copy(memv[:, c, :], ps[:, c, :])
                if c == 0:
                    link(ins)
                else:
                    ins.then_inc(ev["mem_v"], 1)
            take("mem_q", FIRST["mem_q"], 4, qm, S)
            dve.wait_ge(mm_s, 1)
            for q in range(4):
                link(v.tensor_reduce(small[:, 16 + 2 * q:18 + 2 * q],
                                     ps[:, 4 + q, :].rearrange("p (a b) -> p a b", a=2), AX_X, ALU.max))
            ts(small[:, 16:24], small[:, 16:24], -(128 ** -0.5), None, ALU.mult).then_inc(mm_m, 1)
            dve.wait_ge(mm_p, 8)
            link(v.reciprocal(small[:, 24:32], small[:, 24:32]))
            tt(msc, msc, small[:, 24:32].unsqueeze(2).to_broadcast([P, 8, 2 * P]), ALU.mult).then_inc(mm_n, 1)
            dve.wait_ge(mm_t, 1)
            for c in range(2):
                v.tensor_copy(mpt[:, c, 4:8, :], ps[:, 2 * c + 1, :]).then_inc(mm_tc, 1)
            dve.wait_ge(mm_o, 1)
            v.tensor_copy(om[:, :, P:S], ps[:, 5, :].rearrange("p (a b) -> p a b", a=4)).then_inc(mm_y, 1)
            for j in range(8):
                if j % 2:
                    dve.wait_ge(used, FIRST["mem_o"] + j // 2 + 1)
                else:
                    dve.wait_ge(halves, 12 + j // 2 + 1)
                v.tensor_copy(y1[:, j, :], ps[:, j % GB, 0:S]).then_inc(ev["mem_o"], 1)
            residual(6, S, xr, y1, 2)
            link(tt(h, xr, col_wide("g_norm", 32, KT, S), ALU.mult))
            normed_to(h, 7, S, 4)
            dve.sem_inc(up_sq, 4)
            with dve.Fori(0, FF // 8) as it:
                for s in range(8):
                    dve.wait_ge(ev["up"], it * 8 + (GB + s + 1))
                    tt(act_up[:, bass.ds(it * 8 + s, 1), :], tmp[:, s % 4, :], tmp[:, s % 4, :],
                       ALU.mult).then_inc(up_sq, 1)
            b = FIRST["down"]
            with dve.Fori(0, KT // 2) as it:
                for j in range(2):
                    dve.wait_ge(used, it * 8 + (b + 4 * (j + 1)))
                    dve.sem_inc(passed, 1)
                    v.tensor_copy(y1[:, bass.ds(it * 2 + j, 1), :], ps[:, j, 0:S]).then_inc(ev["down"], 1)
            residual(8, S, xr, y1, 3)
            second_vector(dve, link, v, tt, stt, ts, inverse_root, residual, normed_to, take)

        @block.gpsimd
        def _(pool):
            link = Chain(pool, pool_chain)
            g = nc.gpsimd
            pool.wait_ge(ev["qkvs"], GB + 18)
            pool.wait_ge(init_done, 1)
            link(g.tensor_tensor(win_a[:, 0:4, META:L], pcp[:, 0:4, META:L], pcp[:, 0:4, META - 1:L - 1], ALU.add))
            link(g.tensor_tensor(win_b[:, 1:4, META:L], win_a[:, 1:4, META:L], win_a[:, 1:4, META - 2:L - 2], ALU.add))
            link(g.tensor_tensor(win_a[:, 2:4, META:L], win_b[:, 2:4, META:L], win_b[:, 2:4, META - 4:L - 4], ALU.add))
            link(g.tensor_tensor(win_b[:, 3:4, META:L], win_a[:, 3:4, META:L], win_a[:, 3:4, META - 8:L - 8], ALU.add))
            inv = const("inv_cnt").rearrange("p (a b) -> p a b", a=4)
            for k in range(4):
                src = (win_a, win_b)[k % 2]
                link(g.tensor_tensor(src[:, k, META:META + 16], src[:, k, META:META + 16], inv[:, k, :], ALU.mult))
                link(g.tensor_scalar(src[:, k, META + 16:L], src[:, k, META + 16:L], 0.5 ** (k + 1), None, ALU.mult))
                ins = g.tensor_tensor(pcp[:, k, META:L], src[:, k, META:L], pcp[:, k, META:L], ALU.subtract)
                if k < 3:
                    link(ins)
                else:
                    ins.then_inc(pl_w, 1)
            second_gpsimd(pool, link, g)


def blocks_of(w):
    k, n = w.shape
    kt = k // P
    b = w.reshape(kt, P, n // P, P).transpose(2, 1, 0, 3)
    return b.reshape(n // P, P, kt * P)


def deep_blocks(w, per):
    b = blocks_of(w)
    n = b.shape[0]
    out = np.zeros((n, P, per * BLK), w.dtype)
    out[:, :, :b.shape[2]] = b
    return out.reshape(n, P, per, BLK).transpose(0, 2, 1, 3).reshape(n * per, P, BLK)


def feature_tiles(x):
    return np.ascontiguousarray(x.T.reshape(-1, P, x.shape[0]).transpose(1, 0, 2))


def columns(*vectors):
    return [np.asarray(v).reshape(-1, P).T for v in vectors]


def kernel(**a):
    import concourse.bacc as bacc
    from concourse.bass_utils import run_bass_kernel_spmd

    a = {k: np.asarray(v) for k, v in a.items()}
    f = np.float32
    w_in = a["w_in"][0]
    heads = np.arange(512).reshape(2, 4, 64).transpose(1, 0, 2).reshape(-1)
    w_in = np.concatenate([w_in[:, :512][:, heads], w_in[:, 512:]], axis=1)
    br = a["w_branch"][0].copy()
    br[0] = br[0][heads]
    br = br.reshape(3, 4, P, 8, P).transpose(3, 0, 2, 1, 4).reshape(12, 2, P, 4 * P)
    mem_o = a["w_o_mem"][0].reshape(4, P, 8, P).transpose(2, 1, 0, 3).reshape(4, 2, P, 4 * P)
    pair = lambda w: w.reshape(w.shape[0], 2, P, 4 * P).transpose(0, 2, 1, 3).reshape(w.shape[0], P, BLK)
    both = lambda w: w.reshape(*w.shape[:-1], 2, F2, P).swapaxes(-3, -2).reshape(w.shape)
    up2 = both(a["ffn_up_2"])
    parts = {
        "in": blocks_of(w_in), "branch": pair(br), "out": blocks_of(a["w_out"][0]),
        "mem_kv": blocks_of(a["w_kv_mem"][0]), "mem_q": blocks_of(a["w_q_mem"][0]), "mem_o": pair(mem_o),
        "up": blocks_of(a["w_up"][0]), "down": deep_blocks(a["w_down"][0], 4),
        "rw_r": blocks_of(a["rw_wr_2"][0]), "rw_k": blocks_of(a["rw_wk_2"][0]),
        "rw_v": blocks_of(a["rw_wv_2"][0]), "rw_o": blocks_of(a["rw_wo_2"][0]),
        "ffa_up": blocks_of(up2[0]), "ffa_down": deep_blocks(a["ffn_down_2"][0], F2B),
        "sb_k": blocks_of(a["sb_wk_2"]), "sb_v": blocks_of(a["sb_wv_2"]),
        "sb_q": blocks_of(a["sb_wq_2"][0]), "sb_o": blocks_of(a["sb_wo_2"][0]),
        "ffb_up": blocks_of(up2[1]), "ffb_down": deep_blocks(a["ffn_down_2"][1], F2B),
    }
    stream = np.concatenate([parts[name] for name, _ in STREAM])
    cw, cb = both(a["ffn_conv_w_2"]), both(a["ffn_conv_b_2"])
    cols = np.concatenate(columns(
        a["g_norm"], a["g_mem"], a["g_sgu"], a["pool_scale"], a["norm_mix_g_2"], a["norm_ffn_g_2"],
        a["rw_mix_2"], a["rw_w0_2"], a["rw_a0_2"], a["rw_kk_2"], a["rw_ka_2"], a["rw_rk_2"],
        a["rw_lnx_g_2"], a["rw_lnx_b_2"], a["kv_norm_g_2"], a["final_norm_g_2"], cw, cb), axis=1)
    g1 = a["rw_g1_2"][0]
    wide = lambda w: np.ascontiguousarray(w.reshape(KT, P, -1).transpose(1, 0, 2))
    ins = {
        "stream": stream, "x_t": feature_tiles(a["x"][0]), "mem_t": feature_tiles(a["mem"][0]),
        "meta_t": feature_tiles(a["meta_tokens_2"]), "cols": np.ascontiguousarray(cols),
        "consts": CONSTS, "sinks": np.tile(a["attn_sinks"], (P, 1)),
        "ws_t": np.ascontiguousarray(a["w_spatial"][0].transpose(2, 0, 1)),
        "b_sp": a["b_spatial"][0].reshape(1, 512),
        "w_pool": np.ascontiguousarray(a["w_pool"][0].transpose(1, 0, 2)),
        "w1": wide(a["rw_w1_2"][0]), "a1": wide(a["rw_a1_2"][0]), "g1": wide(g1),
        "w2": a["rw_w2_2"][0], "a2": a["rw_a2_2"][0], "g2": a["rw_g2_2"][0],
    }
    nc = bacc.Bacc("TRN2", target_bir_lowering=False, num_devices=1)
    args = [nc.dram_tensor("in_" + n, v.shape, mybir.dt.from_np(v.dtype), kind="ExternalInput").ap()
            for n, v in ins.items()]
    out = nc.dram_tensor("out_t", (P, KT, S), F32, kind="ExternalOutput").ap()
    program(nc, *args, out)
    r = run_bass_kernel_spmd(nc, [{"in_" + n: v for n, v in ins.items()}], core_ids=[0])
    got = np.asarray(r.results[0]["out_t"]).reshape(P, KT, S)
    return np.ascontiguousarray(got.transpose(2, 1, 0).reshape(1, S, D))
```
